# Optimizing a Trainium2 kernel written in Bass

```python
import math
import numpy as np
import jax, jax.numpy as jnp
from jax import lax

D_MODEL = 1024
BATCH = 1
SEQ = 256
DEPTH = 2

HEAD_DIM = 64
ROT_DIM = HEAD_DIM // 4
ROPE_THETA = 500000.0
EPS = 1e-6
Q_BLOCK = 128
A_HEADS = 4
IDX_HEADS = 8
IDX_DIM = 64
INDEX_TOPK = 256
B_HEADS = 4
MOBA_BLOCK = 256
MOBA_TOPK = 3
MOBA_Q_CHUNK = 16
C_HEADS = 4
C_VDIM = 2 * HEAD_DIM
D_FF = 2816

WIDTH_A = A_HEADS * HEAD_DIM
WIDTH_B = B_HEADS * HEAD_DIM
WIDTH_C = C_HEADS * C_VDIM
MIX_WIDTH = WIDTH_A + WIDTH_B + WIDTH_C
IN_SPLITS = (A_HEADS * HEAD_DIM, HEAD_DIM, HEAD_DIM, IDX_HEADS * IDX_DIM, IDX_DIM, IDX_HEADS,
             B_HEADS * HEAD_DIM, B_HEADS * HEAD_DIM, B_HEADS * HEAD_DIM,
             C_HEADS * 2 * HEAD_DIM, C_HEADS * 2 * HEAD_DIM, C_HEADS * C_VDIM,
             D_MODEL, D_MODEL, D_MODEL)
IN_WIDTH = sum(IN_SPLITS)


def rmsnorm(x, g):
    xf = x.astype(jnp.float32)
    y = xf * lax.rsqrt(jnp.mean(xf * xf, axis=-1, keepdims=True) + EPS)
    return y.astype(x.dtype) * g

def rope_tables(positions):
    inv_freq = jnp.power(ROPE_THETA, -jnp.arange(0, ROT_DIM, 2, dtype=jnp.float32) / ROT_DIM)
    ang = positions.astype(jnp.float32)[..., None] * inv_freq
    return jnp.cos(ang), jnp.sin(ang)

def rope(x, cos, sin):
    shape = cos.shape[:2] + (1,) * (x.ndim - 3) + cos.shape[-1:]
    c = cos.reshape(shape).astype(x.dtype)
    s = sin.reshape(shape).astype(x.dtype)
    half = ROT_DIM // 2
    x1, x2 = x[..., :half], x[..., half:ROT_DIM]
    return jnp.concatenate([x1 * c - x2 * s, x2 * c + x1 * s, x[..., ROT_DIM:]], axis=-1)

def masked_softmax(scores, mask):
    return jax.nn.softmax(jnp.where(mask, scores.astype(jnp.float32), -jnp.inf), axis=-1)

def swiglu(h, w_gate, w_up, w_down):
    return (jax.nn.silu(h @ w_gate) * (h @ w_up)) @ w_down

def dsa_attention(q, k, v, qi, ki, wi):
    B, S = q.shape[:2]
    topk = min(INDEX_TOPK, S // 4)
    nb = S // Q_BLOCK
    s_pos = jnp.arange(S)
    b_idx = jnp.arange(B)[:, None, None]
    scale = HEAD_DIM ** -0.5

    def blk(t):
        return t.reshape((B, nb, Q_BLOCK) + t.shape[2:]).swapaxes(0, 1)

    def body(args):
        qb, qib, wib, start = args
        t = start + jnp.arange(Q_BLOCK)
        causal = s_pos[None, :] <= t[:, None]
        logits = jnp.einsum('bqhd,bsd->bqhs', qib, ki)
        iscore = jnp.einsum('bqhs,bqh->bqs', jax.nn.relu(logits).astype(jnp.float32), wib.astype(jnp.float32))
        iscore = jnp.where(causal[None], iscore, -jnp.inf)
        _, idx = lax.top_k(iscore, topk)
        k_sel = k[b_idx, idx]
        v_sel = v[b_idx, idx]
        sc = jnp.einsum('bqhd,bqkd->bhqk', qb, k_sel) * scale
        valid = (idx <= t[None, :, None])[:, None]
        p = masked_softmax(sc, valid).astype(v.dtype)
        return jnp.einsum('bhqk,bqkd->bqhd', p, v_sel)

    starts = jnp.arange(nb) * Q_BLOCK
    out = lax.map(body, (blk(q), blk(qi), blk(wi), starts))
    return out.swapaxes(0, 1).reshape(B, S, -1)

def moba_attention(q, k, v):
    B, S, H, d = q.shape
    nblk = -(-S // MOBA_BLOCK)
    pad = nblk * MOBA_BLOCK - S
    scale = d ** -0.5

    def to_blocks(t):
        t = jnp.pad(t, ((0, 0), (0, pad), (0, 0), (0, 0)))
        return t.reshape(B, nblk, MOBA_BLOCK, H, d).transpose(0, 3, 1, 2, 4)

    kbt, vbt = to_blocks(k), to_blocks(v)
    kmean = jnp.mean(kbt.astype(jnp.float32), axis=3).astype(k.dtype)
    n_sel = min(MOBA_TOPK, nblk)
    nc = S // MOBA_Q_CHUNK
    q_chunks = q.reshape(B, nc, MOBA_Q_CHUNK, H, d).transpose(1, 0, 3, 2, 4)
    b_idx = jnp.arange(B)[:, None, None, None]
    h_idx = jnp.arange(H)[None, :, None, None]
    blk_ids = jnp.arange(nblk)
    own_offsets = jnp.arange(MOBA_BLOCK)

    def body(args):
        qb, start = args
        t = start + jnp.arange(MOBA_Q_CHUNK)
        j = start // MOBA_BLOCK
        gate = jnp.einsum('bhqd,bhnd->bhqn', qb, kmean).astype(jnp.float32)
        gate = jnp.where(blk_ids < j, gate, -jnp.inf)
        _, sel = lax.top_k(gate, n_sel)
        sel_valid = sel < j
        k_sel = kbt[b_idx, h_idx, sel]
        v_sel = vbt[b_idx, h_idx, sel]
        s_sel = jnp.einsum('bhqd,bhqnkd->bhqnk', qb, k_sel) * scale
        s_sel = jnp.where(sel_valid[..., None], s_sel.astype(jnp.float32), -jnp.inf)
        s_sel = s_sel.reshape(B, H, MOBA_Q_CHUNK, n_sel * MOBA_BLOCK)
        k_own = lax.dynamic_index_in_dim(kbt, j, axis=2, keepdims=False)
        v_own = lax.dynamic_index_in_dim(vbt, j, axis=2, keepdims=False)
        s_own = jnp.einsum('bhqd,bhkd->bhqk', qb, k_own) * scale
        own_causal = (j * MOBA_BLOCK + own_offsets)[None, :] <= t[:, None]
        s_own = jnp.where(own_causal, s_own.astype(jnp.float32), -jnp.inf)
        p = jax.nn.softmax(jnp.concatenate([s_sel, s_own], axis=-1), axis=-1).astype(v.dtype)
        p_sel = p[..., :n_sel * MOBA_BLOCK].reshape(B, H, MOBA_Q_CHUNK, n_sel, MOBA_BLOCK)
        p_own = p[..., n_sel * MOBA_BLOCK:]
        return (jnp.einsum('bhqnk,bhqnkd->bhqd', p_sel, v_sel)
                + jnp.einsum('bhqk,bhkd->bhqd', p_own, v_own))

    starts = jnp.arange(nc) * MOBA_Q_CHUNK
    out = lax.map(body, (q_chunks, starts))
    return out.transpose(1, 0, 3, 2, 4).reshape(B, S, H * d)

def diff_attention(q, k, v, lam, lam_init, subln_g):
    B, S, H = q.shape[:3]
    nb = S // Q_BLOCK
    s_pos = jnp.arange(S)
    scale = HEAD_DIM ** -0.5
    q_blocks = q.reshape(B, nb, Q_BLOCK, H, 2, HEAD_DIM).swapaxes(0, 1)

    def body(args):
        qb, start = args
        t = start + jnp.arange(Q_BLOCK)
        causal = s_pos[None, :] <= t[:, None]
        sc = jnp.einsum('bqhcd,bshcd->bhcqs', qb, k) * scale
        p = masked_softmax(sc, causal)
        attn = (p[:, :, 0] - lam * p[:, :, 1]).astype(v.dtype)
        return jnp.einsum('bhqs,bshe->bqhe', attn, v)

    starts = jnp.arange(nb) * Q_BLOCK
    out = lax.map(body, (q_blocks, starts))
    out = out.swapaxes(0, 1).reshape(B, S, H, C_VDIM)
    out = rmsnorm(out, subln_g) * (1.0 - lam_init)
    return out.reshape(B, S, H * C_VDIM)

def hybrid_mixer(h, cos, sin, w_in, qk_g, lam_p, subln_g, w_branch, w_out, lam_init):
    B, S, _ = h.shape
    offsets = np.cumsum(IN_SPLITS)[:-1].tolist()
    proj = h @ w_in
    (qa, ka, va, qi, ki, wi, qb, kb, vb, qc, kc, vc, ga, gb, gc) = jnp.split(proj, offsets, axis=-1)
    qa = rope(rmsnorm(qa.reshape(B, S, A_HEADS, HEAD_DIM), qk_g[0]), cos, sin)
    ka = rope(rmsnorm(ka, qk_g[1]), cos, sin)
    qi = rope(qi.reshape(B, S, IDX_HEADS, IDX_DIM), cos, sin)
    ki = rope(ki, cos, sin)
    wi = wi * (IDX_HEADS * IDX_DIM) ** -0.5
    o_a = dsa_attention(qa, ka, va, qi, ki, wi)
    qb = rope(rmsnorm(qb.reshape(B, S, B_HEADS, HEAD_DIM), qk_g[2]), cos, sin)
    kb = rope(rmsnorm(kb.reshape(B, S, B_HEADS, HEAD_DIM), qk_g[3]), cos, sin)
    o_b = moba_attention(qb, kb, vb.reshape(B, S, B_HEADS, HEAD_DIM))
    qc = rope(rmsnorm(qc.reshape(B, S, C_HEADS, 2, HEAD_DIM), qk_g[4]), cos, sin)
    kc = rope(rmsnorm(kc.reshape(B, S, C_HEADS, 2, HEAD_DIM), qk_g[5]), cos, sin)
    lp = lam_p.astype(jnp.float32)
    lam = jnp.exp(jnp.sum(lp[0] * lp[1])) - jnp.exp(jnp.sum(lp[2] * lp[3])) + lam_init
    o_c = diff_attention(qc, kc, vc.reshape(B, S, C_HEADS, C_VDIM), lam, lam_init, subln_g)
    y_a = o_a @ w_branch[:WIDTH_A]
    y_b = o_b @ w_branch[WIDTH_A:WIDTH_A + WIDTH_B]
    y_c = o_c @ w_branch[WIDTH_A + WIDTH_B:]
    merged = jax.nn.sigmoid(ga) * y_a + jax.nn.sigmoid(gb) * y_b + jax.nn.sigmoid(gc) * y_c
    return merged @ w_out

def first_inputs(seed: int = 0) -> dict:
    key = jax.random.key(seed)
    ks = jax.random.split(key, 14)
    x = jax.random.normal(ks[0], (BATCH, SEQ, D_MODEL), jnp.float32)
    offset = jax.random.randint(ks[1], (BATCH, 1), 0, 4096, dtype=jnp.int32)
    positions = (offset + jnp.arange(SEQ, dtype=jnp.int32)[None, :]).astype(jnp.int32)
    norm_g = 1.0 + 0.02 * jax.random.normal(ks[2], (DEPTH, 3, D_MODEL), jnp.float32)
    w_in = jax.random.normal(ks[3], (DEPTH, D_MODEL, IN_WIDTH), jnp.float32) * D_MODEL ** -0.5
    qk_norm_g = 1.0 + 0.02 * jax.random.normal(ks[4], (DEPTH, 6, HEAD_DIM), jnp.float32)
    lambda_params = 0.1 * jax.random.normal(ks[5], (DEPTH, 4, HEAD_DIM), jnp.float32)
    diff_subln_g = 1.0 + 0.02 * jax.random.normal(ks[6], (DEPTH, C_VDIM), jnp.float32)
    w_branch = jnp.concatenate([
        jax.random.normal(ks[7], (DEPTH, WIDTH_A, D_MODEL), jnp.float32) * WIDTH_A ** -0.5,
        jax.random.normal(ks[8], (DEPTH, WIDTH_B, D_MODEL), jnp.float32) * WIDTH_B ** -0.5,
        jax.random.normal(ks[9], (DEPTH, WIDTH_C, D_MODEL), jnp.float32) * WIDTH_C ** -0.5], axis=1)
    w_out = jax.random.normal(ks[10], (DEPTH, D_MODEL, D_MODEL), jnp.float32) * D_MODEL ** -0.5
    ffn_w_gate = jax.random.normal(ks[11], (DEPTH, 2, D_MODEL, D_FF), jnp.float32) * D_MODEL ** -0.5
    ffn_w_up = jax.random.normal(ks[12], (DEPTH, 2, D_MODEL, D_FF), jnp.float32) * D_MODEL ** -0.5
    ffn_w_down = jax.random.normal(ks[13], (DEPTH, 2, D_FF, D_MODEL), jnp.float32) * D_FF ** -0.5
    return {'x': x, 'positions': positions, 'norm_g': norm_g, 'w_in': w_in, 'qk_norm_g': qk_norm_g,
            'lambda_params': lambda_params, 'diff_subln_g': diff_subln_g, 'w_branch': w_branch,
            'w_out': w_out, 'ffn_w_gate': ffn_w_gate, 'ffn_w_up': ffn_w_up, 'ffn_w_down': ffn_w_down}

def first_block(x, positions, norm_g, w_in, qk_norm_g, lambda_params, diff_subln_g, w_branch,
              w_out, ffn_w_gate, ffn_w_up, ffn_w_down):
    cos, sin = rope_tables(positions)
    for layer in range(DEPTH):
        lam_init = 0.8 - 0.6 * math.exp(-0.3 * layer)
        x = x + 0.5 * swiglu(rmsnorm(x, norm_g[layer, 0]), ffn_w_gate[layer, 0], ffn_w_up[layer, 0], ffn_w_down[layer, 0])
        x = x + hybrid_mixer(rmsnorm(x, norm_g[layer, 1]), cos, sin, w_in[layer], qk_norm_g[layer],
                             lambda_params[layer], diff_subln_g[layer], w_branch[layer], w_out[layer], lam_init)
        x = x + 0.5 * swiglu(rmsnorm(x, norm_g[layer, 2]), ffn_w_gate[layer, 1], ffn_w_up[layer, 1], ffn_w_down[layer, 1])
    return x


GDN_HEADS = 8
GDN_DK = 128
GDN_DV = 128
GDN_CONV = 4
CHUNK = 64
CNV_CH = 1024
CNV_K = 31
W_Q = GDN_HEADS * GDN_DK
W_K = GDN_HEADS * GDN_DK
W_V = GDN_HEADS * GDN_DV
W_Z = GDN_HEADS * GDN_DV
W_BETA = GDN_HEADS
W_A = GDN_HEADS
W_GLU = 2 * CNV_CH
W_GATE = 2 * D_MODEL
SPLITS = [int(s) for s in np.cumsum([W_Q + W_K + W_V, W_Z, W_BETA, W_A, W_GLU])]
P_IN = W_Q + W_K + W_V + W_Z + W_BETA + W_A + W_GLU + W_GATE
RMS_EPS = 1e-6
LN_EPS = 1e-5


def rmsnorm_2(x, w):
    xf = x.astype(jnp.float32)
    y = xf * lax.rsqrt(jnp.mean(xf * xf, axis=-1, keepdims=True) + RMS_EPS)
    return (y * w.astype(jnp.float32)).astype(x.dtype)

def layernorm(x, g, b):
    xf = x.astype(jnp.float32)
    mu = jnp.mean(xf, axis=-1, keepdims=True)
    var = jnp.mean(jnp.square(xf - mu), axis=-1, keepdims=True)
    y = (xf - mu) * lax.rsqrt(var + LN_EPS)
    return (y * g.astype(jnp.float32) + b.astype(jnp.float32)).astype(x.dtype)

def l2norm(x):
    return x * lax.rsqrt(jnp.sum(x * x, axis=-1, keepdims=True) + 1e-6)

def causal_dwconv(x, w):
    k, c = w.shape
    return lax.conv_general_dilated(
        x, w[:, None, :].astype(x.dtype), window_strides=(1,), padding=[(k - 1, 0)],
        dimension_numbers=("NWC", "WIO", "NWC"), feature_group_count=c)

def swiglu_ffn(h, w_in, w_out):
    gate, up = jnp.split(h @ w_in, 2, axis=-1)
    return (jax.nn.silu(gate) * up) @ w_out

def chunk_gated_delta_rule(q, k, v, g, beta):
    b, l, h, dk = q.shape
    dv = v.shape[-1]
    n = l // CHUNK

    def to_chunks(t):
        return t.reshape(b, n, CHUNK, h, -1).transpose(0, 3, 1, 2, 4)

    q, k, v = to_chunks(q), to_chunks(k), to_chunks(v)
    g = g.reshape(b, n, CHUNK, h).transpose(0, 3, 1, 2)
    beta = beta.reshape(b, n, CHUNK, h).transpose(0, 3, 1, 2)
    G = jnp.cumsum(g, axis=-1)
    causal = jnp.tril(jnp.ones((CHUNK, CHUNK), dtype=bool))
    strict = jnp.tril(jnp.ones((CHUNK, CHUNK), dtype=bool), k=-1)
    diff = G[..., :, None] - G[..., None, :]
    decay = jnp.where(causal, jnp.exp(jnp.where(causal, diff, 0.0)), 0.0)
    kk = jnp.einsum("bhncd,bhnsd->bhncs", k, k)
    a_mat = jnp.where(strict, kk * decay * beta[..., :, None], 0.0)
    lhs = jnp.eye(CHUNK, dtype=jnp.float32) + a_mat
    rhs = jnp.concatenate([v * beta[..., None], k * (beta * jnp.exp(G))[..., None]], axis=-1)
    sol = lax.linalg.triangular_solve(lhs, rhs, left_side=True, lower=True, unit_diagonal=True)
    u, w = sol[..., :dv], sol[..., dv:]
    qk = jnp.einsum("bhncd,bhnsd->bhncs", q, k) * decay
    q_dec = q * jnp.exp(G)[..., None]
    k_dec = k * jnp.exp(G[..., -1:] - G)[..., None]
    chunk_decay = jnp.exp(G[..., -1])

    xs = tuple(jnp.moveaxis(t, 2, 0) for t in (q_dec, k_dec, u, w, qk, chunk_decay))

    def step(state, inp):
        q_c, k_c, u_c, w_c, qk_c, d_c = inp
        v_new = u_c - jnp.einsum("bhck,bhkv->bhcv", w_c, state)
        o_c = jnp.einsum("bhck,bhkv->bhcv", q_c, state) + jnp.einsum("bhcs,bhsv->bhcv", qk_c, v_new)
        state = state * d_c[..., None, None] + jnp.einsum("bhck,bhcv->bhkv", k_c, v_new)
        return state, o_c

    s0 = jnp.zeros((b, h, dk, dv), jnp.float32)
    _, o = lax.scan(step, s0, xs)
    return o.transpose(1, 0, 3, 2, 4).reshape(b, l, h, dv)

def gated_deltanet(qkv, z, beta_logit, a_logit, conv_w, a_log, dt_bias, norm_w, w_o):
    b, l, _ = qkv.shape
    qkv = jax.nn.silu(causal_dwconv(qkv, conv_w))
    q, k, v = jnp.split(qkv.astype(jnp.float32), [W_Q, W_Q + W_K], axis=-1)
    q = l2norm(q.reshape(b, l, GDN_HEADS, GDN_DK)) * (GDN_DK ** -0.5)
    k = l2norm(k.reshape(b, l, GDN_HEADS, GDN_DK))
    v = v.reshape(b, l, GDN_HEADS, GDN_DV)
    beta = jax.nn.sigmoid(beta_logit.astype(jnp.float32))
    g = -jnp.exp(a_log.astype(jnp.float32)) * jax.nn.softplus(
        a_logit.astype(jnp.float32) + dt_bias.astype(jnp.float32))
    o = chunk_gated_delta_rule(q, k, v, g, beta)
    zf = z.astype(jnp.float32).reshape(b, l, GDN_HEADS, GDN_DV)
    o = rmsnorm_2(o, norm_w) * jax.nn.silu(zf)
    return o.reshape(b, l, GDN_HEADS * GDN_DV).astype(qkv.dtype) @ w_o

def conformer_conv(glu_in, pw1_b, dw_w, dw_b, ln_g, ln_b, w_o, b_o):
    a, gate = jnp.split(glu_in + pw1_b, 2, axis=-1)
    h = a * jax.nn.sigmoid(gate)
    h = causal_dwconv(h, dw_w) + dw_b
    h = jax.nn.silu(layernorm(h, ln_g, ln_b))
    return h @ w_o + b_o

def second_inputs(seed: int = 0) -> dict:
    key = jax.random.key(seed)
    ks = iter(jax.random.split(key, 40))

    def nrm(shape, scale):
        return jax.random.normal(next(ks), shape, jnp.float32) * scale

    def gain(shape):
        return 1.0 + 0.02 * jax.random.normal(next(ks), shape, jnp.float32)

    L = DEPTH
    inp = {}
    inp["x"] = nrm((BATCH, SEQ, D_MODEL), 1.0)
    inp["ffn1_norm_pre"] = gain((L, D_MODEL))
    inp["ffn1_norm_post"] = gain((L, D_MODEL))
    inp["ffn1_w_in"] = nrm((L, D_MODEL, 2 * D_FF), D_MODEL ** -0.5)
    inp["ffn1_w_out"] = nrm((L, D_FF, D_MODEL), D_FF ** -0.5)
    inp["mix_norm_pre"] = gain((L, D_MODEL))
    inp["mix_norm_post"] = gain((L, D_MODEL))
    inp["mix_w_in"] = nrm((L, D_MODEL, P_IN), D_MODEL ** -0.5)
    inp["gdn_conv_w"] = nrm((L, GDN_CONV, W_Q + W_K + W_V), GDN_CONV ** -0.5)
    inp["gdn_a_log"] = jnp.log(jax.random.uniform(next(ks), (L, GDN_HEADS), jnp.float32, 1.0, 16.0))
    dt = jnp.exp(jax.random.uniform(next(ks), (L, GDN_HEADS), jnp.float32, np.log(1e-3), np.log(1e-1)))
    inp["gdn_dt_bias"] = dt + jnp.log(-jnp.expm1(-dt))
    inp["gdn_norm_w"] = gain((L, GDN_DV))
    inp["gdn_w_o"] = nrm((L, GDN_HEADS * GDN_DV, D_MODEL), (GDN_HEADS * GDN_DV) ** -0.5)
    inp["cnv_pw1_b"] = nrm((L, W_GLU), 0.02)
    inp["cnv_dw_w"] = nrm((L, CNV_K, CNV_CH), CNV_K ** -0.5)
    inp["cnv_dw_b"] = nrm((L, CNV_CH), 0.02)
    inp["cnv_ln_g"] = gain((L, CNV_CH))
    inp["cnv_ln_b"] = nrm((L, CNV_CH), 0.02)
    inp["cnv_w_o"] = nrm((L, CNV_CH, D_MODEL), CNV_CH ** -0.5)
    inp["cnv_b_o"] = nrm((L, D_MODEL), 0.02)
    inp["mix_w_out"] = nrm((L, D_MODEL, D_MODEL), D_MODEL ** -0.5)
    inp["ffn2_norm_pre"] = gain((L, D_MODEL))
    inp["ffn2_norm_post"] = gain((L, D_MODEL))
    inp["ffn2_w_in"] = nrm((L, D_MODEL, 2 * D_FF), D_MODEL ** -0.5)
    inp["ffn2_w_out"] = nrm((L, D_FF, D_MODEL), D_FF ** -0.5)
    return inp

def second_block(x, ffn1_norm_pre, ffn1_norm_post, ffn1_w_in, ffn1_w_out,
              mix_norm_pre, mix_norm_post, mix_w_in,
              gdn_conv_w, gdn_a_log, gdn_dt_bias, gdn_norm_w, gdn_w_o,
              cnv_pw1_b, cnv_dw_w, cnv_dw_b, cnv_ln_g, cnv_ln_b, cnv_w_o, cnv_b_o,
              mix_w_out,
              ffn2_norm_pre, ffn2_norm_post, ffn2_w_in, ffn2_w_out):
    for i in range(DEPTH):
        f = swiglu_ffn(rmsnorm_2(x, ffn1_norm_pre[i]), ffn1_w_in[i], ffn1_w_out[i])
        x = x + 0.5 * rmsnorm_2(f, ffn1_norm_post[i])

        h = rmsnorm_2(x, mix_norm_pre[i])
        p = h @ mix_w_in[i]
        qkv, z, beta_logit, a_logit, glu_in, gates = jnp.split(p, SPLITS, axis=-1)
        y_a = gated_deltanet(qkv, z, beta_logit, a_logit, gdn_conv_w[i], gdn_a_log[i],
                             gdn_dt_bias[i], gdn_norm_w[i], gdn_w_o[i])
        y_b = conformer_conv(glu_in, cnv_pw1_b[i], cnv_dw_w[i], cnv_dw_b[i],
                             cnv_ln_g[i], cnv_ln_b[i], cnv_w_o[i], cnv_b_o[i])
        g_a, g_b = jnp.split(jax.nn.sigmoid(gates), 2, axis=-1)
        y = (g_a * y_a + g_b * y_b) @ mix_w_out[i]
        x = x + rmsnorm_2(y, mix_norm_post[i])

        f = swiglu_ffn(rmsnorm_2(x, ffn2_norm_pre[i]), ffn2_w_in[i], ffn2_w_out[i])
        x = x + 0.5 * rmsnorm_2(f, ffn2_norm_post[i])
    return x


def setup_inputs(seed=0):
    out = dict(first_inputs(seed))
    for name, value in second_inputs(seed + 1).items():
        if name != "x":
            out[name + "_2"] = value
    return out


def reference(
    x, positions, norm_g, w_in, qk_norm_g, lambda_params, diff_subln_g, w_branch, w_out,
    ffn_w_gate, ffn_w_up, ffn_w_down, ffn1_norm_pre_2, ffn1_norm_post_2, ffn1_w_in_2,
    ffn1_w_out_2, mix_norm_pre_2, mix_norm_post_2, mix_w_in_2, gdn_conv_w_2, gdn_a_log_2,
    gdn_dt_bias_2, gdn_norm_w_2, gdn_w_o_2, cnv_pw1_b_2, cnv_dw_w_2, cnv_dw_b_2, cnv_ln_g_2,
    cnv_ln_b_2, cnv_w_o_2, cnv_b_o_2, mix_w_out_2, ffn2_norm_pre_2, ffn2_norm_post_2,
    ffn2_w_in_2, ffn2_w_out_2,
):
    x = first_block(
        x, positions, norm_g, w_in, qk_norm_g, lambda_params, diff_subln_g, w_branch, w_out,
        ffn_w_gate, ffn_w_up, ffn_w_down,
    )
    return second_block(
        x, ffn1_norm_pre_2, ffn1_norm_post_2, ffn1_w_in_2, ffn1_w_out_2, mix_norm_pre_2,
        mix_norm_post_2, mix_w_in_2, gdn_conv_w_2, gdn_a_log_2, gdn_dt_bias_2, gdn_norm_w_2,
        gdn_w_o_2, cnv_pw1_b_2, cnv_dw_w_2, cnv_dw_b_2, cnv_ln_g_2, cnv_ln_b_2, cnv_w_o_2,
        cnv_b_o_2, mix_w_out_2, ffn2_norm_pre_2, ffn2_norm_post_2, ffn2_w_in_2, ffn2_w_out_2,
    )


_drawn_inputs = setup_inputs


def setup_inputs(seed=0):
    import zlib

    import numpy as np

    out = dict(_drawn_inputs(seed))
    spreads = {}
    factors = {'ffn1_norm_pre_2': 3.247,
     'ffn1_norm_post_2': 4.784,
     'mix_norm_post_2': 3.25,
     'gdn_norm_w_2': 11.846,
     'cnv_pw1_b_2': 4.087,
     'cnv_ln_g_2': 9.733,
     'cnv_ln_b_2': 4.214,
     'ffn2_norm_pre_2': 4.865,
     'ffn2_norm_post_2': 20.233,
     'cnv_b_o_2': 7.399}
    for name, (base, spread) in spreads.items():
        noise = np.random.default_rng([zlib.crc32(name.encode()), seed]).standard_normal(out[name].shape)
        drawn = base * np.exp(spread * noise) if base else spread * noise
        out[name] = __import__('jax').numpy.asarray(drawn.astype(out[name].dtype))
    for name, factor in factors.items():
        out[name] = (out[name] * factor).astype(out[name].dtype)
    return out
```

```python
import math
from contextlib import ExitStack

import numpy as np

import concourse.bass as bass
from concourse import mybir

F32 = mybir.dt.float32
I32 = mybir.dt.int32
ALU = mybir.AluOpType
ACT = mybir.ActivationFunctionType
AX = mybir.AxisListType

P = 128
D = 1024
KB = D // P
S = 256
QT = S // P
LAYERS = 2
WIDE = 15616
DFF = 2816
FB = DFF // P
EPS = 1e-6
LN_EPS = 1e-5
NEG = -1e30
TAKEN = -3e38
HD = 64
TOPK = 64
SLOTS = 4
SLOT = 2048
CHUNKS = DFF // 256
TAPS = 31
CTAPS = 4
TWO_PI = 2.0 * math.pi

QA, KA, VA, QI, KI, WI = 0, 256, 320, 384, 896, 960
QB, KBC, VB, QC, KC, VC, GATES = 968, 1224, 1480, 1736, 2248, 2760, 3272
IN_WIDTH = 6344
M_QKV, M_Z, M_BETA, M_A, M_GLU, M_GATES = 0, 3072, 4096, 4104, 4112, 6160
M_WIDTH = 8208
R2 = 55
(G_F1, G_P1, G_MX, G_PM, G_F2, G_P2, B_A, B_G, W_B, LN_G, LN_B, B_O, W_DW, W_CV) = (
    0, 1, 2, 3, 4, 5, 6, 7, 8, 9, 10, 11, 12, 43)
ROWS = 3 * LAYERS + R2 * LAYERS
SMALL = 7 * LAYERS + LAYERS

T1 = 3 * 2 * CHUNKS + 26 + 8
T2 = 3 * 2 * CHUNKS + 34 + 12
assert T1 % SLOTS == 0 and T2 % SLOTS == 0


MIX1_TILES = [("KI", KI, 72), ("QI0", QI, 256), ("QI1", QI + 256, 256), ("KA", KA, 128), ("QA", QA, 256),
              ("QB", QB, 256), ("KB", KBC, 256), ("VB", VB, 256), ("QC0", QC, 256), ("QC1", QC + 256, 256),
              ("KC0", KC, 256), ("KC1", KC + 256, 256), ("VC0", VC, 256), ("VC1", VC + 256, 256)]
N_PROJ = len(MIX1_TILES)
MIX1_TILES += [("GATE", GATES + 256 * i, 256) for i in range(12)]
HEAD_AT = {"KI": (0, None), "KA": (1, 1), "QI0": (2, None), "QI1": (4, None), "QA": (6, 0), "QB": (8, 2),
           "KB": (10, 3), "QC0": (12, 4), "QC1": (14, 4), "KC0": (16, 5), "KC1": (18, 5)}
MIX2_TILES = ([("BETA", M_BETA, 8), ("A", M_A, 8)]
              + [(n, c + 256 * i, 256) for i in range(4) for n, c in (("GLU_A", M_GLU), ("GLU_G", M_GLU + D))]
              + [("QKV", M_QKV + 256 * i, 256) for i in range(12)]
              + [("Z", M_Z + 256 * i, 256) for i in range(4)]
              + [("GATE", M_GATES + 256 * i, 256) for i in range(8)])
UNITS = [(g, q) for g in ("B", "C0", "C1", "A") for q in range(QT)]


INDEX_HEADS = [(0, (0, 2, 4, 6)), (0, (1, 3, 5, 7)), (1, (0, 2)), (1, (1, 3)), (1, (4, 6)), (1, (5, 7))]


class Track:

    def __init__(self, sem, plan, name, env):
        self.sem, self.names, self.env = sem, [], env
        self.plan = plan.setdefault(name, [])

    def did(self, event):
        assert event not in self.names, event
        self.names.append(event)
        return 1

    def at(self, event):
        if event not in self.plan:
            self.env.missing.append((self, event))
            return 1
        return self.env.lay * len(self.plan) + self.plan.index(event) + 1


class Tiles:

    def __init__(self, quads):
        self.quads, self.k, self.it = quads, 0, 0

    def slot(self):
        return self.k % SLOTS

    def landed(self):
        return (self.quads + self.it + (self.k // SLOTS + 1)) * 16

    def free(self):
        return (self.quads + self.it) * SLOTS + (self.k + 1)


class Env:
    pass


def program(nc, a, out, plan):
    env = Env()
    env.lay, env.missing = 0, []
    tracks = {}
    with ExitStack() as ctx:
        def sb(name, shape, dt=F32):
            return ctx.enter_context(nc.sbuf_tensor(name, [P] + shape, dt))[:]

        def sem(name):
            return ctx.enter_context(nc.semaphore(name))

        def track(name):
            tracks[name] = Track(sem(name), plan, name, env)
            return tracks[name]

        ring = sb("ring", [SLOTS, SLOT])
        x = sb("x", [KB, S])
        xn = sb("xn", [KB, S])
        sq = sb("sq", [KB, S])
        lnb = sb("lnb", [2, 2 * S])
        rstd = sb("rstd", [2, 2 * S])
        hid = sb("hid", [24 * S])
        act2 = sb("act2", [2, S])
        heads = sb("heads", [24, S])
        oT = sb("oT", [KB, S])
        ident = sb("ident", [P])
        ones = sb("ones", [P])
        ones64 = sb("ones64", [P])
        rot = sb("rot", [P])
        cmask = sb("cmask", [S])
        cosT = sb("cosT", [S])
        sinT = sb("sinT", [S])
        consts = sb("consts", [4])
        cols = sb("cols", [KB, ROWS])
        small = sb("small", [SMALL])
        lam = sb("lam", [LAYERS])
        gd = sb("gd", [2, 8])
        g1 = sb("g1", [KB, 3])
        h1 = sb("h1", [8])
        g2 = sb("g2", [KB, R2])
        h2 = sb("h2", [4])
        levels = sb("levels", [7, P])
        tmask = sb("tmask", [P])
        sel = sb("sel", [8, P])
        W = sb("W", [WIDE])
        PS = ctx.enter_context(nc.psum_tensor("PS", [P, 8, 512], F32))

        landed = [sem(f"weights_landed_{i}") for i in range(SLOTS)]
        released = sem("weights_released")
        gu_ready = sem("ffn_gate_up_ready")
        silu_ready = sem("ffn_silu_ready")
        hid_done = sem("ffn_hidden_done")
        down_ready = sem("ffn_down_ready")
        x_upd = sem("residual_updated")
        passed = {e: sem(f"wait_passed_{e}") for e in ("sync", "vector", "tensor")}
        params_in = sem("params_loaded")
        out_done = sem("output_written")
        out_ready = sem("output_block_ready")
        pro_pe, pro_act, pro_dve, pro_pool = (track("setup_" + e) for e in ("products", "scalar", "vector", "pool"))
        names = ("norm", "mix", "soft")
        first = {n: [track(f"first_{n}_{e}") for e in ("products", "scalar", "vector", "pool")] for n in names}
        second = {n: [track(f"second_{n}_{e}") for e in ("products", "scalar", "vector", "pool")] for n in
                  ("norm", "mix", "delta", "conv")}

        def bc(ap, n):
            return ap.unsqueeze(1).to_broadcast([ap.shape[0], n, ap.shape[1]])

        def bcl(ap, n):
            return ap.unsqueeze(2).to_broadcast([ap.shape[0], ap.shape[1], n])

        def bank(b, lo=0, hi=512):
            return PS[:, b, lo:hi]

        def slot(s):
            return ring[:, s, :]

        def hold(e, who, s, value):
            e.wait_ge(s, value)
            e.sem_inc(passed[who], 1)

        block = ctx.enter_context(nc.Block())

        off = [0]

        def view(width):
            at = off[0]
            off[0] += width
            assert off[0] <= WIDE, off[0]
            return W[:, at:at + width]

        rows = view(D)
        srow = view(P)
        xin = view(QT * D).rearrange("p (t d) -> p t d", t=QT)
        pos_i = view(S).bitcast(I32)
        posf = view(S)
        ang = view(S)
        red = view(S)
        red2 = view(S)
        lamb = view(LAYERS * 4 * HD)
        lprod = view(LAYERS * 2 * HD)
        lsum = view(LAYERS * 2)
        lexp = view(LAYERS * 2)
        invrow = view(P)
        invf = view(1)
        inv_freq = [float(np.float32(500000.0) ** np.float32(-2.0 * i / 16)) for i in range(8)]
        lam_init = [0.8 - 0.6 * math.exp(-0.3 * i) for i in range(LAYERS)]
        N_PARAM = 0

        def load_params(q):
            n = 0

            def ld(dst, src):
                nonlocal n
                q.dma_start(dst, src, allow_slow_non_contiguous=dst.shape[0] == 8).then_inc(params_in, 16)
                n += 16
            ld(xin, a["x"].rearrange("a (t p) d -> p (a t) d", p=P))
            ld(rows[0:6, :], a["norm_g"].rearrange("l r d -> (l r) d"))
            for l in range(LAYERS):
                r = 6 + R2 * l
                for at, key in ((G_F1, "ffn1_norm_pre_2"), (G_P1, "ffn1_norm_post_2"), (G_MX, "mix_norm_pre_2"),
                                (G_PM, "mix_norm_post_2"), (G_F2, "ffn2_norm_pre_2"), (G_P2, "ffn2_norm_post_2"),
                                (W_B, "cnv_dw_b_2"), (LN_G, "cnv_ln_g_2"), (LN_B, "cnv_ln_b_2"), (B_O, "cnv_b_o_2")):
                    ld(rows[r + at:r + at + 1, :], a[key][l:l + 1, :])
                ld(rows[r + B_A:r + B_A + 2, :], a["cnv_pw1_b_2"][l].rearrange("(r d) -> r d", d=D))
                ld(rows[r + W_DW:r + W_DW + TAPS, :], a["cnv_dw_w_2"][l])
                ld(rows[r + W_CV:r + W_CV + 3 * CTAPS, :], a["gdn_conv_w_2"][l].rearrange("t (s d) -> (t s) d", d=D))
                ld(srow[7 * l:7 * l + 6, 0:HD], a["qk_norm_g"][l])
                ld(srow[7 * l:7 * l + 6, HD:P], a["qk_norm_g"][l])
                ld(srow[7 * l + 6:7 * l + 7, :], a["diff_subln_g"][l:l + 1, :])
                ld(srow[14 + l:15 + l, :], a["gdn_norm_w_2"][l:l + 1, :])
            ld(pos_i, a["positions"].to_broadcast([P, S]))
            ld(lamb, a["lambda_params"].rearrange("l r d -> (l r d)").unsqueeze(0).to_broadcast([P, LAYERS * 4 * HD]))
            ld(gd[0:8, 0, 0:LAYERS], a["gdn_a_log_2"].rearrange("l h -> h l"))
            ld(gd[0:8, 1, 0:LAYERS], a["gdn_dt_bias_2"].rearrange("l h -> h l"))
            return n
        N_PARAM = 16 * (2 + LAYERS * 17 + 4)

        def load_tile(sp, t, parts, width=256):
            hold(sp, "sync", released, t.free())
            dst = slot(t.slot())
            if width is None:
                sp.dma_start(dst.rearrange("p (k n) -> p k n", k=2), parts).then_inc(landed[t.slot()], 16)
            else:
                cells = dst.rearrange("p (k n) -> p k n", k=KB)
                sp.dma_start(cells[:, :, 0:parts.shape[-1]], parts).then_inc(landed[t.slot()], 16)
            t.k += 1

        def kmajor(w2d):
            return w2d.rearrange("(k p) n -> p k n", p=P)

        def load_ffn(sp, t, gate, up, down):
            with sp.Fori(0, CHUNKS // 2) as it:
                t.it = it
                for cc in range(2):
                    for w in (gate, up):
                        load_tile(sp, t, w[:, :, bass.ds(it * 512 + cc * 256, 256)])
            t.it = CHUNKS // 2 - 1
            for w in (gate, up):
                load_tile(sp, t, w[:, :, (CHUNKS - 1) * 256:CHUNKS * 256])
            load_tile(sp, t, kmajor(down[0:256, :]), None)
            at = t.it
            with sp.Fori(0, 2) as it:
                t.it = it + at
                for c in range(4):
                    load_tile(sp, t, kmajor(down[bass.ds(it * 1024 + (1 + c) * 256, 256), :]), None)
            t.it = at + 1
            for c in range(9, CHUNKS):
                load_tile(sp, t, kmajor(down[c * 256:(c + 1) * 256, :]), None)
            t.k += SLOTS * t.it
            t.it = 0

        @block.sync
        def _(sp):
            sp.sem_inc(released, SLOTS - 1)
            with sp.Fori(0, LAYERS) as lay:
                t = Tiles(lay * (T1 // SLOTS))
                for half in range(2):
                    if half == 1:
                        w = kmajor(a["w_in"][lay])
                        for _, c, n in MIX1_TILES:
                            load_tile(sp, t, w[:, :, c:c + n])
                        for key in ("w_branch", "w_out"):
                            for c in range(4):
                                load_tile(sp, t, kmajor(a[key][lay][c * 256:(c + 1) * 256, :]), None)
                    load_ffn(sp, t, kmajor(a["ffn_w_gate"][lay, half]), kmajor(a["ffn_w_up"][lay, half]),
                             a["ffn_w_down"][lay, half])
                assert t.k == T1
            if BLOCKS > 1:
                with sp.Fori(0, LAYERS) as lay:
                    t = Tiles(lay * (T2 // SLOTS) + LAYERS * (T1 // SLOTS))
                    for half in range(2):
                        if half == 1:
                            w = kmajor(a["mix_w_in_2"][lay])
                            for _, c, n in MIX2_TILES:
                                load_tile(sp, t, w[:, :, c:c + n])
                            for key in ("gdn_w_o_2", "cnv_w_o_2", "mix_w_out_2"):
                                for c in range(4):
                                    load_tile(sp, t, kmajor(a[key][lay][c * 256:(c + 1) * 256, :]), None)
                        w = kmajor(a[f"ffn{half + 1}_w_in_2"][lay])
                        load_ffn(sp, t, w[:, :, 0:DFF], w[:, :, DFF:2 * DFF], a[f"ffn{half + 1}_w_out_2"][lay])
                    assert t.k == T2
            ov = out.rearrange("a (t p) d -> p (a t) d", p=P)
            for q in range(QT):
                sp.wait_ge(out_ready, 2 * q + 2)
                sp.dma_start(ov[:, q, :], xn[:, 4 * q:4 * q + 4, :].rearrange("p k s -> p (k s)")).then_inc(out_done, 16)
            sp.wait_ge(out_done, 16 * QT)

        off[0] = 0
        ybuf = view(2 * 512).rearrange("p (i n) -> p i n", i=2)
        tbuf = view(2 * 512).rearrange("p (i n) -> p i n", i=2)
        ubuf = view(2 * 512).rearrange("p (i n) -> p i n", i=2)
        va = view(QT * HD).rearrange("p (t n) -> p t n", t=QT)
        wi = view(QT * 8).rearrange("p (t n) -> p t n", t=QT)
        vb = view(QT * 256).rearrange("p (t n) -> p t n", t=QT)
        vc = view(QT * 512).rearrange("p (t n) -> p t n", t=QT)
        rl = view(2 * 512).rearrange("p (i n) -> p i n", i=2)
        isc = [view(P), view(S)]
        work = [view(P), view(S)]
        top8 = view(8)
        ibias = [view(P), view(S)]
        smb = view(2 * 1024).rearrange("p (i n) -> p i n", i=2)
        ptb = view(2 * 1024).rearrange("p (i n) -> p i n", i=2)
        nmax = view(8).rearrange("p (i n) -> p i n", i=2)
        rsum = view(8).rearrange("p (i n) -> p i n", i=2)
        rinv = view(8).rearrange("p (i n) -> p i n", i=2)

        off[0] = 0
        conv = view(KB * S).rearrange("p (k s) -> p k s", k=KB)
        ab = view(2 * S).rearrange("p (i s) -> p i s", i=2)
        lg = view(4 * S).rearrange("p (i s) -> p i s", i=4)
        gtok = view(QT * 8).rearrange("p (t h) -> p t h", t=QT)
        ngtok = view(QT * 8).rearrange("p (t h) -> p t h", t=QT)
        btok = view(QT * 8).rearrange("p (t h) -> p t h", t=QT)
        bgtok = view(QT * 8).rearrange("p (t h) -> p t h", t=QT)
        cdec = view(4)
        shared_at = off[0]
        glu = view(KB * (S + TAPS - 1)).rearrange("p (k s) -> p k s", k=KB)
        gth = view(2 * 512).rearrange("p (i n) -> p i n", i=2)
        qpad = view(2 * 2 * (S + CTAPS - 1)).rearrange("p (i b s) -> p i b s", i=2, b=2)
        off[0] = shared_at
        DU = {}
        for c in range(QT):
            for n in ("gbm", "at", "al", "qkt", "kx", "vx", "T", "U", "m1", "u"):
                DU[n, c] = view(512).rearrange("p (h n) -> p h n", h=4)
        qd = view(512).rearrange("p (h n) -> p h n", h=4)
        wT = view(512).rearrange("p (h n) -> p h n", h=4)
        st = view(512).rearrange("p (h n) -> p h n", h=4)

        acc = lambda m, b0=0: bank(b0 + m // 2, (m % 2) * S, (m % 2 + 1) * S)
        pair = lambda b: PS[:, b, :].rearrange("p (i s) -> p i s", i=2)

        def hidb(j, n=1):
            return hid[:, j * S:(j + n) * S]

        def sqp(i):
            return sq[:, 2 * i:2 * i + 2, :].rearrange("p k s -> p (k s)")

        def blk2(buf, i):
            return buf[:, 2 * i:2 * i + 2, :].rearrange("p k s -> p (k s)")

        chain = [n for n, _, _ in MIX1_TILES[:N_PROJ] if n in HEAD_AT]
        mm = nc.tensor.matmul
        act_ = nc.scalar.activation
        v_ = nc.vector

        def pe_down(pe, t, b0, tiles, rhs, ready, sig):
            for c in range(tiles):
                pe.wait_ge(landed[t.slot()], t.landed())
                w = slot(t.slot()).rearrange("p (k n) -> p k n", k=2)
                ready(c)
                last = c == tiles - 1
                order = [(f, m) for m in range(KB) for f in range(2)] if last else [(f, m) for f in range(2) for m in range(KB)]
                for i, (f, m) in enumerate(order):
                    ins = mm(acc(m, b0), w[:, f, m * P:(m + 1) * P], rhs(2 * c + f),
                             start=(c == 0 and f == 0 and m % 2 == 0), stop=(last and f == 1), skip_group_check=True)
                    if i == 0:
                        ins.then_inc(released, 1)
                    elif last and f == 1 and m % 2 == 1:
                        tr, name = sig
                        ins.then_inc(tr.sem, tr.did(f"{name}.{m // 2}"))
                t.k += 1

        def pe_sum(pe, tr, tag, bnk, ready, src=None):
            for k in range(KB):
                ready(k)
                ins = mm(bank(bnk, 0, S), ones, (sq if src is None else src)[:, k, :], start=(k == 0), stop=(k == KB - 1))
            ins.then_inc(tr[0].sem, tr[0].did(tag + ".sum"))

        def pe_norm(pe, tr, tag, bnk=7, who="sq"):
            def ready(k):
                if k % 2 == 0:
                    pe.wait_ge(tr[1].sem, tr[1].at(f"{tag}.sq{k // 2}"))
            pe_sum(pe, tr, tag, bnk, ready)

        def pe_ffn(pe, t, f, tr, tag):
            hold(pe, "tensor", tr[2].sem, tr[2].at(tag + ".xn7"))

            def chunk(cc, it):
                gs, gl = t.slot(), t.landed()
                t.k += 1
                us, ul = t.slot(), t.landed()
                t.k += 1
                gw = slot(gs).rearrange("p (k n) -> p k n", k=KB)
                uw = slot(us).rearrange("p (k n) -> p k n", k=KB)
                for b in range(2):
                    j = 2 * cc + b
                    pe.wait_ge(hid_done, f * FB + it * 4 + (j + 1))
                    for w, sm_, lv, o in ((gw, gs, gl, 0), (uw, us, ul, S)):
                        if b == 0:
                            pe.wait_ge(landed[sm_], lv)
                        for k in range(KB):
                            ins = mm(bank(4 + j, o, o + S), w[:, k, b * P:(b + 1) * P], xn[:, k, :],
                                     start=(k == 0), stop=(k == KB - 1))
                            if b == 0 and o == 0 and k == 0:
                                ins.then_inc(released, 1)
                        if b == 1 and o == 0:
                            ins.then_inc(released, 1)
                    ins.then_inc(gu_ready, 1)

            k0 = t.k
            with pe.Fori(0, CHUNKS // 2) as it:
                t.it, t.k = it, k0
                for cc in range(2):
                    chunk(cc, it)
            t.it, t.k = CHUNKS // 2, k0
            chunk(0, CHUNKS // 2)

            def down(c, r):
                hold(pe, "tensor", landed[t.slot()], t.landed())
                w = slot(t.slot()).rearrange("p (k n) -> p k n", k=2)
                last = c == CHUNKS - 1
                order = [(h, m) for m in range(KB) for h in range(2)] if last else [(h, m) for h in range(2) for m in range(KB)]
                for i, (h, m) in enumerate(order):
                    ins = mm(acc(m), w[:, h, m * P:(m + 1) * P], r(h),
                             start=(c == 0 and h == 0 and m % 2 == 0), stop=(last and h == 1), skip_group_check=True)
                    if i == 0:
                        ins.then_inc(released, 1)
                    elif last and h == 1 and m % 2 == 1:
                        ins.then_inc(down_ready, 1)
                t.k += 1

            pe.wait_ge(hid_done, f * FB + (4 + FB))
            down(0, lambda h: hidb(h))
            k0, at = t.k, t.it
            with pe.Fori(0, 2) as it:
                t.it, t.k = it + at, k0
                for c in range(4):
                    down(1 + c, lambda h: hid[:, bass.ds(it * (8 * S) + (2 + 2 * c + h) * S, S)])
            t.it, t.k = at + 2, k0
            for c in range(9, CHUNKS):
                down(c, lambda h: hidb(2 * c + h))
            t.k += SLOTS * t.it
            t.it = 0

        def pe_mix1(pe, t, tr, so):
            pe.wait_ge(first["norm"][2].sem, first["norm"][2].at("mix.xn7"))
            evac = {n: (f"act", f"cp.{n}") if n.startswith("V") or HEAD_AT[n][1] is None else ("dve", f"y.{n}")
                    for n, _, _ in MIX1_TILES[:N_PROJ]}
            who = {"act": tr[1], "dve": tr[2]}
            for i in range(N_PROJ + 3):
                if i < N_PROJ:
                    name, _, width = MIX1_TILES[i]
                    b = i % 4
                    if i >= 4:
                        e, ev = evac[MIX1_TILES[i - 4][0]]
                        pe.wait_ge(who[e].sem, who[e].at(ev))
                    if i == 4:
                        pe.wait_ge(tr[1].sem, tr[1].at("cp2.KI"))
                    if i == 7:
                        pe.wait_ge(tr[1].sem, tr[1].at("cp2.KA"))
                    pe.wait_ge(landed[t.slot()], t.landed())
                    w = slot(t.slot()).rearrange("p (k n) -> p k n", k=KB)
                    paid = [False]

                    def go(o, lhs, rhs, k):
                        ins = mm(o, lhs, rhs, start=(k == 0), stop=(k == KB - 1))
                        if not paid[0]:
                            ins.then_inc(released, 1)
                            paid[0] = True
                        return ins
                    if name in ("KI", "KA"):
                        for h in range(2):
                            for k in range(KB):
                                go(PS[h * HD:(h + 1) * HD, b, 0:S], w[:, k, 0:HD], xn[:, k, :], k)
                        n = width - HD
                        for q in range(QT):
                            for k in range(KB):
                                ins = go(bank(b, S + q * n, S + (q + 1) * n), xn[:, k, q * P:(q + 1) * P],
                                         w[:, k, HD:width], k)
                    elif name.startswith("V"):
                        for q in range(QT):
                            for k in range(KB):
                                ins = go(bank(b, q * 256, (q + 1) * 256), xn[:, k, q * P:(q + 1) * P], w[:, k, :], k)
                    else:
                        for m in range(2):
                            for k in range(KB):
                                ins = go(bank(b, m * S, (m + 1) * S), w[:, k, m * P:(m + 1) * P], xn[:, k, :], k)
                    ins.then_inc(tr[0].sem, tr[0].did("p." + name))
                    t.k += 1
                if 1 <= i <= N_PROJ:
                    name = MIX1_TILES[i - 1][0]
                    if name in HEAD_AT and HEAD_AT[name][1] is not None:
                        n = S if name == "KA" else 512
                        pe.wait_ge(tr[1].sem, tr[1].at("sq." + name))
                        normed = [n_ for n_ in chain if HEAD_AT[n_][1] is not None]
                        if normed.index(name):
                            pe.wait_ge(tr[1].sem, tr[1].at(normed[normed.index(name) - 1] + ".ln"))
                        mm(bank(4, 0, n), ones64[:], sqp(chain.index(name) % 2)[:, 0:n],
                           start=True, stop=True).then_inc(tr[0].sem, tr[0].did("ss." + name))
                if 2 <= i <= N_PROJ + 1:
                    name = MIX1_TILES[i - 2][0]
                    if name in HEAD_AT:
                        c = chain.index(name)
                        n = S if name in ("KA", "KI") else 512
                        e, ev = (who["act"], "cp." + name) if HEAD_AT[name][1] is None else (who["dve"], "y." + name)
                        pe.wait_ge(e.sem, e.at(ev))
                        if c:
                            pe.wait_ge(tr[2].sem, tr[2].at("t." + chain[c - 1]))
                        mm(bank(5, 0, n), rot[:], ybuf[:, c % 2, 0:n], start=True,
                           stop=True).then_inc(tr[0].sem, tr[0].did("rot." + name))
                if 5 <= i <= 10:
                    j = i - 5
                    if j == 0:
                        pe.wait_ge(tr[2].sem, tr[2].at("h.QI1"))
                    if j >= 2:
                        pe.wait_ge(tr[1].sem, tr[1].at(f"relu{j - 2}"))
                    q, hs = INDEX_HEADS[j]
                    nk = P * (q + 1)
                    for i_, h in enumerate(hs):
                        r = slice((h % 2) * HD, (h % 2 + 1) * HD)
                        ins = mm(bank(6 + j % 2, i_ * nk, (i_ + 1) * nk),
                                 heads[r, 2 + h // 2, q * P:(q + 1) * P], heads[r, 0, 0:nk], start=True, stop=True)
                    ins.then_inc(tr[0].sem, tr[0].did(f"index{j}"))

            maps = {"A": [(6 + i, 1, c) for c in range(2) for i in range(2)],
                    "B": [(8 + i, 10 + i, c) for c in range(2) for i in range(2)],
                    "C0": [(12 + i, 16 + i, c) for c in range(2) for i in range(2)],
                    "C1": [(14 + i, 18 + i, c) for c in range(2) for i in range(2)]}
            g = [0]

            def gate():
                k = g[0]
                g[0] += 1
                if k >= 2:
                    pe.wait_ge(so[1].sem, so[1].at(f"gate{k - 2}"))
                pe.wait_ge(landed[t.slot()], t.landed())
                w = slot(t.slot()).rearrange("p (k n) -> p k n", k=KB)
                for m in range(2):
                    for k2 in range(KB):
                        ins = mm(bank(k % 2, m * S, (m + 1) * S), w[:, k2, m * P:(m + 1) * P], xn[:, k2, :],
                                 start=(k2 == 0), stop=(k2 == KB - 1))
                        if m == 0 and k2 == 0:
                            ins.then_inc(released, 1)
                ins.then_inc(so[0].sem, so[0].did(f"gate{k}"))
                t.k += 1

            pe.wait_ge(tr[2].sem, tr[2].at("h.KC1"))
            pe.wait_ge(tr[1].sem, tr[1].at("cp.VC1"))
            pe.wait_ge(tr[1].sem, tr[1].at("relu5"))
            for j in range(len(UNITS) + 2):
                if j < len(UNITS):
                    gr, q = UNITS[j]
                    if j >= 1:
                        pe.wait_ge(so[2].sem, so[2].at(f"sm{j - 1}"))
                    nk = P * (q + 1)
                    for m, (qb, kb, half) in enumerate(maps[gr]):
                        r = slice(half * HD, (half + 1) * HD)
                        o = (m % 2) * nk
                        ins = mm(bank(4 + half, o, o + nk), heads[r, qb, q * P:(q + 1) * P],
                                 heads[r, kb, 0:nk], start=True, stop=True)
                    ins.then_inc(so[0].sem, so[0].did(f"s{j}"))
                gate()
                if 1 <= j <= len(UNITS):
                    u = j - 1
                    gr, q = UNITS[u]
                    pe.wait_ge(so[2].sem, so[2].at(f"p{u}"))
                    if u >= 1:
                        pe.wait_ge(so[1].sem, so[1].at(f"pt{u - 1}"))
                    nm = 2 if gr[0] == "C" else 4
                    src = smb[:, u % 2, :].rearrange("p (m k n) -> p m k n", n=P, k=q + 1)
                    for m in range(nm):
                        for kb in range(q + 1):
                            i = m * (q + 1) + kb
                            ins = nc.tensor.transpose(bank(6 + i // 4, (i % 4) * P, (i % 4 + 1) * P),
                                                      src[:, m, kb, :], ident[:])
                    ins.then_inc(so[0].sem, so[0].did(f"t{u}"))
                if j >= 2:
                    u = j - 2
                    gr, q = UNITS[u]
                    pe.wait_ge(so[1].sem, so[1].at(f"pt{u}"))
                    gi = u // 2
                    if gi >= 2:
                        pe.wait_ge(so[1].sem, so[1].at(f"o{2 * (gi - 2) + 1}"))
                    if q == 1:
                        pe.wait_ge(so[1].sem, so[1].at(f"o{u - 1}"))
                    pt = ptb[:, u % 2, :].rearrange("p (m k n) -> p m k n", n=P, k=q + 1)
                    for m in range(2 if gr[0] == "C" else 4):
                        for kb in range(q + 1):
                            if gr == "A":
                                v, r, blk = va[:, kb, :], slice((m // 2) * HD, (m // 2 + 1) * HD), m % 2
                            elif gr == "B":
                                h = 2 * (m % 2) + m // 2
                                v, r, blk = vb[:, kb, h * HD:(h + 1) * HD], slice((m // 2) * HD, (m // 2 + 1) * HD), m % 2
                            else:
                                h = m + 2 * int(gr[1])
                                v, r, blk = vc[:, kb, h * P:(h + 1) * P], slice(0, P), m
                            o = blk * S + q * P
                            ins = mm(PS[r, 2 + gi % 2, o:o + P], v, pt[:, m, kb, :], start=(kb == 0), stop=(kb == q),
                                     skip_group_check=True)
                    ins.then_inc(so[0].sem, so[0].did(f"o{u}"))
                if j >= len(UNITS):
                    gate()
            def ready_a(c):
                if c == 0:
                    pe.wait_ge(so[1].sem, so[1].at("o7"))
                    pe.wait_ge(so[1].sem, so[1].at("gate11"))
            pe_down(pe, t, 0, 1, lambda k: oT[:, k, :], ready_a, (tr[0], "ya"))
            pe_down(pe, t, 4, 1, lambda k: oT[:, 2 + k, :], lambda c: None, (tr[0], "yb"))
            for i in range(2):
                pe.wait_ge(so[1].sem, so[1].at(f"sqc{i}"))
                if i == 0:
                    pe.wait_ge(tr[2].sem, tr[2].at("ma3"))
                mm(bank(i), ones[:], sqp(i), start=True,
                   stop=True).then_inc(so[0].sem, so[0].did(f"ssc{i}"))

            def ready_c(c):
                if c == 0:
                    pe.wait_ge(so[2].sem, so[2].at("nc1"))
            pe_down(pe, t, 0, 2, lambda k: oT[:, 4 + k, :], ready_c, (tr[0], "yc"))

            def ready_o(c):
                if c == 0:
                    pe.wait_ge(tr[2].sem, tr[2].at("mc3"))
            pe_down(pe, t, 0, 4, lambda k: xn[:, k, :], ready_o, (tr[0], "out"))

        mix2 = []
        for n, c, w_ in MIX2_TILES:
            mix2.append(n + str(sum(m.startswith(n + "") and m[:len(n)] == n and m[len(n):].isdigit() for m in mix2)))
        m2 = second["mix"]
        dl = second["delta"]
        cv = second["conv"]

        def evac2(i):
            n = mix2[i]
            if n.startswith("A"):
                return m2[2], "cp." + n
            if n.startswith("GLU_A"):
                return m2[2], f"glu.{n[5:]}.1"
            if n.startswith("GLU_G"):
                return m2[1], f"gth.{n[5:]}.1"
            return m2[1], "cp." + n

        def pe_tile2(pe, t, i):
            name = mix2[i]
            if i >= 4:
                tr, ev = evac2(i - 4)
                pe.wait_ge(tr.sem, tr.at(ev))
            pe.wait_ge(landed[t.slot()], t.landed())
            w = slot(t.slot()).rearrange("p (k n) -> p k n", k=KB)
            n = MIX2_TILES[i][2]
            for m in range((n + P - 1) // P):
                cn = min(n, P)
                for k in range(KB):
                    ins = mm(PS[0:cn, i % 4, m * S:(m + 1) * S], w[:, k, m * P:m * P + cn], xn[:, k, :],
                             start=(k == 0), stop=(k == KB - 1))
                    if m == 0 and k == 0:
                        ins.then_inc(released, 1)
            ins.then_inc(m2[0].sem, m2[0].did("p." + name))
            t.k += 1

        def pe_mix2(pe, t):
            pe.wait_ge(second["norm"][2].sem, second["norm"][2].at("mix.xn7"))
            first_z = mix2.index("Z0")
            for i in range(len(mix2)):
                pe_tile2(pe, t, i)
                if i == 9:
                    for j, ev in ((0, "gsum1"), (1, "beta")):
                        hold(pe, "tensor", m2[2].sem, m2[2].at(ev))
                        for c in range(QT):
                            src = lg[0:8, 3, c * P:(c + 1) * P] if j == 0 else ab[0:8, 1, c * P:(c + 1) * P]
                            ins = nc.tensor.transpose(bank(4, 16 * j + 8 * c, 16 * j + 8 * c + 8), src, ident[0:8, 0:8])
                    ins.then_inc(m2[0].sem, m2[0].did("tok"))
                if i in (first_z, first_z + 1):
                    for j in range(4 * (i - first_z), 4 * (i - first_z) + 4):
                        pe.wait_ge(m2[1].sem, m2[1].at(f"l2sq{j}"))
                        if j >= 4:
                            pe.wait_ge(m2[1].sem, m2[1].at(f"l2.{j - 4}.ln"))
                        mm(bank(4 + j % 4), ones, sqp(j % 4), start=True,
                           stop=True).then_inc(m2[0].sem, m2[0].did(f"l2s{j}"))
            def conv_ready(k):
                if k == 0:
                    pe.wait_ge(cv[2].sem, cv[2].at("cv.1.30.3"))
                    pe.wait_ge(m2[1].sem, m2[1].at("l2.7.ln"))
            pe_sum(pe, cv, "mean", 4, conv_ready, conv)
            pe_norm(pe, cv, "ln")
            pe_delta(pe)
            for i in range(4):
                pe.wait_ge(dl[1].sem, dl[1].at(f"osq{i}"))
                mm(bank(i), ones, sqp(i), start=True, stop=True).then_inc(dl[0].sem, dl[0].did(f"os{i}"))

            def ready_a(c):
                pe.wait_ge(dl[2].sem, dl[2].at("oz3"))
            pe_down(pe, t, 0, 4, lambda k: oT[:, k, :], ready_a, (m2[0], "ya"))
            pe_down(pe, t, 4, 4, lambda k: conv[:, k, :], lambda c: None, (m2[0], "yb"))

            def ready_o(c):
                pe.wait_ge(m2[2].sem, m2[2].at("mb3"))
            pe_down(pe, t, 0, 4, lambda k: xn[:, k, :], ready_o, (m2[0], "out"))

        def pe_delta(pe):
            did = lambda ins, n: ins.then_inc(dl[0].sem, dl[0].did(n))
            wv = lambda n: pe.wait_ge(dl[2].sem, dl[2].at(n))
            wa = lambda n: pe.wait_ge(dl[1].sem, dl[1].at(n))
            pe.wait_ge(cv[1].sem, cv[1].at("cvs7"))
            pe.wait_ge(m2[1].sem, m2[1].at("cp.GATE7"))

            def four(b, f):
                for h in range(4):
                    ins = f(h, bank(b, h * P, (h + 1) * P))
                return ins
            for g in range(2):
                for c in range(QT):
                    B = 4 * c
                    tk = slice(c * P, (c + 1) * P)
                    if g == 1:
                        wa(f"0.oc.{c}")
                        if c == 1:
                            wv("0.vn")
                        else:
                            wa("0.sc")
                    did(four(B, lambda h, o: mm(o, sel[0:8, 4 * g + h, :], lg[0:8, 3, tk], start=True, stop=True)), f"{g}.gb.{c}")
                    did(four(B + 1, lambda h, o: mm(o, sel[0:8, 4 * g + h, :], ab[0:8, 1, tk], start=True, stop=True)), f"{g}.bb.{c}")
                    if g == 0 and c == 0:
                        pe.wait_ge(m2[2].sem, m2[2].at("l2n7"))
                    did(four(B + 2, lambda h, o: mm(o, heads[:, 8 + 4 * g + h, tk], heads[:, 8 + 4 * g + h, tk], start=True, stop=True)), f"{g}.kk.{c}")
                    did(four(B + 3, lambda h, o: mm(o, heads[:, 8 + 4 * g + h, tk], heads[:, 4 * g + h, tk], start=True, stop=True)), f"{g}.qk.{c}")
                for c in range(QT):
                    B = 4 * c
                    tk = slice(c * P, (c + 1) * P)
                    wv(f"{g}.at0.{c}")
                    did(four(B + 2, lambda h, o: nc.tensor.transpose(o, heads[:, 8 + 4 * g + h, tk], ident)), f"{g}.kt.{c}")
                    wv(f"{g}.qkt.{c}")
                    did(four(B + 3, lambda h, o: nc.tensor.transpose(o, heads[:, 16 + 4 * g + h, tk], ident)), f"{g}.vt.{c}")
                for c in range(QT):
                    B = 4 * c
                    U = DU["U", c]
                    wv(f"{g}.U0.{c}")
                    if c == 1:
                        wa(f"{g}.eg")
                    else:
                        wv(f"{g}.cd0")
                    did(four(B, lambda h, o: nc.tensor.transpose(o, U[:, h, :], ident)), f"{g}.tt.{c}")
                for l in range(1, 7):
                    for c in range(QT):
                        B = 4 * c
                        al, T = DU["al", c], DU["T", c]
                        pe.wait_ge(dl[3].sem, dl[3].at(f"{g}.al{l}.{c}"))
                        if l == 1:
                            wa(f"{g}.T0.{c}")
                            wv(f"{g}.vx.{c}")
                        else:
                            wv(f"{g}.T{l - 1}.{c}")
                        did(four(B + 3, lambda h, o: mm(o, al[:, h, :], T[:, h, :], start=True, stop=True)), f"{g}.m{l}.{c}")
                    for c in range(QT):
                        B = 4 * c
                        U, m1 = DU["U", c], DU["m1", c]
                        wa(f"{g}.mc{l}.{c}")
                        did(four(B, lambda h, o: mm(o, m1[:, h, :], U[:, h, :], start=True, stop=True)), f"{g}.pu{l}.{c}")
                        if l < 6:
                            did(four(B + 1, lambda h, o: mm(o, U[:, h, :], m1[:, h, :], start=True, stop=True)), f"{g}.pt{l}.{c}")
                for c in range(QT):
                    B = 4 * c
                    U = DU["U", c]
                    wv(f"{g}.U6.{c}")
                    if c == 0:
                        wv(f"{g}.kx.{c}")
                    else:
                        wv(f"{g}.kx.{c}")
                    did(four(B + 2, lambda h, o: mm(o, U[:, h, :], DU["vx", c][:, h, :], start=True, stop=True)), f"{g}.u.{c}")
                did(four(5, lambda h, o: mm(o, DU["kx", 1][:, h, :], DU["U", 1][:, h, :], start=True, stop=True)), f"{g}.w")
                wa(f"{g}.uc.0")
                did(four(1, lambda h, o: mm(o, DU["kx", 0][:, h, :], DU["u", 0][:, h, :], start=True, stop=True)), f"{g}.s")
                did(four(3, lambda h, o: mm(o, DU["u", 0][:, h, :], DU["qkt", 0][:, h, :], start=True, stop=True)), f"{g}.o.0")
                wa(f"{g}.wc")
                wa(f"{g}.sc")
                did(four(4, lambda h, o: mm(o, wT[:, h, :], st[:, h, :], start=True, stop=True)), f"{g}.ws")
                wv(f"{g}.qd")

                wv(f"{g}.vn")

                def both(h, o):
                    mm(o, st[:, h, :], qd[:, h, :], start=True, stop=False)
                    return mm(o, DU["u", 1][:, h, :], DU["qkt", 1][:, h, :], start=False, stop=True)
                did(four(7, both), f"{g}.o.1")

        def pe_setup(pe):
            pe.wait_ge(params_in, N_PARAM)
            pe.wait_ge(pro_pool.sem, pro_pool.at("ident"))
            for b in range(4):
                for k in (2 * b, 2 * b + 1):
                    for q in range(QT):
                        o = (k % 2) * S + q * P
                        ins = nc.tensor.transpose(bank(b, o, o + P), xin[:, q, k * P:(k + 1) * P], ident[:])
                ins.then_inc(pro_pe.sem, pro_pe.did(f"x{b}"))
            for b in range(2):
                for k in range(4):
                    ins = nc.tensor.transpose(bank(4 + b, k * ROWS, (k + 1) * ROWS),
                                              rows[0:ROWS, (4 * b + k) * P:(4 * b + k + 1) * P], ident[0:ROWS, 0:ROWS])
                ins.then_inc(pro_pe.sem, pro_pe.did(f"cols{b}"))
            nc.tensor.transpose(bank(6, 0, SMALL), srow[0:SMALL, :], ident[0:SMALL, 0:SMALL])
            pe.wait_ge(pro_dve.sem, pro_dve.at("invrow"))
            pe.wait_ge(pro_pool.sem, pro_pool.at("ones"))
            mm(bank(7, 0, 1), invrow[0:1, :], ones[0:1, 0:1], start=True,
               stop=True).then_inc(pro_pe.sem, pro_pe.did("small"))

        def pe_finish(pe):
            for q in range(QT):
                for h in range(2):
                    b = 2 * q + h
                    if b == 0:
                        pe.wait_ge(x_upd, 4 + 4 * 3 * LAYERS * BLOCKS)
                    for k in range(4):
                        ins = nc.tensor.transpose(bank(4 + b, k * P, (k + 1) * P), x[:, 4 * h + k, q * P:(q + 1) * P],
                                                  ident[:])
                    ins.then_inc(pro_pe.sem, pro_pe.did(f"fin{b}"))

        @block.tensor
        def _(pe):
            pe_setup(pe)
            with pe.Fori(0, LAYERS) as lay:
                env.lay = lay
                t = Tiles(lay * (T1 // SLOTS))
                tr = first["norm"]
                pe_norm(pe, tr, "f0")
                pe_ffn(pe, t, lay * 2, tr, "f0")
                pe_norm(pe, tr, "mix")
                pe_mix1(pe, t, first["mix"], first["soft"])
                pe_norm(pe, tr, "f1")
                pe_ffn(pe, t, lay * 2 + 1, tr, "f1")
            if BLOCKS > 1:
                with pe.Fori(0, LAYERS) as lay:
                    env.lay = lay
                    t = Tiles(lay * (T2 // SLOTS) + LAYERS * (T1 // SLOTS))
                    tr = second["norm"]
                    pe_norm(pe, tr, "f0")
                    pe_ffn(pe, t, lay * 2 + 4, tr, "f0")
                    pe_norm(pe, tr, "pf0")
                    pe_norm(pe, tr, "mix")
                    pe_mix2(pe, t)
                    pe_norm(pe, tr, "pmix")
                    pe_norm(pe, tr, "f1")
                    pe_ffn(pe, t, lay * 2 + 5, tr, "f1")
                    pe_norm(pe, tr, "pf1")
            env.lay = 0
            pe_finish(pe)

        def act_rstd(e, tr, tag, src, scale, eps, n, i=0, ready=None, name=None):
            act_(lnb[:, i, 0:n], src, ACT.Ln, bias=consts[:, eps:eps + 1], scale=scale).then_inc(
                tr[1].sem, tr[1].did(f"{tag}.ln"))
            e.wait_ge(tr[1].sem, tr[1].at(f"{tag}.ln"))
            act_(rstd[:, i, 0:n], lnb[:, i, 0:n], ACT.Exp, scale=-0.5).then_inc(
                tr[1].sem, tr[1].did(f"{tag}.rstd"))

        def act_norm(e, tr, tag, upd, bnk=7):
            for k in range(4):
                e.wait_ge(x_upd, upd + (k + 1))
                act_(sqp(k), blk2(x, k), ACT.Square).then_inc(tr[1].sem, tr[1].did(f"{tag}.sq{k}"))
            e.wait_ge(tr[0].sem, tr[0].at(tag + ".sum"))
            act_rstd(e, tr, tag, bank(bnk, 0, S), 1.0 / D, 0, S)

        def act_post(e, tr, tag, ready, scale=1.0):
            for k in range(4):
                ready(k)
                act_(sqp(k), bank(k), ACT.Square, scale=scale).then_inc(tr[1].sem, tr[1].did(f"{tag}.sq{k}"))
            e.wait_ge(tr[0].sem, tr[0].at(tag + ".sum"))
            act_rstd(e, tr, tag, bank(7, 0, S), 1.0 / D, 0, S)

        def act_ffn(e, f):
            def one(it, jj):
                e.wait_ge(gu_ready, f * FB + it * 4 + (jj + 1))
                e.wait_ge(hid_done, f * FB + it * 4 + (jj + 3))
                act_(act2[:, jj % 2, :], bank(4 + jj, 0, S), ACT.Silu).then_inc(silu_ready, 1)
            with e.Fori(0, CHUNKS // 2) as it:
                for jj in range(4):
                    one(it, jj)
            for jj in range(2):
                one(CHUNKS // 2, jj)

        def act_mix1(e, tr, so):
            for i in range(N_PROJ + 1):
                if i < N_PROJ:
                    name = MIX1_TILES[i][0]
                    b = i % 4
                    e.wait_ge(tr[0].sem, tr[0].at("p." + name))
                    if name.startswith("V"):
                        dst = vb if name == "VB" else vc[:, :, (name == "VC1") * 256:(name == "VC1") * 256 + 256]
                        act_(dst, pair(b), ACT.Copy).then_inc(tr[1].sem, tr[1].did("cp." + name))
                    else:
                        c = chain.index(name)
                        n = S if name in ("KI", "KA") else 512
                        if HEAD_AT[name][1] is None:
                            if c >= 2:
                                e.wait_ge(tr[2].sem, tr[2].at("h." + chain[c - 2]))
                            act_(ybuf[:, c % 2, 0:n], bank(b, 0, n), ACT.Copy).then_inc(
                                tr[1].sem, tr[1].did("cp." + name))
                        else:
                            act_(sqp(c % 2)[:, 0:n], bank(b, 0, n), ACT.Square).then_inc(
                                tr[1].sem, tr[1].did("sq." + name))
                        if name == "KI":
                            act_(wi, bank(b, S, S + QT * 8).rearrange("p (q n) -> p q n", q=QT), ACT.Copy,
                                 scale=float((8 * 64) ** -0.5)).then_inc(tr[1].sem, tr[1].did("cp2.KI"))
                        if name == "KA":
                            act_(va, bank(b, S, S + QT * HD).rearrange("p (q n) -> p q n", q=QT),
                                 ACT.Copy).then_inc(tr[1].sem, tr[1].did("cp2.KA"))
                if i >= 1:
                    name = MIX1_TILES[i - 1][0]
                    if name in HEAD_AT and HEAD_AT[name][1] is not None:
                        c = chain.index(name)
                        n = S if name == "KA" else 512
                        e.wait_ge(tr[0].sem, tr[0].at("ss." + name))
                        if HEAD_AT[chain[c - 2]][1] is not None:
                            e.wait_ge(tr[2].sem, tr[2].at("y." + chain[c - 2]))
                        act_rstd(e, tr, name, bank(4, 0, n), 1.0 / HD, 0, n, c % 2)
                if 5 <= i <= 10:
                    j = i - 5
                    e.wait_ge(tr[0].sem, tr[0].at(f"index{j}"))
                    if j >= 2:
                        e.wait_ge(tr[2].sem, tr[2].at(f"acc{j - 2}"))
                    act_(rl[:, j % 2, :], bank(6 + j % 2), ACT.Relu).then_inc(tr[1].sem, tr[1].did(f"relu{j}"))
            g = [0]

            def gate():
                k = g[0]
                g[0] += 1
                e.wait_ge(so[0].sem, so[0].at(f"gate{k}"))
                act_(hidb(2 * k, 2), bank(k % 2), ACT.Tanh, scale=0.5).then_inc(so[1].sem, so[1].did(f"gate{k}"))
            for j in range(len(UNITS) + 2):
                if j < len(UNITS):
                    nk = P * (UNITS[j][1] + 1)
                    e.wait_ge(so[2].sem, so[2].at(f"nm{j}"))
                    for m in range(4):
                        z = smb[:, j % 2, m * nk:(m + 1) * nk]
                        ins = act_(z, z, ACT.Exp, bias=nmax[:, j % 2, m:m + 1], accum_out=rsum[:, j % 2, m:m + 1])
                    ins.then_inc(so[1].sem, so[1].did(f"e{j}"))
                gate()
                if 1 <= j <= len(UNITS):
                    u = j - 1
                    gr, q = UNITS[u]
                    e.wait_ge(so[0].sem, so[0].at(f"t{u}"))
                    n = (2 if gr[0] == "C" else 4) * (q + 1) * P
                    src = PS[:, 6:8, :].rearrange("p b n -> p (b n)")
                    act_(ptb[:, u % 2, 0:n], src[:, 0:n], ACT.Copy).then_inc(so[1].sem, so[1].did(f"pt{u}"))
                if j >= 2:
                    u = j - 2
                    gr, q = UNITS[u]
                    e.wait_ge(so[0].sem, so[0].at(f"o{u}"))
                    b0 = {"A": 0, "B": 2, "C0": 4, "C1": 6}[gr]
                    act_(oT[:, b0:b0 + 2, q * P:(q + 1) * P], pair(2 + (u // 2) % 2)[:, :, q * P:(q + 1) * P],
                         ACT.Copy).then_inc(so[1].sem, so[1].did(f"o{u}"))
                    if gr[0] == "C" and q == 1:
                        i = int(gr[1])
                        e.wait_ge(so[1].sem, so[1].at(f"o{u}"))
                        act_(sqp(i), blk2(oT, 2 + i), ACT.Square).then_inc(so[1].sem, so[1].did(f"sqc{i}"))
                if j >= len(UNITS):
                    gate()
            for i in range(2):
                e.wait_ge(so[0].sem, so[0].at(f"ssc{i}"))
                act_rstd(e, so, f"c{i}", bank(i), 1.0 / P, 0, 512, i)

        def act_l2(e):
            def square(j):
                if j >= 4:
                    e.wait_ge(m2[0].sem, m2[0].at(f"l2s{j - 4}"))
                e.wait_ge(m2[1].sem, m2[1].at(f"silu{j}"))
                act_(sqp(j % 4), blk2(heads, j), ACT.Square).then_inc(m2[1].sem, m2[1].did(f"l2sq{j}"))
            for j in range(4):
                square(j)
            for j in range(8):
                e.wait_ge(m2[0].sem, m2[0].at(f"l2s{j}"))
                if j >= 2:
                    e.wait_ge(m2[2].sem, m2[2].at(f"l2n{j - 2}"))
                act_rstd(e, m2, f"l2.{j}", bank(4 + j % 4), 1.0, 0, 512, j % 2)
                if j + 4 < 8:
                    square(j + 4)

        def act_mix2(e):
            def silu(j):
                e.wait_ge(m2[2].sem, m2[2].at(f"q.{j}.3.1"))
                act_(blk2(heads, j), blk2(heads, j), ACT.Silu).then_inc(m2[1].sem, m2[1].did(f"silu{j}"))
            for i, name in enumerate(mix2):
                if name == "A0":
                    continue
                e.wait_ge(m2[0].sem, m2[0].at("p." + name))
                num = int("".join(ch for ch in name if ch.isdigit()))
                if name == "BETA0":
                    act_(ab[0:8, 1, :], PS[0:8, i % 4, 0:S], ACT.Tanh, scale=0.5).then_inc(m2[1].sem, m2[1].did("cp.BETA0"))
                elif name.startswith("GLU_A"):
                    pass
                elif name.startswith("GLU_G"):
                    if num >= 2:
                        e.wait_ge(m2[2].sem, m2[2].at(f"glu.{num - 2}.1"))
                    for b in range(2):
                        act_(gth[:, num % 2, b * S:(b + 1) * S], bank(i % 4, b * S, (b + 1) * S), ACT.Tanh, scale=0.5,
                             bias=g2[:, 2 * num + b, B_G:B_G + 1]).then_inc(m2[1].sem, m2[1].did(f"gth.{num}.{b}"))
                elif name.startswith("QKV"):
                    if num >= 2:
                        e.wait_ge(m2[2].sem, m2[2].at(f"q.{num - 2}.3.1"))
                    act_(qpad[:, num % 2, :, CTAPS - 1:], pair(i % 4), ACT.Copy).then_inc(m2[1].sem, m2[1].did("cp." + name))
                    if num >= 1:
                        silu(num - 1)
                elif name.startswith("Z"):
                    act_(hidb(16 + 2 * num, 2), bank(i % 4), ACT.Silu).then_inc(m2[1].sem, m2[1].did("cp." + name))
                    if num == 0:
                        silu(11)
                        act_l2(e)
                else:
                    act_(hidb(2 * num, 2), bank(i % 4), ACT.Tanh, scale=0.5).then_inc(m2[1].sem, m2[1].did("cp." + name))
                if name == "GLU_G0":
                    e.wait_ge(m2[2].sem, m2[2].at("absa"))
                    act_(lg[0:8, 1, :], lg[0:8, 0, :], ACT.Exp, scale=-1.0).then_inc(m2[1].sem, m2[1].did("sp.e"))
                    e.wait_ge(m2[1].sem, m2[1].at("sp.e"))
                    act_(lg[0:8, 1, :], lg[0:8, 1, :], ACT.Ln, bias=1.0).then_inc(m2[1].sem, m2[1].did("sp.ln"))
                if name == "GLU_G3":
                    e.wait_ge(m2[0].sem, m2[0].at("tok"))
                    act_(gtok, bank(4, 0, 16).rearrange("p (t h) -> p t h", t=QT), ACT.Copy).then_inc(m2[1].sem, m2[1].did("gtok"))
                    act_(ngtok, bank(4, 0, 16).rearrange("p (t h) -> p t h", t=QT), ACT.Copy, scale=-1.0).then_inc(m2[1].sem, m2[1].did("ngtok"))
                    act_(bgtok, bank(4, 0, 16).rearrange("p (t h) -> p t h", t=QT), ACT.Exp).then_inc(m2[1].sem, m2[1].did("egtok"))
                    act_(btok, bank(4, 16, 32).rearrange("p (t h) -> p t h", t=QT), ACT.Copy).then_inc(m2[1].sem, m2[1].did("btok"))
            e.wait_ge(cv[0].sem, cv[0].at("mean.sum"))
            act_(lnb[:, 0, 0:S], bank(4, 0, S), ACT.Copy, scale=1.0 / D).then_inc(cv[1].sem, cv[1].did("mean"))
            for k in range(4):
                e.wait_ge(cv[2].sem, cv[2].at(f"cent{k}"))
                act_(sqp(k), blk2(conv, k), ACT.Square).then_inc(cv[1].sem, cv[1].did(f"ln.sq{k}"))
            e.wait_ge(cv[0].sem, cv[0].at("ln.sum"))
            act_rstd(e, cv, "ln", bank(7, 0, S), 1.0 / D, 1, S)
            for k in range(KB):
                e.wait_ge(cv[2].sem, cv[2].at(f"lnx{k}"))
                act_(conv[:, k, :], conv[:, k, :], ACT.Silu, bias=g2[:, k, LN_B:LN_B + 1]).then_inc(cv[1].sem, cv[1].did(f"cvs{k}"))
            act_delta(e)
            for i in range(4):
                e.wait_ge(dl[1].sem, dl[1].at(f"{i // 2}.oc.1"))
                act_(sqp(i), blk2(oT, i), ACT.Square).then_inc(dl[1].sem, dl[1].did(f"osq{i}"))
            for i in range(4):
                e.wait_ge(dl[0].sem, dl[0].at(f"os{i}"))
                if i >= 2:
                    e.wait_ge(dl[2].sem, dl[2].at(f"on{i - 2}"))
                act_rstd(e, dl, f"o{i}", bank(i), 1.0 / P, 0, 512, i % 2)
            for k in range(KB):
                e.wait_ge(m2[0].sem, m2[0].at(f"yb.{k // 2}"))
                act_(sq[:, k, :], acc(k, 4), ACT.Identity, bias=g2[:, k, B_O:B_O + 1]).then_inc(m2[1].sem, m2[1].did(f"yo{k}"))

        def act_delta(e):
            wp = lambda n: e.wait_ge(dl[0].sem, dl[0].at(n))
            wv = lambda n: e.wait_ge(dl[2].sem, dl[2].at(n))

            def four(b):
                return bank(b).rearrange("p (h n) -> p h n", h=4)

            def copy(dst, b, n):
                act_(dst, four(b), ACT.Copy).then_inc(dl[1].sem, dl[1].did(n))
            for g in range(2):
                for c in range(QT):
                    wv(f"{g}.gbm.{c}")
                    for h in range(4):
                        z = DU["gbm", c][:, h, :]
                        ins = act_(z, z, ACT.Exp, bias=ngtok[:, c, 4 * g + h:4 * g + h + 1])
                    ins.then_inc(dl[1].sem, dl[1].did(f"{g}.dt.{c}"))
                    if c == 0:
                        wv(f"{g}.cd0")
                        act_(cdec, cdec, ACT.Exp).then_inc(dl[1].sem, dl[1].did(f"{g}.cdec"))
                    else:
                        act_(qd, four(4), ACT.Exp).then_inc(dl[1].sem, dl[1].did(f"{g}.eg"))
                for c in range(QT):
                    wp(f"{g}.tt.{c}")
                    copy(DU["T", c], 4 * c, f"{g}.T0.{c}")
                for l in range(1, 7):
                    for c in range(QT):
                        wp(f"{g}.m{l}.{c}")
                        copy(DU["m1", c], 4 * c + 3, f"{g}.mc{l}.{c}")
                for c in range(QT):
                    wp(f"{g}.u.{c}")
                    copy(DU["u", c], 4 * c + 2, f"{g}.uc.{c}")
                wp(f"{g}.w")
                copy(wT, 5, f"{g}.wc")
                wp(f"{g}.s")
                copy(st, 1, f"{g}.sc")
                for c in range(QT):
                    wp(f"{g}.o.{c}")
                    copy(oT[:, 4 * g:4 * g + 4, c * P:(c + 1) * P], 4 * c + 3, f"{g}.oc.{c}")

        @block.scalar
        def _(e):
            e.wait_ge(params_in, N_PARAM)
            for b in range(2):
                e.wait_ge(pro_pe.sem, pro_pe.at(f"cols{b}"))
                act_(cols[:, 4 * b:4 * b + 4, :], bank(4 + b, 0, 4 * ROWS).rearrange("p (k r) -> p k r", k=4),
                     ACT.Copy).then_inc(pro_act.sem, pro_act.did(f"cols{b}"))
            e.wait_ge(pro_pe.sem, pro_pe.at("small"))
            act_(small[:], bank(6, 0, SMALL), ACT.Copy).then_inc(pro_act.sem, pro_act.did("small"))
            e.wait_ge(pro_dve.sem, pro_dve.at("lsum"))
            act_(lexp, lsum, ACT.Exp).then_inc(pro_act.sem, pro_act.did("lexp"))
            act_(gd[0:8, 0, 4:4 + LAYERS], gd[0:8, 0, 0:LAYERS], ACT.Exp).then_inc(pro_act.sem, pro_act.did("decay"))
            e.wait_ge(pro_dve.sem, pro_dve.at("angles"))
            act_(sinT[:], red, ACT.Sin).then_inc(pro_act.sem, pro_act.did("sin"))
            act_(cosT[:], red2, ACT.Sin).then_inc(pro_act.sem, pro_act.did("cos"))
            with e.Fori(0, LAYERS) as lay:
                env.lay = lay
                tr = first["norm"]
                act_norm(e, tr, "f0", lay * 12)
                act_ffn(e, lay * 2)
                act_norm(e, tr, "mix", lay * 12 + 4)
                act_mix1(e, first["mix"], first["soft"])
                act_norm(e, tr, "f1", lay * 12 + 8)
                act_ffn(e, lay * 2 + 1)
            if BLOCKS > 1:
                with e.Fori(0, LAYERS) as lay:
                    env.lay = lay
                    tr = second["norm"]
                    upd = lay * 12 + 12 * LAYERS
                    for half in range(2):
                        if half == 1:
                            act_norm(e, tr, "mix", upd + 4)
                            act_mix2(e)
                            act_post(e, tr, "pmix", lambda k: e.wait_ge(second["mix"][0].sem, second["mix"][0].at(f"out.{k}")), 0.5)
                        act_norm(e, tr, f"f{half}", upd + 8 * half)
                        f = lay * 2 + (4 + half)
                        act_ffn(e, f)
                        act_post(e, tr, f"pf{half}", lambda k: e.wait_ge(down_ready, f * 4 + (k + 1)))
            env.lay = 0
            for b in range(4):
                e.wait_ge(pro_pe.sem, pro_pe.at(f"fin{b}"))
                act_(blk2(xn, b), bank(4 + b), ACT.Copy).then_inc(out_ready, 1)

        def step(e, tr, ins, name):
            ins.then_inc(tr[2].sem, tr[2].did(name))
            e.wait_ge(tr[2].sem, tr[2].at(name))

        def dve_scale(e, tr, tag, gain):
            e.wait_ge(tr[1].sem, tr[1].at(tag + ".rstd"))
            for k in range(KB):
                v_.scalar_tensor_tensor(xn[:, k, :], x[:, k, :], gain(k), rstd[:, 0, 0:S], ALU.mult,
                                        ALU.mult).then_inc(tr[2].sem, tr[2].did(f"{tag}.xn{k}"))

        def dve_post(e, tr, tag, gain):
            e.wait_ge(tr[1].sem, tr[1].at(tag + ".rstd"))
            for k in range(KB):
                v_.scalar_tensor_tensor(sq[:, k, :], acc(k), gain(k), rstd[:, 0, 0:S], ALU.mult,
                                        ALU.mult).then_inc(tr[2].sem, tr[2].did(f"{tag}.s{k}"))
            for k in range(4):
                e.wait_ge(tr[2].sem, tr[2].at(f"{tag}.s{2 * k + 1}"))
                v_.tensor_tensor(blk2(x, k), blk2(x, k), sqp(k), ALU.add).then_inc(x_upd, 1)

        def dve_ffn(e, f):
            def one(it, jj, dst):
                e.wait_ge(silu_ready, f * FB + it * 4 + (jj + 1))
                v_.tensor_tensor(dst, act2[:, jj % 2, :], bank(4 + jj, S, 2 * S), ALU.mult).then_inc(hid_done, 1)
            with e.Fori(0, CHUNKS // 2) as it:
                for jj in range(4):
                    one(it, jj, hid[:, bass.ds(it * (4 * S) + jj * S, S)])
            for jj in range(2):
                one(CHUNKS // 2, jj, hidb(FB - 2 + jj))

        def dve_residual(e, ready):
            for b in range(4):
                ready(b)
                v_.scalar_tensor_tensor(blk2(x, b), bank(b), 0.5, blk2(x, b), ALU.mult, ALU.add).then_inc(x_upd, 1)

        def dve_index(e, tr, j):
            q, hs = INDEX_HEADS[j]
            nk = P * (q + 1)
            e.wait_ge(tr[1].sem, tr[1].at(f"relu{j}"))
            for i, h in enumerate(hs):
                src = rl[:, j % 2, i * nk:(i + 1) * nk]
                name = f"acc{j}" if h == hs[-1] else f"acc{j}.{h}"
                if h == 0:
                    ins = v_.tensor_scalar(isc[q], src, wi[:, q, 0:1], None, ALU.mult)
                else:
                    ins = v_.scalar_tensor_tensor(isc[q], src, wi[:, q, h:h + 1], isc[q], ALU.mult, ALU.add)
                step(e, tr, ins, name)
            if j in (1, 5):
                v_.tensor_tensor(isc[q], isc[q], cmask[:, S - nk:S], ALU.add).then_inc(tr[2].sem, tr[2].did(f"isc{q}"))
                hold(e, "vector", tr[2].sem, tr[2].at(f"isc{q}"))

        def dve_topk(e, tr, q, r):
            src = isc[q] if r == 0 else work[q]
            if r % 2 == 0:
                e.sem_inc(passed["vector"], 1)
            v_.max(top8, src).then_inc(tr[2].sem, tr[2].did(f"top{q}.{r}"))
            hold(e, "vector", tr[2].sem, tr[2].at(f"top{q}.{r}"))
            v_.match_replace(work[q], top8, src, TAKEN).then_inc(tr[2].sem, tr[2].did(f"take{q}.{r}"))
            hold(e, "vector", tr[2].sem, tr[2].at(f"take{q}.{r}"))
            if r == TOPK // 8 - 1:
                nk = P * (q + 1)
                step(e, tr, v_.tensor_tensor(ibias[q], work[q], isc[q], ALU.not_equal), f"kept{q}")
                step(e, tr, v_.tensor_scalar(ibias[q], ibias[q], 1.0, -NEG, ALU.subtract, ALU.mult), f"bias{q}")
                step(e, tr, v_.tensor_tensor(ibias[q], ibias[q], cmask[:, S - nk:S], ALU.add), f"ibias{q}")

        def dve_mix1(e, tr, so, lay):
            for i in range(N_PROJ + 3):
                if 1 <= i <= N_PROJ:
                    name = MIX1_TILES[i - 1][0]
                    if name in HEAD_AT and HEAD_AT[name][1] is not None:
                        c = chain.index(name)
                        n = S if name == "KA" else 512
                        e.wait_ge(tr[1].sem, tr[1].at(name + ".rstd"))
                        r = HEAD_AT[name][1]
                        v_.scalar_tensor_tensor(ybuf[:, c % 2, 0:n], bank((i - 1) % 4, 0, n), h1[:, r:r + 1],
                                                rstd[:, c % 2, 0:n], ALU.mult,
                                                ALU.mult).then_inc(tr[2].sem, tr[2].did("y." + name))
                if 2 <= i <= N_PROJ + 1:
                    name = MIX1_TILES[i - 2][0]
                    if name in HEAD_AT:
                        c = chain.index(name)
                        nb = 1 if name in ("KI", "KA") else 2
                        n = nb * S
                        shape = lambda ap: ap.rearrange("p (b s) -> p b s", b=nb)
                        e.wait_ge(tr[0].sem, tr[0].at("rot." + name))
                        step(e, tr, v_.tensor_tensor(shape(tbuf[:, c % 2, 0:n]), shape(bank(5, 0, n)), bc(sinT[:], nb),
                                                     ALU.mult), "t." + name)
                        e.wait_ge(tr[3].sem, tr[3].at("u." + name))
                        at = HEAD_AT[name][0]
                        v_.tensor_tensor(heads[:, at:at + nb, :].rearrange("p b s -> p (b s)"), tbuf[:, c % 2, 0:n],
                                         ubuf[:, c % 2, 0:n], ALU.add).then_inc(tr[2].sem, tr[2].did("h." + name))
                if 6 <= i <= 11:
                    dve_index(e, tr, i - 6)
                if 8 <= i <= 11:
                    for r in (2 * (i - 8), 2 * (i - 8) + 1):
                        dve_topk(e, tr, 0, r)
                if 12 <= i <= 15:
                    for r in (2 * (i - 12), 2 * (i - 12) + 1):
                        dve_topk(e, tr, 1, r)
            for j, (gr, q) in enumerate(UNITS):
                nk = P * (q + 1)
                e.wait_ge(so[0].sem, so[0].at(f"s{j}"))
                if j >= 2:
                    e.wait_ge(so[0].sem, so[0].at(f"t{j - 2}"))
                z = smb[:, j % 2, 0:4 * nk].rearrange("p (m n) -> p m n", m=4)
                mask = ibias[q] if gr == "A" else cmask[:, S - nk:S]
                for c in range(2):
                    src = bank(4 + c, 0, 2 * nk).rearrange("p (i n) -> p i n", i=2)
                    ins = v_.scalar_tensor_tensor(z[:, 2 * c:2 * c + 2, :], src, HD ** -0.5, bc(mask, 2), ALU.mult, ALU.add)
                    if c == 0:
                        ins.then_inc(so[2].sem, so[2].did(f"sm{j}.0"))
                step(e, so, ins, f"sm{j}")
                v_.tensor_reduce(nmax[:, j % 2, :], z, AX.X, ALU.max, negate=True).then_inc(so[2].sem, so[2].did(f"nm{j}"))
                e.wait_ge(so[1].sem, so[1].at(f"e{j}"))
                ri = rinv[:, j % 2, :]
                step(e, so, v_.reciprocal(ri, rsum[:, j % 2, :]), f"ri{j}")
                if gr[0] == "C":
                    second_maps = ri[:, 2:4]
                    step(e, so, v_.tensor_scalar(second_maps, second_maps, lam[:, bass.ds(lay, 1)], None, ALU.mult), f"rl{j}")
                    step(e, so, v_.tensor_tensor(z, z, bcl(ri, nk), ALU.mult), f"pp{j}")
                    ins = v_.tensor_tensor(z[:, 0:2, :], z[:, 0:2, :], z[:, 2:4, :], ALU.subtract)
                else:
                    ins = v_.tensor_tensor(z, z, bcl(ri, nk), ALU.mult)
                ins.then_inc(so[2].sem, so[2].did(f"p{j}"))
            e.wait_ge(so[1].sem, so[1].at("gate11"))
            for b in range(4):
                e.wait_ge(tr[0].sem, tr[0].at(f"ya.{b}"))
                v_.scalar_tensor_tensor(blk2(xn, b), hidb(2 * b, 2), 1.0, bank(b), ALU.add, ALU.mult).then_inc(
                    tr[2].sem, tr[2].did(f"ma{b}"))
            for i in range(2):
                e.wait_ge(so[1].sem, so[1].at(f"c{i}.rstd"))
                o = blk2(oT, 2 + i)
                v_.scalar_tensor_tensor(o, o, h1[:, 6:7], rstd[:, i, :], ALU.mult, ALU.mult).then_inc(
                    so[2].sem, so[2].did(f"nc{i}"))
            for n, h0, b0 in (("b", 8, 4), ("c", 16, 0)):
                for b in range(4):
                    tmp = smb[:, b // 2, (b % 2) * 512:(b % 2 + 1) * 512]
                    e.wait_ge(tr[0].sem, tr[0].at(f"y{n}.{b}"))
                    step(e, tr, v_.scalar_tensor_tensor(tmp, hidb(h0 + 2 * b, 2), 1.0, bank(b0 + b), ALU.add, ALU.mult),
                         f"g{n}{b}")
                    v_.tensor_tensor(blk2(xn, b), blk2(xn, b), tmp, ALU.add).then_inc(tr[2].sem, tr[2].did(f"m{n}{b}"))
            dve_residual(e, lambda b: e.wait_ge(tr[0].sem, tr[0].at(f"out.{b}")))

        def dve_setup(e):
            pr = (pro_pe, pro_act, pro_dve, pro_pool)
            e.sem_inc(hid_done, 4)
            step(e, pr, v_.memset(invrow[0:1, :], 0.0), "inv0")
            for i, f in enumerate(inv_freq):
                o = invrow[0:1, :].rearrange("p (h r j) -> p h r j", h=2, j=8)[:, :, 0:2, i]
                ins = v_.memset(o, f)
            ins.then_inc(pro_dve.sem, pro_dve.did("invrow"))
            v_.memset(consts[:, 0:1], EPS)
            v_.memset(consts[:, 1:2], LN_EPS).then_inc(pro_dve.sem, pro_dve.did("consts"))
            e.wait_ge(params_in, N_PARAM)
            for b in range(4):
                e.wait_ge(pro_pe.sem, pro_pe.at(f"x{b}"))
                v_.tensor_copy(blk2(x, b), bank(b)).then_inc(x_upd, 1)
            l4 = lamb.rearrange("p (l a b d) -> p l a b d", l=LAYERS, a=2, b=2)
            lp = lprod.rearrange("p (l a d) -> p l a d", l=LAYERS, a=2)
            step(e, pr, v_.tensor_tensor(lp, l4[:, :, :, 0, :], l4[:, :, :, 1, :], ALU.mult), "lprod")
            v_.tensor_reduce(lsum.rearrange("p (l a) -> p l a", l=LAYERS), lp, AX.X, ALU.add).then_inc(
                pro_dve.sem, pro_dve.did("lsum"))
            v_.tensor_copy(posf, pos_i).then_inc(pro_dve.sem, pro_dve.did("posf"))
            e.wait_ge(pro_pe.sem, pro_pe.at("small"))
            step(e, pr, v_.tensor_copy(invf, bank(7, 0, 1)), "invf")
            step(e, pr, v_.tensor_scalar(ang, posf, invf, None, ALU.mult), "ang")
            magic = 1.5 * 2.0 ** 23
            step(e, pr, v_.tensor_scalar(red, ang, 1.0 / TWO_PI, magic, ALU.mult, ALU.add), "turns0")
            step(e, pr, v_.tensor_scalar(red, red, magic, None, ALU.subtract), "turns")
            c1 = 6.28125
            c2 = float(np.float32(np.round((TWO_PI - c1) * 2 ** 21) / 2 ** 21))
            c3 = TWO_PI - c1 - c2
            for i, c in enumerate((c1, c2, c3)):
                step(e, pr, v_.scalar_tensor_tensor(ang, red, -c, ang, ALU.mult, ALU.add), f"red{i}")
            lim = 3.1415925
            step(e, pr, v_.tensor_scalar(red, ang, lim, -lim, ALU.min, ALU.max), "redsin")
            step(e, pr, v_.scalar_tensor_tensor(ang, red, -1.0, red, ALU.mult, ALU.max), "absang")
            step(e, pr, v_.tensor_scalar(red2, ang, -1.0, math.pi / 2, ALU.mult, ALU.add), "angles")
            e.wait_ge(pro_act.sem, pro_act.at("lexp"))
            l2 = lexp.rearrange("p (l a) -> p l a", l=LAYERS)
            for l in range(LAYERS):
                step(e, pr, v_.tensor_tensor(lam[:, l:l + 1], l2[:, l, 0:1], l2[:, l, 1:2], ALU.subtract), f"lam{l}")
                step(e, pr, v_.tensor_scalar(lam[:, l:l + 1], lam[:, l:l + 1], lam_init[l], None, ALU.add), f"lami{l}")
                e.wait_ge(pro_act.sem, pro_act.at("small"))
                c = small[:, 7 * l + 6:7 * l + 7]
                step(e, pr, v_.tensor_scalar(c, c, 1.0 - lam_init[l], None, ALU.mult), f"subln{l}")
            e.wait_ge(pro_act.sem, pro_act.at("decay"))
            step(e, pr, v_.tensor_scalar(gd[0:8, 0, 0:LAYERS], gd[0:8, 0, 4:4 + LAYERS], -1.0, None, ALU.mult), "ndecay")
            e.wait_ge(pro_act.sem, pro_act.at("cos"))
            e.wait_ge(pro_pool.sem, pro_pool.at("masks"))

        def dve_conv(e, n0, n1):
            for n in range(n0, min(n1, 2 * TAPS * 4)):
                hf, tap, b4 = n // (4 * TAPS), n // 4 % TAPS, n % 4
                b = 4 * hf + b4
                src = glu[:, b, tap:tap + S]
                w = g2[:, b, W_DW + tap:W_DW + tap + 1]
                if tap == 0:
                    e.wait_ge(m2[2].sem, m2[2].at(f"glu.{b // 2}.{b % 2}"))
                    ins = v_.tensor_scalar(conv[:, b, :], src, w, g2[:, b, W_B:W_B + 1], ALU.mult, ALU.add)
                else:
                    e.wait_ge(cv[2].sem, cv[2].at(f"cv.{hf}.{tap - 1}.{b4}"))
                    ins = v_.scalar_tensor_tensor(conv[:, b, :], src, w, conv[:, b, :], ALU.mult, ALU.add)
                ins.then_inc(cv[2].sem, cv[2].did(f"cv.{hf}.{tap}.{b4}"))

        def dve_mix2(e, lay):
            did = lambda ins, n: ins.then_inc(m2[2].sem, m2[2].did(n))
            did(v_.memset(glu[:, :, 0:TAPS - 1], 0.0), "pad0")
            did(v_.memset(qpad[:, :, :, 0:CTAPS - 1], 0.0), "pad1")
            e.wait_ge(m2[0].sem, m2[0].at("p.A0"))
            step(e, m2, v_.tensor_scalar(ab[0:8, 0, :], PS[0:8, 1, 0:S], gd[0:8, 1, bass.ds(lay, 1)], None, ALU.add), "cp.A0")
            did(v_.scalar_tensor_tensor(lg[0:8, 0, :], ab[0:8, 0, :], -1.0, ab[0:8, 0, :], ALU.mult, ALU.max), "absa")
            e.wait_ge(m2[1].sem, m2[1].at("cp.BETA0"))
            did(v_.tensor_scalar(ab[0:8, 1, :], ab[0:8, 1, :], 1.0, 0.5, ALU.add, ALU.mult), "beta")
            steps = 0
            for i, name in enumerate(mix2):
                num = int("".join(ch for ch in name if ch.isdigit()))
                if name.startswith("GLU_G"):
                    e.wait_ge(m2[1].sem, m2[1].at(f"gth.{num}.1"))
                    z = gth[:, num % 2, :]
                    step(e, m2, v_.tensor_scalar(z, z, 1.0, 0.5, ALU.add, ALU.mult), f"sg{num}")
                    for b in range(2):
                        did(v_.scalar_tensor_tensor(glu[:, 2 * num + b, TAPS - 1:], bank((i - 1) % 4, b * S, (b + 1) * S),
                                                    g2[:, 2 * num + b, B_A:B_A + 1], z[:, b * S:(b + 1) * S], ALU.add,
                                                    ALU.mult), f"glu.{num}.{b}")
                if name == "GLU_G0":
                    e.wait_ge(m2[1].sem, m2[1].at("sp.ln"))
                    step(e, m2, v_.scalar_tensor_tensor(lg[0:8, 2, :], ab[0:8, 0, :], 0.0, lg[0:8, 1, :], ALU.max, ALU.add), "softplus")
                    step(e, m2, v_.tensor_scalar(lg[0:8, 2, :], lg[0:8, 2, :], gd[0:8, 0, bass.ds(lay, 1)], None, ALU.mult), "decay")
                    for c in range(QT):
                        did(v_.tensor_tensor_scan(lg[0:8, 3, c * P:(c + 1) * P], ones[0:8, :], lg[0:8, 2, c * P:(c + 1) * P],
                                                  0.0, ALU.mult, ALU.add), f"gsum{c}")
                if name.startswith("QKV"):
                    e.wait_ge(m2[1].sem, m2[1].at("cp." + name))
                    for tap in range(CTAPS):
                        for b in range(2):
                            src = qpad[:, num % 2, b, tap:tap + S]
                            r = W_CV + 3 * tap + num // 4
                            w = g2[:, 2 * (num % 4) + b, r:r + 1]
                            o = heads[:, 2 * num + b, :]
                            if tap == 0:
                                ins = v_.tensor_scalar(o, src, w, None, ALU.mult)
                            else:
                                e.wait_ge(m2[2].sem, m2[2].at(f"q.{num}.{tap - 1}.{b}"))
                                ins = v_.scalar_tensor_tensor(o, src, w, o, ALU.mult, ALU.add)
                            did(ins, f"q.{num}.{tap}.{b}")
                if name == "Z0":
                    for j in range(8):
                        e.wait_ge(m2[1].sem, m2[1].at(f"l2.{j}.rstd"))
                        z = blk2(heads, j)
                        did(v_.scalar_tensor_tensor(z, z, P ** -0.5 if j < 4 else 1.0, rstd[:, j % 2, :], ALU.mult,
                                                    ALU.mult), f"l2n{j}")
                if i >= mix2.index("QKV0"):
                    dve_conv(e, steps, steps + 11)
                    steps += 11
            dve_conv(e, steps, 10 ** 6)
            e.wait_ge(m2[1].sem, m2[1].at("btok"))
            step(e, m2, v_.tensor_tensor(bgtok, bgtok, btok, ALU.mult), "bgtok")
            e.wait_ge(cv[1].sem, cv[1].at("mean"))
            for k in range(4):
                z = conv[:, 2 * k:2 * k + 2, :]
                v_.tensor_tensor(z, z, bc(lnb[:, 0, 0:S], 2), ALU.subtract).then_inc(cv[2].sem, cv[2].did(f"cent{k}"))
            e.wait_ge(cv[1].sem, cv[1].at("ln.rstd"))
            for k in range(KB):
                v_.scalar_tensor_tensor(conv[:, k, :], conv[:, k, :], g2[:, k, LN_G:LN_G + 1], rstd[:, 0, 0:S],
                                        ALU.mult, ALU.mult).then_inc(cv[2].sem, cv[2].did(f"lnx{k}"))
            dve_delta(e)
            for i in range(4):
                e.wait_ge(dl[1].sem, dl[1].at(f"o{i}.rstd"))
                z = blk2(oT, i)
                step(e, dl, v_.scalar_tensor_tensor(z, z, h2[:, 0:1], rstd[:, i % 2, :], ALU.mult, ALU.mult), f"on{i}")
                v_.tensor_tensor(z, z, hidb(16 + 2 * i, 2), ALU.mult).then_inc(dl[2].sem, dl[2].did(f"oz{i}"))
            for b in range(4):
                e.wait_ge(m2[0].sem, m2[0].at(f"ya.{b}"))
                did(v_.scalar_tensor_tensor(blk2(xn, b), hidb(2 * b, 2), 1.0, bank(b), ALU.add, ALU.mult), f"ma{b}")
            for b in range(4):
                e.wait_ge(m2[1].sem, m2[1].at(f"yo{2 * b + 1}"))
                step(e, m2, v_.scalar_tensor_tensor(sqp(b), hidb(8 + 2 * b, 2), 1.0, sqp(b), ALU.add, ALU.mult), f"gb{b}")
                did(v_.tensor_tensor(blk2(xn, b), blk2(xn, b), sqp(b), ALU.add), f"mb{b}")

        def dve_delta(e):
            did = lambda ins, n: ins.then_inc(dl[2].sem, dl[2].did(n))
            wp = lambda n: e.wait_ge(dl[0].sem, dl[0].at(n))
            wa = lambda n: e.wait_ge(dl[1].sem, dl[1].at(n))
            four = lambda b: bank(b).rearrange("p (h n) -> p h n", h=4)
            tt = v_.tensor_tensor
            for g in range(2):
                hs = slice(4 * g, 4 * g + 4)
                for c in range(QT):
                    wp(f"{g}.gb.{c}")
                    did(tt(DU["gbm", c], four(4 * c), bc(tmask, 4), ALU.add), f"{g}.gbm.{c}")
                    if c == 0:
                        did(tt(cdec, four(0)[:, :, P - 1], gtok[:, 0, hs], ALU.subtract), f"{g}.cd0")
                for c in range(QT):
                    wa(f"{g}.dt.{c}")
                    wp(f"{g}.kk.{c}")
                    did(tt(DU["at", c], four(4 * c + 2), DU["gbm", c], ALU.mult), f"{g}.at0.{c}")
                    wp(f"{g}.qk.{c}")
                    did(tt(DU["qkt", c], four(4 * c + 3), DU["gbm", c], ALU.mult), f"{g}.qkt.{c}")
                    e.wait_ge(dl[2].sem, dl[2].at(f"{g}.at0.{c}"))
                    did(tt(DU["at", c], DU["at", c], four(4 * c + 1), ALU.mult), f"{g}.at.{c}")
                for c in range(QT):
                    e.wait_ge(dl[3].sem, dl[3].at(f"{g}.al0.{c}"))
                    did(tt(DU["U", c], bc(ident, 4), DU["al", c], ALU.subtract), f"{g}.U0.{c}")
                wa(f"{g}.cdec")
                for c in range(QT):
                    wp(f"{g}.vt.{c}")
                    did(tt(DU["vx", c], four(4 * c + 3), bcl(btok[:, c, hs], P), ALU.mult), f"{g}.vx.{c}")
                    col = cdec if c == 0 else bgtok[:, 1, hs]
                    did(tt(DU["kx", c], four(4 * c + 2), bcl(col, P), ALU.mult), f"{g}.kx.{c}")
                wa(f"{g}.eg")
                did(tt(qd, qd, heads[:, hs, P:S], ALU.mult), f"{g}.qd")
                for l in range(1, 7):
                    for c in range(QT):
                        U, T = DU["U", c], DU["T", c]
                        wp(f"{g}.pt{l}.{c}" if l < 6 else f"{g}.pu{l}.{c}")
                        did(tt(U, U, four(4 * c), ALU.subtract), f"{g}.U{l}.{c}")
                        if l < 6:
                            did(tt(T, T, four(4 * c + 1), ALU.subtract), f"{g}.T{l}.{c}")
                wp(f"{g}.ws")
                wa(f"{g}.uc.1")
                did(tt(DU["u", 1], DU["u", 1], four(4), ALU.subtract), f"{g}.vn")

        @block.vector
        def _(e):
            dve_setup(e)
            with e.Fori(0, LAYERS) as lay:
                env.lay = lay
                tr = first["norm"]
                v_.tensor_copy(g1[:], cols[:, :, bass.ds(lay * 3, 3)])
                step(e, tr, v_.tensor_copy(h1[:, 0:7], small[:, bass.ds(lay * 7, 7)]), "gains")
                for half in range(2):
                    if half == 1:
                        dve_scale(e, tr, "mix", lambda k: g1[:, k, 1:2])
                        dve_mix1(e, first["mix"], first["soft"], lay)
                    dve_scale(e, tr, f"f{half}", lambda k: g1[:, k, 2 * half:2 * half + 1])
                    f = lay * 2 + half
                    dve_ffn(e, f)
                    dve_residual(e, lambda b: e.wait_ge(down_ready, f * 4 + (b + 1)))
            if BLOCKS > 1:
                with e.Fori(0, LAYERS) as lay:
                    env.lay = lay
                    tr = second["norm"]
                    v_.tensor_copy(g2[:], cols[:, :, bass.ds(lay * R2 + 3 * LAYERS, R2)])
                    step(e, tr, v_.tensor_copy(h2[:, 0:1], small[:, bass.ds(lay + 7 * LAYERS, 1)]), "gains")
                    for r in (G_P1, G_PM, G_P2, B_G):
                        step(e, tr, v_.tensor_scalar(g2[:, :, r], g2[:, :, r], 0.5, None, ALU.mult), f"half{r}")
                    for half in range(2):
                        if half == 1:
                            dve_scale(e, tr, "mix", lambda k: g2[:, k, G_MX:G_MX + 1])
                            dve_mix2(e, lay)
                            dve_post(e, tr, "pmix", lambda k: g2[:, k, G_PM:G_PM + 1])
                        gp, gq = ((G_F1, G_P1), (G_F2, G_P2))[half]
                        dve_scale(e, tr, f"f{half}", lambda k: g2[:, k, gp:gp + 1])
                        dve_ffn(e, lay * 2 + (4 + half))
                        dve_post(e, tr, f"pf{half}", lambda k: g2[:, k, gq:gq + 1])
            env.lay = 0

        def pool_mix2(e):
            for g in range(2):
                for l in range(7):
                    for c in range(QT):
                        if l == 0:
                            e.wait_ge(dl[2].sem, dl[2].at(f"{g}.at.{c}"))
                        elif l == 1:
                            e.wait_ge(dl[2].sem, dl[2].at(f"{g}.U0.{c}"))
                        else:
                            e.wait_ge(dl[0].sem, dl[0].at(f"{g}.m{l - 1}.{c}"))
                        nc.gpsimd.tensor_tensor(DU["al", c], DU["at", c], bc(levels[:, l, :], 4), ALU.mult).then_inc(
                            dl[3].sem, dl[3].did(f"{g}.al{l}.{c}"))

        @block.gpsimd
        def _(e):
            p_ = nc.gpsimd
            N_PARAMS = load_params(e)
            assert N_PARAMS == N_PARAM, N_PARAMS
            T = pro_pool
            n = [0]

            def ok(ins, name=None):
                name = name or f"s{n[0]}"
                n[0] += 1
                ins.then_inc(T.sem, T.did(name))
                e.wait_ge(T.sem, T.at(name))

            def fill(buf, pattern, base, mult, op, value, name=None):
                ok(p_.affine_select(out=buf, in_=buf, compare_op=op, fill=value, base=base, pattern=pattern,
                                    channel_multiplier=mult), name)
            ok(p_.memset(ident[:], 0.0))
            fill(ident[:], [[-1, P]], 0, 1, ALU.not_equal, 1.0, "ident")
            ok(p_.memset(ones[:], 1.0), "ones")
            ok(p_.memset(ones64[:], 0.0))
            for h in range(2):
                c = ones64[:, h * HD:(h + 1) * HD]
                ok(p_.memset(c, 1.0))
                if h == 0:
                    fill(c, [[0, HD]], HD - 1, -1, ALU.is_ge, 0.0)
                else:
                    fill(c, [[0, HD]], -HD, 1, ALU.is_ge, 0.0)
            ok(p_.memset(rot[:], 0.0))
            for h in range(2):
                fill(rot[:, h * HD:h * HD + 8], [[-1, 8]], -(h * HD + 8), 1, ALU.not_equal, -1.0)
                fill(rot[:, h * HD + 8:h * HD + 16], [[-1, 8]], -(h * HD), 1, ALU.not_equal, 1.0)
            ok(p_.memset(cmask[:], 0.0))
            fill(cmask[:, P:S], [[-1, P]], 0, 1, ALU.is_ge, NEG)
            ok(p_.memset(tmask[:], 0.0))
            fill(tmask[:], [[1, P]], 0, -1, ALU.is_ge, NEG)
            ok(p_.memset(sel[0:8, :, :], 0.0))
            fill(sel[0:8, :, :], [[-1, 8], [0, P]], 0, 1, ALU.not_equal, 1.0)
            ok(p_.memset(levels[:], 0.0))
            for l in range(7):
                w = 1 << l
                v = levels[:, l, :].rearrange("p (i y) -> p i y", y=2 * w)[:, :, w:2 * w]
                ok(p_.memset(v, 1.0))
                fill(v, [[-2 * w, P // (2 * w)], [0, w]], 0, 1, ALU.is_ge, 0.0)
                fill(v, [[2 * w, P // (2 * w)], [0, w]], w - 1, -1, ALU.is_ge, 0.0, "masks" if l == 6 else None)
            e.wait_ge(pro_act.sem, pro_act.at("cos"))
            with e.Fori(0, LAYERS) as lay:
                env.lay = lay
                tr = first["mix"]
                for c, name in enumerate(chain):
                    nb = 1 if name in ("KI", "KA") else 2
                    if HEAD_AT[name][1] is None:
                        e.wait_ge(tr[1].sem, tr[1].at("cp." + name))
                    else:
                        e.wait_ge(tr[2].sem, tr[2].at("y." + name))
                    if c >= 2:
                        e.wait_ge(tr[2].sem, tr[2].at("h." + chain[c - 2]))
                    shape = lambda ap: ap.rearrange("p (b s) -> p b s", b=nb)
                    p_.tensor_tensor(shape(ubuf[:, c % 2, 0:nb * S]), shape(ybuf[:, c % 2, 0:nb * S]), bc(cosT[:], nb),
                                     ALU.mult).then_inc(tr[3].sem, tr[3].did("u." + name))
            if BLOCKS > 1:
                with e.Fori(0, LAYERS) as lay:
                    env.lay = lay
                    pool_mix2(e)
            env.lay = 0

    return {n: t.names for n, t in tracks.items()}


BLOCKS = 2


def kernel(**inputs):
    import concourse.bacc as bacc
    from concourse.bass_utils import run_bass_kernel_spmd

    def build(plan):
        nc = bacc.Bacc("TRN2", target_bir_lowering=False, num_devices=1)
        args = {k: nc.dram_tensor(f"in_{k}_dram", v.shape, mybir.dt.from_np(v.dtype), kind="ExternalInput").ap()
                for k, v in arrays.items()}
        out = nc.dram_tensor("out_0_dram", (1, S, D), F32, kind="ExternalOutput").ap()
        return nc, program(nc, args, out, plan)

    arrays = {k: np.ascontiguousarray(v) for k, v in inputs.items()}
    _, plan = build({})
    nc, _ = build(plan)
    r = run_bass_kernel_spmd(nc, [{f"in_{k}_dram": v for k, v in arrays.items()}], core_ids=[0])
    return r.results[0]["out_0_dram"]
```

```python
import math
from contextlib import ExitStack

import numpy as np

import concourse.bass as bass
from concourse import mybir

F32 = mybir.dt.float32
F32R = mybir.dt.float32r
I32 = mybir.dt.int32
ALU = mybir.AluOpType
ACT = mybir.ActivationFunctionType
AX = mybir.AxisListType

P = 128
D = 1024
KB = D // P
S = 256
QT = S // P
LAYERS = 2
WIDE = 13480
DFF = 2816
FB = DFF // P
EPS = 1e-6
LN_EPS = 1e-5
NEG = -1e30
TAKEN = -3e38
HD = 64
TOPK = 64
SLOTS = 4
SLOT = 1024
AHEAD = SLOTS - 1
FFN_TILES = 3 * FB
TAPS = 31
CTAPS = 4
DELTA_AT = KB * S + 6 * S + 4 * QT * 8 + 4
LN_EXP, SILU_TANH = 6, 18
TWO_PI = 2.0 * math.pi

QA, KA, VA, QI, KI, WI = 0, 256, 320, 384, 896, 960
QB, KBC, VB, QC, KC, VC, GATES = 968, 1224, 1480, 1736, 2248, 2760, 3272
IN_WIDTH = 6344
M_QKV, M_Z, M_BETA, M_A, M_GLU, M_GATES = 0, 3072, 4096, 4104, 4112, 6160
M_WIDTH = 8208
R2 = 55
(G_F1, G_P1, G_MX, G_PM, G_F2, G_P2, B_A, B_G, W_B, LN_G, LN_B, B_O, W_DW, W_CV) = (
    0, 1, 2, 3, 4, 5, 6, 7, 8, 9, 10, 11, 12, 43)
ROWS1, ROWS2 = 3 * LAYERS, R2 * LAYERS
SMALL = 7 * LAYERS

T1 = 2 * FFN_TILES + 2 * 26 + 16
T2 = 2 * FFN_TILES + 2 * 34 + 24
assert T1 % SLOTS == 0 and T2 % SLOTS == 0


MIX1_TILES = [("KI", KI, 72), ("QI0", QI, 256), ("QI1", QI + 256, 256), ("KA", KA, 128), ("QA", QA, 256),
              ("QB", QB, 256), ("KB", KBC, 256), ("VB", VB, 256), ("QC0", QC, 256), ("QC1", QC + 256, 256),
              ("KC0", KC, 256), ("KC1", KC + 256, 256), ("VC0", VC, 256), ("VC1", VC + 256, 256)]
N_PROJ = len(MIX1_TILES)
MIX1_TILES += [("GATE", GATES + 256 * i, 256) for i in range(12)]
KEY_TILES = [FFN_TILES + 2 * i for i in range(N_PROJ) if MIX1_TILES[i][0] in ("KI", "KA")]
HEAD_AT = {"KI": (0, None), "KA": (1, 1), "QI0": (2, None), "QI1": (4, None), "QA": (6, 0), "QB": (8, 2),
           "KB": (10, 3), "QC0": (12, 4), "QC1": (14, 4), "KC0": (16, 5), "KC1": (18, 5)}
MIX2_TILES = ([("BETA", M_BETA, 8), ("A", M_A, 8)]
              + [(n, c + 256 * i, 256) for i in range(4) for n, c in (("GLU_A", M_GLU), ("GLU_G", M_GLU + D))]
              + [("QKV", M_QKV + 256 * i, 256) for i in range(12)]
              + [("Z", M_Z + 256 * i, 256) for i in range(4)]
              + [("GATE", M_GATES + 256 * i, 256) for i in range(8)])
UNITS = [(g, q) for g in ("B", "C0", "C1", "A") for q in range(QT)]


INDEX_HEADS = [(0, (0, 2, 4, 6)), (0, (1, 3, 5, 7)), (1, (0, 2)), (1, (1, 3)), (1, (4, 6)), (1, (5, 7))]


class Track:

    def __init__(self, sem, plan, name, env):
        self.sem, self.names, self.env = sem, [], env
        self.plan = plan.setdefault(name, [])

    def did(self, event):
        assert event not in self.names, event
        self.names.append(event)
        return 1

    def at(self, event):
        if event not in self.plan:
            self.env.missing.append((self, event))
            return 1
        return self.env.lay * len(self.plan) + self.plan.index(event) + 1


class Tiles:

    def __init__(self, quads, k=0, twice=()):
        self.quads, self.k, self.it, self.twice = quads, k, 0, twice

    def number(self):
        return (self.quads + self.it) * SLOTS + self.k

    def slot(self):
        return self.k % SLOTS

    def landed(self):
        return (self.quads + self.it + (self.k // SLOTS + 1)) * 16

    def loop(self, e, rounds, tiles, body):
        k0 = self.k
        with e.Fori(0, rounds) as it:
            self.it = it * (tiles // SLOTS)
            body(it)
        assert self.k == k0 + tiles and tiles % SLOTS == 0
        self.k, self.it = k0 + rounds * tiles, 0


class Env:
    pass


def program(nc, a, out, plan):
    env = Env()
    counted = bool(plan)
    env.lay, env.missing = 0, []
    tracks = {}
    with ExitStack() as ctx:
        def sb(name, shape, dt=F32):
            return ctx.enter_context(nc.sbuf_tensor(name, [P] + shape, dt))[:]

        def sem(name):
            return ctx.enter_context(nc.semaphore(name))

        def track(name):
            tracks[name] = Track(sem(name), plan, name, env)
            return tracks[name]

        ring = sb("ring", [SLOTS, SLOT])
        x = sb("x", [KB, S])
        xh = sb("xh", [KB, S], F32R)
        xl = sb("xl", [KB, S], F32R)
        wh = sb("wh", [SLOTS, SLOT], F32R)
        wl = sb("wl", [SLOTS, SLOT], F32R)
        sq = sb("sq", [KB, S])
        rstd = sb("rstd", [2, 2 * S])
        act2 = sb("act2", [2, 2, S])
        with nc.sbuf_tensor("hh", [P, FB * S], F32R) as t_hh, nc.sbuf_tensor("hl", [P, FB * S], F32R) as t_hl:
            hh, hl = t_hh[:], t_hl[:]
        hid = sb("hid", [24 * S])
        with nc.sbuf_tensor("oh", [P, KB, S], F32R) as t_oh, nc.sbuf_tensor("ol", [P, KB, S], F32R) as t_ol:
            oh, ol = t_oh[:], t_ol[:]
        heads = sb("heads", [24, S])
        merged = heads[:, 16:24, :]
        ident = sb("ident", [P])
        ones = sb("ones", [P])
        ones64 = sb("ones64", [P])
        rot = sb("rot", [P])
        cmask = sb("cmask", [S])
        cosT = sb("cosT", [S])
        sinT = sb("sinT", [S])
        consts = sb("consts", [4])
        cols1 = sb("cols1", [KB, ROWS1])
        cols2 = sb("cols2", [KB, ROWS2])
        small = sb("small", [SMALL])
        small2 = sb("small2", [LAYERS])
        lam = sb("lam", [LAYERS])
        gd = sb("gd", [2, 8])
        g1 = sb("g1", [KB, 3])
        h1 = sb("h1", [8])
        g2 = sb("g2", [KB, R2])
        h2 = sb("h2", [4])
        levels = sb("levels", [7, P])
        tmask = sb("tmask", [P])
        with nc.sbuf_tensor("before", [P, DELTA_AT], F32), nc.sbuf_tensor("ch", [P, KB, S], F32R) as t_ch, \
                nc.sbuf_tensor("cl", [P, KB, S], F32R) as t_cl:
            ch, cl = t_ch[:], t_cl[:]
        W = sb("W", [WIDE])
        PS = ctx.enter_context(nc.psum_tensor("PS", [P, 8, 512], F32))

        landed = [sem(f"weights_landed_{i}") for i in range(SLOTS)]
        used = sem("weight_parts_used")
        hi_ready = sem("weight_high_part_ready")
        lo_ready = sem("weight_low_part_ready")
        gu_ready = sem("ffn_gate_up_ready")
        gate_ready = sem("ffn_gate_normed")
        silu_ready = sem("ffn_silu_ready")
        hid_steps = sem("ffn_hidden_steps")
        hid_done = sem("ffn_hidden_done")
        down_ready = sem("ffn_down_ready")
        x_upd = sem("residual_updated")
        passed = {e: sem(f"wait_passed_{e}") for e in ("sync", "vector", "tensor", "gpsimd")}
        x_in = sem("x_loaded")
        params_in = sem("params_loaded")
        params2_in = sem("second_params_loaded")
        out_done = sem("output_written")
        out_ready = sem("output_block_ready")
        pro_pe, pro_act, pro_dve, pro_pool = (track("setup_" + e) for e in ("products", "scalar", "vector", "pool"))
        names = ("norm", "mix", "soft")
        first = {n: [track(f"first_{n}_{e}") for e in ("products", "scalar", "vector", "pool")] for n in names}
        second = {n: [track(f"second_{n}_{e}") for e in ("products", "scalar", "vector", "pool")] for n in
                  ("norm", "mix", "delta", "conv")}

        def bc(ap, n):
            return ap.unsqueeze(1).to_broadcast([ap.shape[0], n, ap.shape[1]])

        def bcl(ap, n):
            return ap.unsqueeze(2).to_broadcast([ap.shape[0], ap.shape[1], n])

        def bank(b, lo=0, hi=512):
            return PS[:, b, lo:hi]

        def slot(s):
            return ring[:, s, :]

        def hold(e, who, s, value):
            e.wait_ge(s, value)
            e.sem_inc(passed[who], 1)

        block = ctx.enter_context(nc.Block())

        off = [0]

        def view(width):
            at = off[0]
            off[0] += width
            assert off[0] <= WIDE, off[0]
            return W[:, at:at + width]

        rows = view(D)
        srow = view(P)
        xin = view(QT * D).rearrange("p (t d) -> p t d", t=QT)
        pos_i = view(S).bitcast(I32)
        posf = view(S)
        ang = view(S)
        red = view(S)
        red2 = view(S)
        lamb = view(LAYERS * 4 * HD)
        lprod = view(LAYERS * 2 * HD)
        lsum = view(LAYERS * 2)
        lexp = view(LAYERS * 2)
        invrow = view(P)
        invf = view(1)
        inv_freq = [float(np.float32(500000.0) ** np.float32(-2.0 * i / 16)) for i in range(8)]
        lam_init = [0.8 - 0.6 * math.exp(-0.3 * i) for i in range(LAYERS)]
        def loader(q, signal):
            def ld(dst, src):
                q.dma_start(dst, src, allow_slow_non_contiguous=dst.shape[0] == 8).then_inc(signal, 16)
            return ld

        def load_params(q):
            ld = loader(q, params_in)
            ld(pos_i, a["positions"].to_broadcast([P, S]))
            ld(lamb, a["lambda_params"].rearrange("l r d -> (l r d)").unsqueeze(0).to_broadcast([P, LAYERS * 4 * HD]))
            ld(gd[0:8, 0, 0:LAYERS], a["gdn_a_log_2"].rearrange("l h -> h l"))
            ld(gd[0:8, 1, 0:LAYERS], a["gdn_dt_bias_2"].rearrange("l h -> h l"))
            ld(rows[0:3 * LAYERS, :], a["norm_g"].rearrange("l r d -> (l r) d"))
            for l in range(LAYERS):
                ld(srow[7 * l:7 * l + 6, 0:HD], a["qk_norm_g"][l])
                ld(srow[7 * l:7 * l + 6, HD:P], a["qk_norm_g"][l])
                ld(srow[7 * l + 6:7 * l + 7, :], a["diff_subln_g"][l:l + 1, :])
        N_PARAM = 16 * (5 + LAYERS * 3)

        def load_params2(q):
            ld = loader(q, params2_in)
            for l in range(LAYERS):
                r = R2 * l
                for at, key in ((G_F1, "ffn1_norm_pre_2"), (G_P1, "ffn1_norm_post_2"), (G_MX, "mix_norm_pre_2"),
                                (G_PM, "mix_norm_post_2"), (G_F2, "ffn2_norm_pre_2"), (G_P2, "ffn2_norm_post_2"),
                                (W_B, "cnv_dw_b_2"), (LN_G, "cnv_ln_g_2"), (LN_B, "cnv_ln_b_2"), (B_O, "cnv_b_o_2")):
                    ld(rows[r + at:r + at + 1, :], a[key][l:l + 1, :])
                ld(rows[r + B_A:r + B_A + 2, :], a["cnv_pw1_b_2"][l].rearrange("(r d) -> r d", d=D))
                ld(rows[r + W_DW:r + W_DW + TAPS, :], a["cnv_dw_w_2"][l])
                ld(rows[r + W_CV:r + W_CV + 3 * CTAPS, :], a["gdn_conv_w_2"][l].rearrange("t (s d) -> (t s) d", d=D))
                ld(srow[l:l + 1, :], a["gdn_norm_w_2"][l:l + 1, :])
        N_PARAM2 = 16 * LAYERS * 14

        def load_tile(sp, t, part):
            hold(sp, "sync", lo_ready, t.number() + 1)
            dst = slot(t.slot())
            if len(part.shape) == 3:
                dst = dst.rearrange("p (k n) -> p k n", k=KB)[:, 0:part.shape[1], :]
            sp.dma_start(dst, part).then_inc(landed[t.slot()], 16)
            t.k += 1

        def kmajor(w2d):
            return w2d.rearrange("(k p) n -> p k n", p=P)

        def load_ffn(sp, t, gate, up, down):
            def gate_up(it):
                for jj in range(4):
                    for w in (gate, up):
                        load_tile(sp, t, w[:, :, bass.ds(it * (4 * P) + jj * P, P)])
            t.loop(sp, FB // 4, 8, gate_up)
            for j in range(FB - FB % 4, FB):
                for w in (gate, up):
                    load_tile(sp, t, w[:, :, j * P:(j + 1) * P])

            def downs(it):
                for c in range(4):
                    load_tile(sp, t, down[bass.ds(it * (4 * P) + c * P, P), :])
            t.loop(sp, FB // 4, 4, downs)
            for c in range(FB - FB % 4, FB):
                load_tile(sp, t, down[c * P:(c + 1) * P, :])

        def load_step(sp, t, w, name, c, n):
            if name in ("KI", "KA"):
                load_tile(sp, t, w[:, :, c:c + P])
                load_tile(sp, t, w[:, :, c + HD:c + HD + P])
            elif name in ("BETA", "A"):
                for h in range(2):
                    load_tile(sp, t, w[:, 4 * h:4 * h + 4, c:c + P])
            else:
                for m in range(2):
                    load_tile(sp, t, w[:, :, c + m * P:c + (m + 1) * P])

        @block.sync
        def _(sp):
            sp.dma_start(xin, a["x"].rearrange("a (t p) d -> p (a t) d", p=P)).then_inc(x_in, 16)
            with sp.Fori(0, LAYERS) as lay:
                t = Tiles(lay * (T1 // SLOTS))
                for half in range(2):
                    if half == 1:
                        w = kmajor(a["w_in"][lay])
                        for name, c, n in MIX1_TILES:
                            load_step(sp, t, w, name, c, n)
                        for key in ("w_branch", "w_out"):
                            for c in range(KB):
                                load_tile(sp, t, a[key][lay][c * P:(c + 1) * P, :])
                    load_ffn(sp, t, kmajor(a["ffn_w_gate"][lay, half]), kmajor(a["ffn_w_up"][lay, half]),
                             a["ffn_w_down"][lay, half])
                assert t.k == T1
            if BLOCKS > 1:
                with sp.Fori(0, LAYERS) as lay:
                    t = Tiles(lay * (T2 // SLOTS) + LAYERS * (T1 // SLOTS))
                    for half in range(2):
                        if half == 1:
                            w = kmajor(a["mix_w_in_2"][lay])
                            for name, c, n in MIX2_TILES:
                                load_step(sp, t, w, name, c, n)
                            for key in ("gdn_w_o_2", "cnv_w_o_2", "mix_w_out_2"):
                                for c in range(KB):
                                    load_tile(sp, t, a[key][lay][c * P:(c + 1) * P, :])
                        w = kmajor(a[f"ffn{half + 1}_w_in_2"][lay])
                        load_ffn(sp, t, w[:, :, 0:DFF], w[:, :, DFF:2 * DFF], a[f"ffn{half + 1}_w_out_2"][lay])
                    assert t.k == T2
            ov = out.rearrange("a (t p) d -> p (a t) d", p=P)
            for q in range(QT):
                sp.wait_ge(out_ready, 2 * q + 2)
                sp.dma_start(ov[:, q, :], heads[:, 4 * q:4 * q + 4, :].rearrange("p k s -> p (k s)")).then_inc(out_done, 16)
            sp.wait_ge(out_done, 16 * QT)

        off[0] = 0
        ybuf = view(2 * 512).rearrange("p (i n) -> p i n", i=2)
        tbuf = view(2 * 512).rearrange("p (i n) -> p i n", i=2)
        ubuf = view(2 * 512).rearrange("p (i n) -> p i n", i=2)
        va = view(QT * HD).rearrange("p (t n) -> p t n", t=QT)
        wi = view(QT * 8).rearrange("p (t n) -> p t n", t=QT)
        vb = view(QT * 256).rearrange("p (t n) -> p t n", t=QT)
        vc = view(QT * 512).rearrange("p (t n) -> p t n", t=QT)
        rl = view(2 * 512).rearrange("p (i n) -> p i n", i=2)
        isc = [view(P), view(S)]
        work = [view(P), view(S)]
        top8 = view(8)
        ibias = [view(P), view(S)]
        smb = view(2 * 1024).rearrange("p (i n) -> p i n", i=2)
        ptb = view(2 * 1024).rearrange("p (i n) -> p i n", i=2)
        nmax = view(8).rearrange("p (i n) -> p i n", i=2)
        rsum = view(8).rearrange("p (i n) -> p i n", i=2)
        rinv = view(8).rearrange("p (i n) -> p i n", i=2)
        oT1 = view(KB * S).rearrange("p (k s) -> p k s", k=KB)

        off[0] = 0
        conv = view(KB * S).rearrange("p (k s) -> p k s", k=KB)
        ab = view(2 * S).rearrange("p (i s) -> p i s", i=2)
        lg = view(4 * S).rearrange("p (i s) -> p i s", i=4)
        gtok = view(QT * 8).rearrange("p (t h) -> p t h", t=QT)
        ngtok = view(QT * 8).rearrange("p (t h) -> p t h", t=QT)
        btok = view(QT * 8).rearrange("p (t h) -> p t h", t=QT)
        bgtok = view(QT * 8).rearrange("p (t h) -> p t h", t=QT)
        cdec = view(4)
        shared_at = off[0]
        assert shared_at == DELTA_AT, shared_at
        glu = view(KB * (S + TAPS - 1)).rearrange("p (k s) -> p k s", k=KB)
        gth = view(2 * 512).rearrange("p (i n) -> p i n", i=2)
        qpad = view(2 * 2 * (S + CTAPS - 1)).rearrange("p (i b s) -> p i b s", i=2, b=2)
        off[0] = shared_at
        DU = {}
        for c in range(QT):
            for n in ("gbm", "at", "al", "qkt", "kx", "vx", "T", "U"):
                DU[n, c] = view(512).rearrange("p (h n) -> p h n", h=4)
            DU["m1", c], DU["u", c] = DU["gbm", c], DU["at", c]
        qd = view(512).rearrange("p (h n) -> p h n", h=4)
        wT = view(512).rearrange("p (h n) -> p h n", h=4)
        st = view(512).rearrange("p (h n) -> p h n", h=4)

        acc = lambda m, b0=0: bank(b0 + m // 2, (m % 2) * S, (m % 2 + 1) * S)
        pair = lambda b: PS[:, b, :].rearrange("p (i s) -> p i s", i=2)

        oT2 = heads[:, 16:24, :]

        def three(o, w, x, start, stop):
            first_ = mm(o, w[0], x[0], start=start, stop=False, skip_group_check=True)
            mm(o, w[0], x[1], start=False, stop=False, skip_group_check=True)
            return first_, mm(o, w[1], x[0], start=False, stop=stop, skip_group_check=True)

        def wblk(s, i, lo=0, hi=P):
            return wh[:, s, i * P + lo:i * P + hi], wl[:, s, i * P + lo:i * P + hi]

        def xblk(k, lo=0, hi=S):
            return xh[:, k, lo:hi], xl[:, k, lo:hi]

        def part_views(t, parts):
            dst, src = parts[:, t.slot(), :], slot(t.slot())
            if t.k in t.twice:
                dst = dst.rearrange("p (k i n) -> p k i n", k=KB, i=2)
                src = src.rearrange("p (k n) -> p k n", k=KB)[:, :, 0:HD].unsqueeze(2).to_broadcast([P, KB, 2, HD])
            return dst, src

        def high(e, t, n=1):
            for _ in range(n):
                s_ = t.slot()
                e.wait_ge(landed[s_], t.landed())
                e.wait_ge(used, t.number() + 1)
                dst, src = part_views(t, wh)
                act_(dst, src, ACT.Copy).then_inc(hi_ready, 1)
                t.k += 1

        def low(e, t, n=1, engine=None, handed=False):
            for _ in range(n):
                if handed:
                    hold(e, "gpsimd" if engine is nc.gpsimd else "vector", lo_ready, t.number() + SLOTS)
                    handed = False
                e.wait_ge(hi_ready, t.number() + 1)
                dst, src = part_views(t, wl)
                (engine or v_).tensor_tensor(dst, src, part_views(t, wh)[0], ALU.subtract).then_inc(lo_ready, 1)
                t.k += 1

        def hidb(j, n=1):
            return hid[:, j * S:(j + n) * S]

        def sqp(i):
            return sq[:, 2 * i:2 * i + 2, :].rearrange("p k s -> p (k s)")

        def blk2(buf, i):
            return buf[:, 2 * i:2 * i + 2, :].rearrange("p k s -> p (k s)")

        chain = [n for n, _, _ in MIX1_TILES[:N_PROJ] if n in HEAD_AT]
        mm = nc.tensor.matmul
        act_ = nc.scalar.activation
        v_ = nc.vector

        def pe_down(pe, t, b0, tiles, rhs, ready, sig):
            for c in range(tiles):
                pe.wait_ge(lo_ready, t.number() + (SLOTS + 1))
                ready(c)
                last = c == tiles - 1
                for m in range(KB):
                    one, ins = three(acc(m, b0), wblk(t.slot(), m), rhs(c), c == 0 and m % 2 == 0, last)
                    if m == 0:
                        one.then_inc(used, 1)
                    elif last and m % 2 == 1:
                        tr, name = sig
                        ins.then_inc(tr.sem, tr.did(f"{name}.{m // 2}"))
                t.k += 1

        def pe_sum(pe, tr, tag, bnk, ready, src=None):
            for k in range(KB):
                ready(k)
                ins = mm(bank(bnk, 0, S), ones, (sq if src is None else src)[:, k, :], start=(k == 0), stop=(k == KB - 1))
            ins.then_inc(tr[0].sem, tr[0].did(tag + ".sum"))

        def pe_norm(pe, tr, tag, bnk=7, who="sq"):
            def ready(k):
                if k % 2 == 0:
                    pe.wait_ge(tr[1].sem, tr[1].at(f"{tag}.sq{k // 2}"))
            pe_sum(pe, tr, tag, bnk, ready)

        def pe_ffn(pe, t, f, tr, tag):
            def gate_up(it, j):
                pe.wait_ge(hid_done, f * FB + it * 4 + (j + 1))
                for o in (0, S):
                    pe.wait_ge(lo_ready, t.number() + (SLOTS + 1))
                    for k in range(KB):
                        if (j, o) == (0, 0):
                            pe.wait_ge(tr[2].sem, tr[2].at(f"{tag}.xl{k}"))
                        one, ins = three(bank(4 + j % 4, o, o + S), wblk(t.slot(), k), xblk(k), k == 0, k == KB - 1)
                        if k == 0:
                            one.then_inc(used, 1)
                    t.k += 1
                ins.then_inc(gu_ready, 1)
            gate_up(0, 0)
            for k in range(2):
                pe.wait_ge(tr[2].sem, tr[2].at(f"{tag}.add2"))
                ins = mm(bank(0, 0, S), ones, sq[:, k, :], start=(k == 0), stop=(k == 1))
            ins.then_inc(tr[0].sem, tr[0].did(tag + ".sum"))
            gate_up(0, 1)
            t.loop(pe, (FB - 2) // 4, 8, lambda it: [gate_up(it, 2 + jj) for jj in range(4)])

            def down(c, x):
                hold(pe, "tensor", lo_ready, t.number() + (SLOTS + 1))
                for m in range(KB):
                    one, ins = three(acc(m), wblk(t.slot(), m), x, c == 0 and m % 2 == 0, c == FB - 1)
                    if m == 0:
                        one.then_inc(used, 1)
                    elif c == FB - 1 and m % 2 == 1:
                        ins.then_inc(down_ready, 1)
                t.k += 1

            def hblk(c):
                return hh[:, c * S:(c + 1) * S], hl[:, c * S:(c + 1) * S]

            pe.wait_ge(hid_done, f * FB + (4 + FB - 2))
            for c in range(2):
                down(c, hblk(c))

            def four_downs(it):
                for c in range(4):
                    at = bass.ds(it * (4 * S) + (2 + c) * S, S)
                    down(-1, (hh[:, at], hl[:, at]))
            t.loop(pe, (FB - 6) // 4, 4, four_downs)
            for c in range(FB - 4, FB):
                if c == FB - 2:
                    hold(pe, "tensor", hid_done, f * FB + (4 + FB))
                down(c, hblk(c))

        def pe_mix1(pe, t, tr, so):
            norm = first["norm"][2]
            owed = [1]
            evac = {n: (f"act", f"cp.{n}") if n.startswith("V") or HEAD_AT[n][1] is None else ("dve", f"y.{n}")
                    for n, _, _ in MIX1_TILES[:N_PROJ]}
            who = {"act": tr[1], "dve": tr[2]}
            for i in range(N_PROJ + 3):
                if i < N_PROJ:
                    name, _, width = MIX1_TILES[i]
                    b = i % 4
                    if i >= 4:
                        e, ev = evac[MIX1_TILES[i - 4][0]]
                        pe.wait_ge(who[e].sem, who[e].at(ev))
                    if i == 4:
                        pe.wait_ge(tr[1].sem, tr[1].at("cp2.KI"))
                    if i == 7:
                        pe.wait_ge(tr[1].sem, tr[1].at("cp2.KA"))
                    if name.startswith("V"):
                        pe.wait_ge(lo_ready, t.number() + (SLOTS + 2))
                        s_ = t.slot()
                        for q in range(QT):
                            for k in range(KB):
                                w = [z[:, s_:s_ + 2, k * P:(k + 1) * P] for z in (wh, wl)]
                                o = bank(b, q * 256, (q + 1) * 256).rearrange("p (i n) -> p i n", i=2)
                                one, ins = three(o, xblk(k, q * P, (q + 1) * P), w, k == 0, k == KB - 1)
                                if q == 0 and k == 0:
                                    one.then_inc(used, owed[0])
                        t.k += 2
                        owed[0] = 2
                    else:
                        for m in range(2):
                            pe.wait_ge(lo_ready, t.number() + (SLOTS + 1))
                            s_ = t.slot()
                            todo = []
                            if name in ("KI", "KA") and m == 1:
                                n = width - HD
                                for q in range(QT):
                                    todo += [(bank(b, S + q * n, S + (q + 1) * n), xblk(k, q * P, (q + 1) * P),
                                              wblk(s_, k, 0, n), k) for k in range(KB)]
                            else:
                                todo = [(bank(b, m * S, (m + 1) * S), wblk(s_, k), xblk(k), k) for k in range(KB)]
                            for i_, (o, lhs, rhs, k) in enumerate(todo):
                                if (i, m) == (0, 0) and k % 2 == 0:
                                    pe.wait_ge(norm.sem, norm.at(f"mix.xl{k // 2}"))
                                one, ins = three(o, lhs, rhs, k == 0, k == KB - 1)
                                if i_ == 0:
                                    one.then_inc(used, owed[0])
                                    owed[0] = 1
                            t.k += 1
                    ins.then_inc(tr[0].sem, tr[0].did("p." + name))
                if 1 <= i <= N_PROJ:
                    name = MIX1_TILES[i - 1][0]
                    if name in HEAD_AT and HEAD_AT[name][1] is not None:
                        n = S if name == "KA" else 512
                        pe.wait_ge(tr[1].sem, tr[1].at("sq." + name))
                        normed = [n_ for n_ in chain if HEAD_AT[n_][1] is not None]
                        if normed.index(name):
                            pe.wait_ge(tr[1].sem, tr[1].at(normed[normed.index(name) - 1] + ".ln"))
                        mm(bank(4, 0, n), ones64[:], sqp(chain.index(name) % 2)[:, 0:n],
                           start=True, stop=True).then_inc(tr[0].sem, tr[0].did("ss." + name))
                if 2 <= i <= N_PROJ + 1:
                    name = MIX1_TILES[i - 2][0]
                    if name in HEAD_AT:
                        c = chain.index(name)
                        n = S if name in ("KA", "KI") else 512
                        e, ev = (who["act"], "cp." + name) if HEAD_AT[name][1] is None else (who["dve"], "y." + name)
                        pe.wait_ge(e.sem, e.at(ev))
                        if c:
                            pe.wait_ge(tr[2].sem, tr[2].at("t." + chain[c - 1]))
                        mm(bank(5, 0, n), rot[:], ybuf[:, c % 2, 0:n], start=True,
                           stop=True).then_inc(tr[0].sem, tr[0].did("rot." + name))
                if 5 <= i <= 10:
                    j = i - 5
                    if j == 0:
                        pe.wait_ge(tr[2].sem, tr[2].at("h.QI1"))
                    if j >= 2:
                        pe.wait_ge(tr[1].sem, tr[1].at(f"relu{j - 2}"))
                    q, hs = INDEX_HEADS[j]
                    nk = P * (q + 1)
                    for i_, h in enumerate(hs):
                        r = slice((h % 2) * HD, (h % 2 + 1) * HD)
                        ins = mm(bank(6 + j % 2, i_ * nk, (i_ + 1) * nk),
                                 heads[r, 2 + h // 2, q * P:(q + 1) * P], heads[r, 0, 0:nk], start=True, stop=True)
                    ins.then_inc(tr[0].sem, tr[0].did(f"index{j}"))

            maps = {"A": [(6 + i, 1, c) for c in range(2) for i in range(2)],
                    "B": [(8 + i, 10 + i, c) for c in range(2) for i in range(2)],
                    "C0": [(12 + i, 16 + i, c) for c in range(2) for i in range(2)],
                    "C1": [(14 + i, 18 + i, c) for c in range(2) for i in range(2)]}
            g = [0]

            def gate():
                k = g[0]
                g[0] += 1
                if k >= 2:
                    pe.wait_ge(so[1].sem, so[1].at(f"gate{k - 2}"))
                for m in range(2):
                    pe.wait_ge(lo_ready, t.number() + (SLOTS + 1))
                    for k2 in range(KB):
                        one, ins = three(bank(k % 2, m * S, (m + 1) * S), wblk(t.slot(), k2), xblk(k2), k2 == 0,
                                         k2 == KB - 1)
                        if k2 == 0:
                            one.then_inc(used, owed[0])
                            owed[0] = 1
                    t.k += 1
                ins.then_inc(so[0].sem, so[0].did(f"gate{k}"))

            pe.wait_ge(tr[2].sem, tr[2].at("h.KC1"))
            pe.wait_ge(tr[1].sem, tr[1].at("cp.VC1"))
            pe.wait_ge(tr[1].sem, tr[1].at("relu5"))
            for j in range(len(UNITS) + 2):
                if j < len(UNITS):
                    gr, q = UNITS[j]
                    if j >= 1:
                        pe.wait_ge(so[2].sem, so[2].at(f"sm{j - 1}"))
                    nk = P * (q + 1)
                    for m, (qb, kb, half) in enumerate(maps[gr]):
                        r = slice(half * HD, (half + 1) * HD)
                        o = (m % 2) * nk
                        ins = mm(bank(4 + half, o, o + nk), heads[r, qb, q * P:(q + 1) * P],
                                 heads[r, kb, 0:nk], start=True, stop=True)
                    ins.then_inc(so[0].sem, so[0].did(f"s{j}"))
                gate()
                if 1 <= j <= len(UNITS):
                    u = j - 1
                    gr, q = UNITS[u]
                    pe.wait_ge(so[2].sem, so[2].at(f"p{u}"))
                    if u >= 1:
                        pe.wait_ge(so[1].sem, so[1].at(f"pt{u - 1}"))
                    nm = 2 if gr[0] == "C" else 4
                    src = smb[:, u % 2, :].rearrange("p (m k n) -> p m k n", n=P, k=q + 1)
                    for m in range(nm):
                        for kb in range(q + 1):
                            i = m * (q + 1) + kb
                            ins = nc.tensor.transpose(bank(6 + i // 4, (i % 4) * P, (i % 4 + 1) * P),
                                                      src[:, m, kb, :], ident[:])
                    ins.then_inc(so[0].sem, so[0].did(f"t{u}"))
                if j >= 2:
                    u = j - 2
                    gr, q = UNITS[u]
                    pe.wait_ge(so[1].sem, so[1].at(f"pt{u}"))
                    gi = u // 2
                    if gi >= 2:
                        pe.wait_ge(so[1].sem, so[1].at(f"o{2 * (gi - 2) + 1}"))
                    if q == 1:
                        pe.wait_ge(so[1].sem, so[1].at(f"o{u - 1}"))
                    pt = ptb[:, u % 2, :].rearrange("p (m k n) -> p m k n", n=P, k=q + 1)
                    for m in range(2 if gr[0] == "C" else 4):
                        for kb in range(q + 1):
                            if gr == "A":
                                v, r, blk = va[:, kb, :], slice((m // 2) * HD, (m // 2 + 1) * HD), m % 2
                            elif gr == "B":
                                h = 2 * (m % 2) + m // 2
                                v, r, blk = vb[:, kb, h * HD:(h + 1) * HD], slice((m // 2) * HD, (m // 2 + 1) * HD), m % 2
                            else:
                                h = m + 2 * int(gr[1])
                                v, r, blk = vc[:, kb, h * P:(h + 1) * P], slice(0, P), m
                            o = blk * S + q * P
                            ins = mm(PS[r, 2 + gi % 2, o:o + P], v, pt[:, m, kb, :], start=(kb == 0), stop=(kb == q),
                                     skip_group_check=True)
                    ins.then_inc(so[0].sem, so[0].did(f"o{u}"))
                if j >= len(UNITS):
                    gate()
            oblk = lambda k: (oh[:, k, :], ol[:, k, :])

            def ready_a(c):
                if c == 0:
                    pe.wait_ge(so[2].sem, so[2].at("ol1"))
                    pe.wait_ge(so[1].sem, so[1].at("gate11"))
            pe_down(pe, t, 0, 2, lambda k: oblk(k), ready_a, (tr[0], "ya"))
            pe_down(pe, t, 4, 2, lambda k: oblk(2 + k), lambda c: None, (tr[0], "yb"))
            for i in range(2):
                pe.wait_ge(so[1].sem, so[1].at(f"sqc{i}"))
                if i == 0:
                    pe.wait_ge(tr[2].sem, tr[2].at("ma3"))
                mm(bank(i), ones[:], sqp(i), start=True,
                   stop=True).then_inc(so[0].sem, so[0].did(f"ssc{i}"))

            def ready_c(c):
                if c % 2 == 0:
                    pe.wait_ge(so[2].sem, so[2].at(f"ol{2 + c // 2}"))
            pe_down(pe, t, 0, 4, lambda k: oblk(4 + k), ready_c, (tr[0], "yc"))

            def ready_o(c):
                if c % 2 == 0:
                    pe.wait_ge(tr[2].sem, tr[2].at(f"ml{c // 2}"))
            pe_down(pe, t, 0, 8, xblk, ready_o, (tr[0], "out"))

        mix2 = []
        for n, c, w_ in MIX2_TILES:
            mix2.append(n + str(sum(m.startswith(n + "") and m[:len(n)] == n and m[len(n):].isdigit() for m in mix2)))
        m2 = second["mix"]
        dl = second["delta"]
        cv = second["conv"]

        def evac2(i):
            n = mix2[i]
            if n.startswith("A"):
                return m2[2], "cp." + n
            if n.startswith("GLU_A"):
                return m2[2], f"glu.{n[5:]}.1"
            if n.startswith("GLU_G"):
                return m2[1], f"gth.{n[5:]}.1"
            return m2[1], "cp." + n

        def pe_tile2(pe, t, i):
            name = mix2[i]
            if i >= 4:
                tr, ev = evac2(i - 4)
                pe.wait_ge(tr.sem, tr.at(ev))
            for m in range(2):
                pe.wait_ge(lo_ready, t.number() + (SLOTS + 1))
                if name in ("BETA0", "A0"):
                    todo = [(bank(i % 4, 0, S), j, 4 * m + j) for j in range(4)]
                else:
                    todo = [(bank(i % 4, m * S, (m + 1) * S), k, k) for k in range(KB)]
                for o, j, k in todo:
                    if i == 0 and k % 2 == 0:
                        pe.wait_ge(second["norm"][2].sem, second["norm"][2].at(f"mix.xl{k // 2}"))
                    one, ins = three(o, wblk(t.slot(), j), xblk(k), k == 0, k == KB - 1)
                    if j == 0:
                        one.then_inc(used, 1)
                t.k += 1
            ins.then_inc(m2[0].sem, m2[0].did("p." + name))

        def pe_mix2(pe, t):
            first_z = mix2.index("Z0")
            for i in range(len(mix2)):
                pe_tile2(pe, t, i)
                if i == 9:
                    for j, ev in ((0, "gsum1"), (1, "beta")):
                        hold(pe, "tensor", m2[2].sem, m2[2].at(ev))
                        for c in range(QT):
                            src = lg[0:8, 3, c * P:(c + 1) * P] if j == 0 else ab[0:8, 1, c * P:(c + 1) * P]
                            ins = nc.tensor.transpose(bank(4, 16 * j + 8 * c, 16 * j + 8 * c + 8), src, ident[0:8, 0:8])
                    ins.then_inc(m2[0].sem, m2[0].did("tok"))
                if i in (first_z, first_z + 1):
                    for j in range(4 * (i - first_z), 4 * (i - first_z) + 4):
                        pe.wait_ge(m2[1].sem, m2[1].at(f"l2sq{j}"))
                        if j >= 4:
                            pe.wait_ge(m2[1].sem, m2[1].at(f"l2.{j - 4}.ln"))
                        mm(bank(4 + j % 4), ones, sqp(j % 4), start=True,
                           stop=True).then_inc(m2[0].sem, m2[0].did(f"l2s{j}"))
            pe_delta(pe)
            for i in range(4):
                pe.wait_ge(dl[1].sem, dl[1].at(f"osq{i}"))
                mm(bank(i), ones, sqp(i), start=True, stop=True).then_inc(dl[0].sem, dl[0].did(f"os{i}"))

            def ready_a(c):
                if c % 2 == 0:
                    pe.wait_ge(dl[2].sem, dl[2].at(f"ol{c // 2}"))
            pe_down(pe, t, 0, 8, lambda k: (oh[:, k, :], ol[:, k, :]), ready_a, (m2[0], "ya"))

            def ready_b(c):
                if c % 2 == 0:
                    pe.wait_ge(cv[2].sem, cv[2].at(f"cl{c // 2}"))
            pe_down(pe, t, 4, 8, lambda k: (ch[:, k, :], cl[:, k, :]), ready_b, (m2[0], "yb"))

            def ready_o(c):
                if c % 2 == 0:
                    pe.wait_ge(m2[2].sem, m2[2].at(f"ml{c // 2}"))
            pe_down(pe, t, 0, 8, xblk, ready_o, (m2[0], "out"))

        def pe_delta(pe):
            did = lambda ins, n: ins.then_inc(dl[0].sem, dl[0].did(n))
            wv = lambda n: pe.wait_ge(dl[2].sem, dl[2].at(n))
            wa = lambda n: pe.wait_ge(dl[1].sem, dl[1].at(n))
            pe.wait_ge(m2[1].sem, m2[1].at("cp.GATE7"))

            def conv_ready(k):
                if k == 0:
                    pe.wait_ge(cv[2].sem, cv[2].at("cv.1.30.3"))
                    wv("0.kx.0")

            def four(b, f):
                for h in range(4):
                    ins = f(h, bank(b, h * P, (h + 1) * P))
                return ins
            for g in range(2):
                for c in range(QT):
                    B = 4 * c
                    tk = slice(c * P, (c + 1) * P)
                    if g == 1:
                        wa(f"0.oc.{c}")
                        if c == 1:
                            wv("0.vn")
                        else:
                            wa("0.sc")
                    did(four(B, lambda h, o: mm(o, ident[0:8, 4 * g + h:4 * g + h + 1].to_broadcast([8, P]), lg[0:8, 3, tk], start=True, stop=True)), f"{g}.gb.{c}")
                    did(four(B + 1, lambda h, o: mm(o, ident[0:8, 4 * g + h:4 * g + h + 1].to_broadcast([8, P]), ab[0:8, 1, tk], start=True, stop=True)), f"{g}.bb.{c}")
                    if g == 0 and c == 0:
                        pe.wait_ge(m2[2].sem, m2[2].at("l2n7"))
                    did(four(B + 2, lambda h, o: mm(o, heads[:, 8 + 4 * g + h, tk], heads[:, 8 + 4 * g + h, tk], start=True, stop=True)), f"{g}.kk.{c}")
                    did(four(B + 3, lambda h, o: mm(o, heads[:, 8 + 4 * g + h, tk], heads[:, 4 * g + h, tk], start=True, stop=True)), f"{g}.qk.{c}")
                for c in range(QT):
                    B = 4 * c
                    tk = slice(c * P, (c + 1) * P)
                    wv(f"{g}.at0.{c}")
                    did(four(B + 2, lambda h, o: nc.tensor.transpose(o, heads[:, 8 + 4 * g + h, tk], ident)), f"{g}.kt.{c}")
                    wv(f"{g}.qkt.{c}")
                    did(four(B + 3, lambda h, o: nc.tensor.transpose(o, heads[:, 16 + 4 * g + h, tk], ident)), f"{g}.vt.{c}")
                for c in range(QT):
                    B = 4 * c
                    U = DU["U", c]
                    wv(f"{g}.U0.{c}")
                    if c == 1:
                        wa(f"{g}.eg")
                    else:
                        wv(f"{g}.cd0")
                    did(four(B, lambda h, o: nc.tensor.transpose(o, U[:, h, :], ident)), f"{g}.tt.{c}")
                for l in range(1, 7):
                    for c in range(QT):
                        B = 4 * c
                        al, T = DU["al", c], DU["T", c]
                        pe.wait_ge(dl[3].sem, dl[3].at(f"{g}.al{l}.{c}"))
                        if l == 1:
                            wa(f"{g}.T0.{c}")
                            wv(f"{g}.vx.{c}")
                        else:
                            wv(f"{g}.T{l - 1}.{c}")
                        did(four(B + 3, lambda h, o: mm(o, al[:, h, :], T[:, h, :], start=True, stop=True)), f"{g}.m{l}.{c}")
                    if (g, l) == (0, 1):
                        pe_sum(pe, cv, "mean", 2, conv_ready, conv)
                    if (g, l) == (0, 6):
                        wv("0.kx.1")
                        pe_norm(pe, cv, "ln", 6)
                    for c in range(QT):
                        B = 4 * c
                        U, m1 = DU["U", c], DU["m1", c]
                        wa(f"{g}.mc{l}.{c}")
                        did(four(B, lambda h, o: mm(o, m1[:, h, :], U[:, h, :], start=True, stop=True)), f"{g}.pu{l}.{c}")
                        if l < 6:
                            did(four(B + 1, lambda h, o: mm(o, U[:, h, :], m1[:, h, :], start=True, stop=True)), f"{g}.pt{l}.{c}")
                for c in range(QT):
                    B = 4 * c
                    U = DU["U", c]
                    wv(f"{g}.U6.{c}")
                    wv(f"{g}.kx.{c}")
                    if g == 0:
                        pe.wait_ge(cv[1].sem, cv[1].at(("mean", "ln.ln")[c]))
                    did(four(B + 2, lambda h, o: mm(o, U[:, h, :], DU["vx", c][:, h, :], start=True, stop=True)), f"{g}.u.{c}")
                did(four(5, lambda h, o: mm(o, DU["kx", 1][:, h, :], DU["U", 1][:, h, :], start=True, stop=True)), f"{g}.w")
                wa(f"{g}.uc.0")
                did(four(1, lambda h, o: mm(o, DU["kx", 0][:, h, :], DU["u", 0][:, h, :], start=True, stop=True)), f"{g}.s")
                did(four(3, lambda h, o: mm(o, DU["u", 0][:, h, :], DU["qkt", 0][:, h, :], start=True, stop=True)), f"{g}.o.0")
                wa(f"{g}.wc")
                wa(f"{g}.sc")
                did(four(4, lambda h, o: mm(o, wT[:, h, :], st[:, h, :], start=True, stop=True)), f"{g}.ws")
                wv(f"{g}.qd")

                wv(f"{g}.vn")

                def both(h, o):
                    mm(o, st[:, h, :], qd[:, h, :], start=True, stop=False)
                    return mm(o, DU["u", 1][:, h, :], DU["qkt", 1][:, h, :], start=False, stop=True)
                did(four(7, both), f"{g}.o.1")

        def pe_setup(pe):
            pe.wait_ge(x_in, 16)
            pe.wait_ge(pro_pool.sem, pro_pool.at("ident"))
            for b in range(4):
                for k in (2 * b, 2 * b + 1):
                    for q in range(QT):
                        o = (k % 2) * S + q * P
                        ins = nc.tensor.transpose(bank(b, o, o + P), xin[:, q, k * P:(k + 1) * P], ident[:])
                ins.then_inc(pro_pe.sem, pro_pe.did(f"x{b}"))
            pe.wait_ge(params_in, N_PARAM)
            for k in range(KB):
                nc.tensor.transpose(bank(4, k * ROWS1, (k + 1) * ROWS1), rows[0:ROWS1, k * P:(k + 1) * P],
                                    ident[0:ROWS1, 0:ROWS1])
            nc.tensor.transpose(bank(6, 0, SMALL), srow[0:SMALL, :], ident[0:SMALL, 0:SMALL])
            pe.wait_ge(pro_dve.sem, pro_dve.at("invrow"))
            pe.wait_ge(pro_pool.sem, pro_pool.at("ones"))
            mm(bank(7, 0, 1), invrow[0:1, :], ones[0:1, 0:1], start=True,
               stop=True).then_inc(pro_pe.sem, pro_pe.did("small"))

        def pe_setup2(pe):
            pe.wait_ge(params2_in, N_PARAM2)
            for b in range(2):
                for k in range(4):
                    ins = nc.tensor.transpose(bank(4 + b, k * ROWS2, (k + 1) * ROWS2),
                                              rows[0:ROWS2, (4 * b + k) * P:(4 * b + k + 1) * P],
                                              ident[0:ROWS2, 0:ROWS2])
                ins.then_inc(pro_pe.sem, pro_pe.did(f"cols2.{b}"))
            nc.tensor.transpose(bank(6, 0, LAYERS), srow[0:LAYERS, :], ident[0:LAYERS, 0:LAYERS]).then_inc(
                pro_pe.sem, pro_pe.did("small2"))

        def pe_finish(pe):
            for q in range(QT):
                for h in range(2):
                    b = 2 * q + h
                    if b == 0:
                        pe.wait_ge(x_upd, 4 + 4 * 3 * LAYERS * BLOCKS)
                    for k in range(4):
                        ins = nc.tensor.transpose(bank(4 + b, k * P, (k + 1) * P), x[:, 4 * h + k, q * P:(q + 1) * P],
                                                  ident[:])
                    ins.then_inc(pro_pe.sem, pro_pe.did(f"fin{b}"))

        @block.tensor
        def _(pe):
            pe.sem_inc(used, AHEAD)
            pe_setup(pe)
            with pe.Fori(0, LAYERS) as lay:
                env.lay = lay
                t = Tiles(lay * (T1 // SLOTS))
                tr = first["norm"]
                pe_ffn(pe, t, lay * 2, tr, "f0")
                pe_norm(pe, tr, "mix")
                pe_mix1(pe, t, first["mix"], first["soft"])
                pe_ffn(pe, t, lay * 2 + 1, tr, "f1")
            env.lay = 0
            if BLOCKS > 1:
                pe_setup2(pe)
                with pe.Fori(0, LAYERS) as lay:
                    env.lay = lay
                    t = Tiles(lay * (T2 // SLOTS) + LAYERS * (T1 // SLOTS))
                    tr = second["norm"]
                    pe_ffn(pe, t, lay * 2 + 4, tr, "f0")
                    pe_norm(pe, tr, "pf0")
                    pe_norm(pe, tr, "mix")
                    pe_mix2(pe, t)
                    pe_norm(pe, tr, "pmix")
                    pe_ffn(pe, t, lay * 2 + 5, tr, "f1")
                    pe_norm(pe, tr, "pf1")
            env.lay = 0
            pe_finish(pe)

        def tables(which):
            nc.scalar.add_instruction(mybir.InstLoadActFuncSet(
                act_func_set_id=which, name=nc.get_next_instruction_name(), engine=mybir.EngineType.Activation))

        def act_rstd(e, tr, tag, src, scale, eps, n, i=0, ready=None, name=None):
            r_ = rstd[:, i, 0:n]
            act_(r_, src, ACT.Ln, bias=consts[:, eps:eps + 1], scale=scale).then_inc(
                tr[1].sem, tr[1].did(f"{tag}.ln"))
            e.wait_ge(tr[1].sem, tr[1].at(f"{tag}.ln"))
            act_(r_, r_, ACT.Exp, scale=-0.5).then_inc(
                tr[1].sem, tr[1].did(f"{tag}.rstd"))

        def act_parts(e, tr, dst, src, made, name):
            for b in range(4):
                e.wait_ge(*made(b))
                act_(blk2(dst, b), blk2(src, b), ACT.Copy).then_inc(tr[1].sem, tr[1].did(f"{name}{b}"))

        def act_norm(e, t, tr, tag, upd, bnk=7):
            for k in range(4):
                e.wait_ge(x_upd, upd + (k + 1))
                act_(sqp(k), blk2(x, k), ACT.Square).then_inc(tr[1].sem, tr[1].did(f"{tag}.sq{k}"))
            high(e, t, AHEAD)
            tables(LN_EXP)
            e.wait_ge(tr[0].sem, tr[0].at(tag + ".sum"))
            act_rstd(e, tr, tag, bank(bnk, 0, S), 1.0 / D, 0, S)
            act_parts(e, tr, xh, sq, lambda b: (tr[2].sem, tr[2].at(f"{tag}.xn{2 * b + 1}")), tag + ".xh")

        def act_post(e, tr, tag, ready, scale=1.0):
            for k in range(4):
                ready(k)
                act_(sqp(k), bank(k), ACT.Square, scale=scale).then_inc(tr[1].sem, tr[1].did(f"{tag}.sq{k}"))
            tables(LN_EXP)
            e.wait_ge(tr[0].sem, tr[0].at(tag + ".sum"))
            act_rstd(e, tr, tag, bank(7, 0, S), 1.0 / D, 0, S)

        def act_ffn(e, t, f, tr, tag, upd, gain, gains_at):
            high(e, t, AHEAD)
            if gains_at:
                e.wait_ge(tr[2].sem, tr[2].at(gains_at))
            for k in range(KB):
                e.wait_ge(x_upd, upd + (k // 2 + 1))
                act_(xh[:, k, :], x[:, k, :], ACT.Identity, scale=gain(k)).then_inc(tr[1].sem, tr[1].did(f"{tag}.xh{k}"))
            for k in range(4):
                act_(sqp(k), blk2(x, k), ACT.Square).then_inc(tr[1].sem, tr[1].did(f"{tag}.sq{k}"))
            tables(LN_EXP)
            e.wait_ge(tr[0].sem, tr[0].at(tag + ".sum"))
            act_rstd(e, tr, tag, bank(0, 0, S), 1.0 / D, 0, S)
            tables(SILU_TANH)

            def one(it, j):
                high(e, t, 2)
                e.wait_ge(gate_ready, f * FB + it * 4 + (j + 1))
                z = act2[:, j % 2, 0, :]
                act_(z, z, ACT.Silu).then_inc(silu_ready, 1)
            for j in range(2):
                one(0, j)
            t.loop(e, (FB - 2) // 4, 8, lambda it: [one(it, 2 + jj) for jj in range(4)])
            t.loop(e, (FB - AHEAD) // 4, 4, lambda it: high(e, t, 4))
            high(e, t, (FB - AHEAD) % 4)

        def act_mix1(e, t, tr, so):
            for i in range(N_PROJ + 1):
                if i < N_PROJ:
                    name = MIX1_TILES[i][0]
                    b = i % 4
                    before_evac = 1 if name.startswith("V") else 2
                    high(e, t, before_evac)
                    e.wait_ge(tr[0].sem, tr[0].at("p." + name))
                    if name.startswith("V"):
                        dst = vb if name == "VB" else vc[:, :, (name == "VC1") * 256:(name == "VC1") * 256 + 256]
                        act_(dst, pair(b), ACT.Copy).then_inc(tr[1].sem, tr[1].did("cp." + name))
                    else:
                        c = chain.index(name)
                        n = S if name in ("KI", "KA") else 512
                        if HEAD_AT[name][1] is None:
                            if c >= 2:
                                e.wait_ge(tr[2].sem, tr[2].at("h." + chain[c - 2]))
                            act_(ybuf[:, c % 2, 0:n], bank(b, 0, n), ACT.Copy).then_inc(
                                tr[1].sem, tr[1].did("cp." + name))
                        else:
                            act_(sqp(c % 2)[:, 0:n], bank(b, 0, n), ACT.Square).then_inc(
                                tr[1].sem, tr[1].did("sq." + name))
                        if name == "KI":
                            act_(wi, bank(b, S, S + QT * 8).rearrange("p (q n) -> p q n", q=QT), ACT.Copy,
                                 scale=float((8 * 64) ** -0.5)).then_inc(tr[1].sem, tr[1].did("cp2.KI"))
                        if name == "KA":
                            act_(va, bank(b, S, S + QT * HD).rearrange("p (q n) -> p q n", q=QT),
                                 ACT.Copy).then_inc(tr[1].sem, tr[1].did("cp2.KA"))
                if i >= 1:
                    name = MIX1_TILES[i - 1][0]
                    if name in HEAD_AT and HEAD_AT[name][1] is not None:
                        c = chain.index(name)
                        n = S if name == "KA" else 512
                        e.wait_ge(tr[0].sem, tr[0].at("ss." + name))
                        if HEAD_AT[chain[c - 2]][1] is not None:
                            e.wait_ge(tr[2].sem, tr[2].at("y." + chain[c - 2]))
                        act_rstd(e, tr, name, bank(4, 0, n), 1.0 / HD, 0, n, c % 2)
                if 5 <= i <= 10:
                    j = i - 5
                    e.wait_ge(tr[0].sem, tr[0].at(f"index{j}"))
                    if j >= 2:
                        e.wait_ge(tr[2].sem, tr[2].at(f"acc{j - 2}"))
                    act_(rl[:, j % 2, :], bank(6 + j % 2), ACT.Relu).then_inc(tr[1].sem, tr[1].did(f"relu{j}"))
                if i < N_PROJ:
                    high(e, t, 2 - before_evac)
            g = [0]

            def gate():
                k = g[0]
                g[0] += 1
                high(e, t, 2)
                e.wait_ge(so[0].sem, so[0].at(f"gate{k}"))
                act_(hidb(2 * k, 2), bank(k % 2), ACT.Tanh, scale=0.5).then_inc(so[1].sem, so[1].did(f"gate{k}"))
            for j in range(len(UNITS) + 2):
                if j < len(UNITS):
                    nk = P * (UNITS[j][1] + 1)
                    e.wait_ge(so[2].sem, so[2].at(f"nm{j}"))
                    for m in range(4):
                        z = smb[:, j % 2, m * nk:(m + 1) * nk]
                        ins = act_(z, z, ACT.Exp, bias=nmax[:, j % 2, m:m + 1], accum_out=rsum[:, j % 2, m:m + 1])
                    ins.then_inc(so[1].sem, so[1].did(f"e{j}"))
                gate()
                if 1 <= j <= len(UNITS):
                    u = j - 1
                    gr, q = UNITS[u]
                    e.wait_ge(so[0].sem, so[0].at(f"t{u}"))
                    n = (2 if gr[0] == "C" else 4) * (q + 1) * P
                    src = PS[:, 6:8, :].rearrange("p b n -> p (b n)")
                    act_(ptb[:, u % 2, 0:n], src[:, 0:n], ACT.Copy).then_inc(so[1].sem, so[1].did(f"pt{u}"))
                if j >= 2:
                    u = j - 2
                    gr, q = UNITS[u]
                    e.wait_ge(so[0].sem, so[0].at(f"o{u}"))
                    b0 = {"A": 0, "B": 2, "C0": 4, "C1": 6}[gr]
                    act_(oT1[:, b0:b0 + 2, q * P:(q + 1) * P], pair(2 + (u // 2) % 2)[:, :, q * P:(q + 1) * P],
                         ACT.Copy).then_inc(so[1].sem, so[1].did(f"o{u}"))
                    if gr[0] == "C" and q == 1:
                        i = int(gr[1])
                        e.wait_ge(so[1].sem, so[1].at(f"o{u}"))
                        act_(sqp(i), blk2(oT1, 2 + i), ACT.Square).then_inc(so[1].sem, so[1].did(f"sqc{i}"))
                if j >= len(UNITS):
                    gate()
            for i in range(2):
                if i == 0:
                    e.wait_ge(so[1].sem, so[1].at("o7"))
                act_(blk2(oh, i), blk2(oT1, i), ACT.Copy).then_inc(so[1].sem, so[1].did(f"oh{i}"))
            high(e, t, 4)
            tables(LN_EXP)
            for i in range(2):
                e.wait_ge(so[0].sem, so[0].at(f"ssc{i}"))
                act_rstd(e, so, f"c{i}", bank(i), 1.0 / P, 0, 512, i)
            for i in range(2):
                e.wait_ge(so[2].sem, so[2].at(f"nc{i}"))
                act_(blk2(oh, 2 + i), blk2(oT1, 2 + i), ACT.Copy).then_inc(so[1].sem, so[1].did(f"oh{2 + i}"))
            high(e, t, 4)
            act_parts(e, tr, xh, merged, lambda b: (tr[2].sem, tr[2].at(f"mc{b}")), "mh")
            high(e, t, 8 - AHEAD)

        def act_l2(e):
            def square(j):
                if j >= 4:
                    e.wait_ge(m2[0].sem, m2[0].at(f"l2s{j - 4}"))
                e.wait_ge(m2[1].sem, m2[1].at(f"silu{j}"))
                act_(sqp(j % 4), blk2(heads, j), ACT.Square).then_inc(m2[1].sem, m2[1].did(f"l2sq{j}"))
            for j in range(4):
                square(j)
            tables(LN_EXP)
            for j in range(8):
                e.wait_ge(m2[0].sem, m2[0].at(f"l2s{j}"))
                if j >= 2:
                    e.wait_ge(m2[2].sem, m2[2].at(f"l2n{j - 2}"))
                act_rstd(e, m2, f"l2.{j}", bank(4 + j % 4), 1.0, 0, 512, j % 2)
                if j + 4 < 8:
                    square(j + 4)

        def act_mix2(e, t):
            def silu(j):
                e.wait_ge(m2[2].sem, m2[2].at(f"q.{j}.3.1"))
                act_(blk2(heads, j), blk2(heads, j), ACT.Silu).then_inc(m2[1].sem, m2[1].did(f"silu{j}"))
            for i, name in enumerate(mix2):
                high(e, t, 2)
                if name == "A0":
                    continue
                e.wait_ge(m2[0].sem, m2[0].at("p." + name))
                num = int("".join(ch for ch in name if ch.isdigit()))
                if name == "BETA0":
                    act_(ab[0:8, 1, :], PS[0:8, i % 4, 0:S], ACT.Tanh, scale=0.5).then_inc(m2[1].sem, m2[1].did("cp.BETA0"))
                elif name.startswith("GLU_A"):
                    pass
                elif name.startswith("GLU_G"):
                    if num >= 2:
                        e.wait_ge(m2[2].sem, m2[2].at(f"glu.{num - 2}.1"))
                    for b in range(2):
                        act_(gth[:, num % 2, b * S:(b + 1) * S], bank(i % 4, b * S, (b + 1) * S), ACT.Tanh, scale=0.5,
                             bias=g2[:, 2 * num + b, B_G:B_G + 1]).then_inc(m2[1].sem, m2[1].did(f"gth.{num}.{b}"))
                elif name.startswith("QKV"):
                    if num >= 2:
                        e.wait_ge(m2[2].sem, m2[2].at(f"q.{num - 2}.3.1"))
                    act_(qpad[:, num % 2, :, CTAPS - 1:], pair(i % 4), ACT.Copy).then_inc(m2[1].sem, m2[1].did("cp." + name))
                    if num >= 1:
                        silu(num - 1)
                elif name.startswith("Z"):
                    act_(hidb(16 + 2 * num, 2), bank(i % 4), ACT.Silu).then_inc(m2[1].sem, m2[1].did("cp." + name))
                    if num == 0:
                        silu(11)
                        act_l2(e)
                else:
                    act_(hidb(2 * num, 2), bank(i % 4), ACT.Tanh, scale=0.5).then_inc(m2[1].sem, m2[1].did("cp." + name))
                if name == "GLU_G0":
                    e.wait_ge(m2[2].sem, m2[2].at("absa"))
                    act_(lg[0:8, 1, :], lg[0:8, 0, :], ACT.Exp, scale=-1.0).then_inc(m2[1].sem, m2[1].did("sp.e"))
                    e.wait_ge(m2[1].sem, m2[1].at("sp.e"))
                    act_(lg[0:8, 1, :], lg[0:8, 1, :], ACT.Ln, bias=1.0).then_inc(m2[1].sem, m2[1].did("sp.ln"))
                if name == "GLU_G3":
                    e.wait_ge(m2[0].sem, m2[0].at("tok"))
                    act_(gtok, bank(4, 0, 16).rearrange("p (t h) -> p t h", t=QT), ACT.Copy).then_inc(m2[1].sem, m2[1].did("gtok"))
                    act_(ngtok, bank(4, 0, 16).rearrange("p (t h) -> p t h", t=QT), ACT.Copy, scale=-1.0).then_inc(m2[1].sem, m2[1].did("ngtok"))
                    act_(bgtok, bank(4, 0, 16).rearrange("p (t h) -> p t h", t=QT), ACT.Exp).then_inc(m2[1].sem, m2[1].did("egtok"))
                    act_(btok, bank(4, 16, 32).rearrange("p (t h) -> p t h", t=QT), ACT.Copy).then_inc(m2[1].sem, m2[1].did("btok"))
            act_delta(e)
            for i in range(4):
                e.wait_ge(dl[1].sem, dl[1].at(f"{i // 2}.oc.1"))
                act_(sqp(i), blk2(oT2, i), ACT.Square).then_inc(dl[1].sem, dl[1].did(f"osq{i}"))
            tables(LN_EXP)
            for i in range(4):
                e.wait_ge(dl[0].sem, dl[0].at(f"os{i}"))
                if i >= 2:
                    e.wait_ge(dl[2].sem, dl[2].at(f"on{i - 2}"))
                act_rstd(e, dl, f"o{i}", bank(i), 1.0 / P, 0, 512, i % 2)
            act_parts(e, dl, oh, oT2, lambda b: (dl[2].sem, dl[2].at(f"oz{b}")), "oh")
            act_parts(e, cv, ch, conv, lambda b: (cv[1].sem, cv[1].at(f"cvs{2 * b + 1}")), "ch")
            high(e, t, 16)
            for k in range(KB):
                e.wait_ge(m2[0].sem, m2[0].at(f"yb.{k // 2}"))
                act_(sq[:, k, :], acc(k, 4), ACT.Identity, bias=g2[:, k, B_O:B_O + 1]).then_inc(m2[1].sem, m2[1].did(f"yo{k}"))
            act_parts(e, m2, xh, merged, lambda b: (m2[2].sem, m2[2].at(f"mb{b}")), "mh")
            high(e, t, 8 - AHEAD)

        def act_conv(e, g, l):
            if (g, l) == (0, 1):
                e.wait_ge(cv[0].sem, cv[0].at("mean.sum"))
                act_(rstd[:, 1, 0:S], bank(2, 0, S), ACT.Copy, scale=1.0 / D).then_inc(cv[1].sem, cv[1].did("mean"))
            if g == 0 and l in (4, 5):
                for k in (2 * (l - 4), 2 * (l - 4) + 1):
                    e.wait_ge(cv[2].sem, cv[2].at(f"cent{k}"))
                    act_(sqp(k), blk2(conv, k), ACT.Square).then_inc(cv[1].sem, cv[1].did(f"ln.sq{k}"))
            if (g, l) == (0, 6):
                tables(LN_EXP)
                e.wait_ge(cv[0].sem, cv[0].at("ln.sum"))
                act_rstd(e, cv, "ln", bank(6, 0, S), 1.0 / D, 1, S)
            if g == 1 and l == 2:
                tables(SILU_TANH)
            if g == 1 and 2 <= l <= 5:
                for k in (2 * (l - 2), 2 * (l - 2) + 1):
                    e.wait_ge(cv[2].sem, cv[2].at(f"lnx{k}"))
                    act_(conv[:, k, :], conv[:, k, :], ACT.Silu, bias=g2[:, k, LN_B:LN_B + 1]).then_inc(cv[1].sem, cv[1].did(f"cvs{k}"))

        def act_delta(e):
            wp = lambda n: e.wait_ge(dl[0].sem, dl[0].at(n))
            wv = lambda n: e.wait_ge(dl[2].sem, dl[2].at(n))

            def four(b):
                return bank(b).rearrange("p (h n) -> p h n", h=4)

            def copy(dst, b, n):
                act_(dst, four(b), ACT.Copy).then_inc(dl[1].sem, dl[1].did(n))
            for g in range(2):
                for c in range(QT):
                    wv(f"{g}.gbm.{c}")
                    for h in range(4):
                        z = DU["gbm", c][:, h, :]
                        ins = act_(z, z, ACT.Exp, bias=ngtok[:, c, 4 * g + h:4 * g + h + 1])
                    ins.then_inc(dl[1].sem, dl[1].did(f"{g}.dt.{c}"))
                    if c == 0:
                        wv(f"{g}.cd0")
                        act_(cdec, cdec, ACT.Exp).then_inc(dl[1].sem, dl[1].did(f"{g}.cdec"))
                    else:
                        act_(qd, four(4), ACT.Exp).then_inc(dl[1].sem, dl[1].did(f"{g}.eg"))
                for c in range(QT):
                    wp(f"{g}.tt.{c}")
                    copy(DU["T", c], 4 * c, f"{g}.T0.{c}")
                for l in range(1, 7):
                    for c in range(QT):
                        wp(f"{g}.m{l}.{c}")
                        copy(DU["m1", c], 4 * c + 3, f"{g}.mc{l}.{c}")
                    act_conv(e, g, l)
                for c in range(QT):
                    wp(f"{g}.u.{c}")
                    copy(DU["u", c], 4 * c + 2, f"{g}.uc.{c}")
                wp(f"{g}.w")
                copy(wT, 5, f"{g}.wc")
                wp(f"{g}.s")
                copy(st, 1, f"{g}.sc")
                for c in range(QT):
                    wp(f"{g}.o.{c}")
                    copy(oT2[:, 4 * g:4 * g + 4, c * P:(c + 1) * P], 4 * c + 3, f"{g}.oc.{c}")

        @block.scalar
        def _(e):
            load_params(e)
            e.wait_ge(params_in, N_PARAM)
            e.wait_ge(pro_pe.sem, pro_pe.at("small"))
            act_(cols1[:], bank(4, 0, KB * ROWS1).rearrange("p (k r) -> p k r", k=KB), ACT.Copy).then_inc(
                pro_act.sem, pro_act.did("cols1"))
            act_(small[:], bank(6, 0, SMALL), ACT.Copy).then_inc(pro_act.sem, pro_act.did("small"))
            e.wait_ge(pro_dve.sem, pro_dve.at("lsum"))
            act_(lexp, lsum, ACT.Exp).then_inc(pro_act.sem, pro_act.did("lexp"))
            act_(gd[0:8, 0, 4:4 + LAYERS], gd[0:8, 0, 0:LAYERS], ACT.Exp).then_inc(pro_act.sem, pro_act.did("decay"))
            e.wait_ge(pro_dve.sem, pro_dve.at("angles"))
            act_(sinT[:], red, ACT.Sin).then_inc(pro_act.sem, pro_act.did("sin"))
            act_(cosT[:], red2, ACT.Sin).then_inc(pro_act.sem, pro_act.did("cos"))
            with e.Fori(0, LAYERS) as lay:
                env.lay = lay
                t = Tiles(lay * (T1 // SLOTS), 0, KEY_TILES)
                tr = first["norm"]
                act_ffn(e, t, lay * 2, tr, "f0", lay * 12, lambda k: g1[:, k, 0:1], "gains")
                act_norm(e, t, tr, "mix", lay * 12 + 4)
                act_mix1(e, t, first["mix"], first["soft"])
                act_ffn(e, t, lay * 2 + 1, tr, "f1", lay * 12 + 8, lambda k: g1[:, k, 2:3], None)
                assert t.k == T1
            env.lay = 0
            if BLOCKS > 1:
                for b in range(2):
                    e.wait_ge(pro_pe.sem, pro_pe.at(f"cols2.{b}"))
                    act_(cols2[:, 4 * b:4 * b + 4, :], bank(4 + b, 0, 4 * ROWS2).rearrange("p (k r) -> p k r", k=4),
                         ACT.Copy).then_inc(pro_act.sem, pro_act.did(f"cols2.{b}"))
                e.wait_ge(pro_pe.sem, pro_pe.at("small2"))
                act_(small2[:], bank(6, 0, LAYERS), ACT.Copy).then_inc(pro_act.sem, pro_act.did("small2"))
                with e.Fori(0, LAYERS) as lay:
                    env.lay = lay
                    t = Tiles(lay * (T2 // SLOTS) + LAYERS * (T1 // SLOTS))
                    tr = second["norm"]
                    upd = lay * 12 + 12 * LAYERS
                    for half in range(2):
                        if half == 1:
                            act_norm(e, t, tr, "mix", upd + 4)
                            act_mix2(e, t)
                            act_post(e, tr, "pmix", lambda k: e.wait_ge(second["mix"][0].sem, second["mix"][0].at(f"out.{k}")), 0.5)
                        f = lay * 2 + (4 + half)
                        gp = (G_F1, G_F2)[half]
                        act_ffn(e, t, f, tr, f"f{half}", upd + 8 * half, lambda k: g2[:, k, gp:gp + 1],
                                None if half else f"half{B_G}")
                        act_post(e, tr, f"pf{half}", lambda k: e.wait_ge(down_ready, f * 4 + (k + 1)))
                    assert t.k == T2
            env.lay = 0
            for b in range(4):
                e.wait_ge(pro_pe.sem, pro_pe.at(f"fin{b}"))
                act_(blk2(heads, b), bank(4 + b), ACT.Copy).then_inc(out_ready, 1)

        def step(e, tr, ins, name):
            ins.then_inc(tr[2].sem, tr[2].did(name))
            e.wait_ge(tr[2].sem, tr[2].at(name))

        def dve_scale(e, tr, tag, gain):
            e.wait_ge(tr[1].sem, tr[1].at(tag + ".rstd"))
            for k in range(KB):
                v_.scalar_tensor_tensor(sq[:, k, :], x[:, k, :], gain(k), rstd[:, 0, 0:S], ALU.mult,
                                        ALU.mult).then_inc(tr[2].sem, tr[2].did(f"{tag}.xn{k}"))
                if k % 2 == 1 and k >= 3:
                    dve_parts(e, tr, xl, sq, xh, tag + ".xh", tag + ".xl", [k // 2 - 1])
            dve_parts(e, tr, xl, sq, xh, tag + ".xh", tag + ".xl", [3])

        def dve_parts(e, tr, dst, src, highs, made, name, blocks=range(4)):
            for b in blocks:
                e.wait_ge(tr[1].sem, tr[1].at(f"{made}{b}"))
                v_.tensor_tensor(blk2(dst, b), blk2(src, b), blk2(highs, b), ALU.subtract).then_inc(
                    tr[2].sem, tr[2].did(f"{name}{b}"))

        def dve_post(e, tr, tag, gain):
            e.wait_ge(tr[1].sem, tr[1].at(tag + ".rstd"))
            for k in range(KB):
                v_.scalar_tensor_tensor(sq[:, k, :], acc(k), gain(k), rstd[:, 0, 0:S], ALU.mult,
                                        ALU.mult).then_inc(tr[2].sem, tr[2].did(f"{tag}.s{k}"))
                for b in [k // 2 - 1] * (k % 2 and k >= 3) + [3] * (k == KB - 1):
                    e.wait_ge(tr[2].sem, tr[2].at(f"{tag}.s{2 * b + 1}"))
                    v_.tensor_tensor(blk2(x, b), blk2(x, b), sqp(b), ALU.add).then_inc(x_upd, 1)

        def dve_ffn(e, t, f, tr, tag, gain):
            low(e, t, 1, handed=True)
            for k in range(KB):
                e.wait_ge(tr[1].sem, tr[1].at(f"{tag}.xh{k}"))
                v_.scalar_tensor_tensor(xl[:, k, :], x[:, k, :], gain(k), xh[:, k, :], ALU.mult,
                                        ALU.subtract).then_inc(tr[2].sem, tr[2].did(f"{tag}.xl{k}"))
            low(e, t, AHEAD - 1)
            for i, (p, q) in enumerate(((0, 1), (2, 3), (0, 2))):
                e.wait_ge(tr[1].sem, tr[1].at(f"{tag}.sq{(1, 3, 3)[i]}"))
                if i == 2:
                    e.wait_ge(tr[2].sem, tr[2].at(f"{tag}.add1"))
                v_.tensor_tensor(sqp(p), sqp(p), sqp(q), ALU.add).then_inc(tr[2].sem, tr[2].did(f"{tag}.add{i}"))

            def one(it, j, at):
                low(e, t, 2)
                if j == 0:
                    e.wait_ge(tr[1].sem, tr[1].at(tag + ".rstd"))
                e.wait_ge(gu_ready, f * FB + it * 4 + (j + 1))
                made = (f * FB + it * 4 + j) * 3
                g_, u_ = act2[:, j % 2, 0, :], act2[:, j % 2, 1, :]
                v_.tensor_tensor(g_, bank(4 + j % 4, 0, S), rstd[:, 0, 0:S], ALU.mult).then_inc(gate_ready, 1)
                v_.tensor_tensor(u_, bank(4 + j % 4, S, 2 * S), rstd[:, 0, 0:S], ALU.mult).then_inc(hid_steps, 1)
                e.wait_ge(silu_ready, f * FB + it * 4 + (j + 1))
                e.wait_ge(hid_steps, made + 1)
                v_.tensor_tensor(g_, g_, u_, ALU.mult).then_inc(hid_steps, 1)
                e.wait_ge(hid_steps, made + 2)
                v_.tensor_copy(hh[:, at], g_).then_inc(hid_steps, 1)
                e.wait_ge(hid_steps, made + 3)
                v_.tensor_tensor(hl[:, at], g_, hh[:, at], ALU.subtract).then_inc(hid_done, 1)
            for j in range(2):
                one(0, j, slice(j * S, (j + 1) * S))
            t.loop(e, (FB - 2) // 4, 8,
                   lambda it: [one(it, 2 + jj, bass.ds(it * (4 * S) + (2 + jj) * S, S)) for jj in range(4)])
            t.loop(e, (FB - AHEAD) // 4, 4, lambda it: low(e, t, 4))
            low(e, t, (FB - AHEAD) % 4)

        def dve_residual(e, ready):
            for b in range(4):
                ready(b)
                v_.scalar_tensor_tensor(blk2(x, b), bank(b), 0.5, blk2(x, b), ALU.mult, ALU.add).then_inc(x_upd, 1)

        def dve_index(e, tr, j):
            q, hs = INDEX_HEADS[j]
            nk = P * (q + 1)
            e.wait_ge(tr[1].sem, tr[1].at(f"relu{j}"))
            for i, h in enumerate(hs):
                src = rl[:, j % 2, i * nk:(i + 1) * nk]
                name = f"acc{j}" if h == hs[-1] else f"acc{j}.{h}"
                if h == 0:
                    ins = v_.tensor_scalar(isc[q], src, wi[:, q, 0:1], None, ALU.mult)
                else:
                    ins = v_.scalar_tensor_tensor(isc[q], src, wi[:, q, h:h + 1], isc[q], ALU.mult, ALU.add)
                step(e, tr, ins, name)
            if j in (1, 5):
                v_.tensor_tensor(isc[q], isc[q], cmask[:, S - nk:S], ALU.add).then_inc(tr[2].sem, tr[2].did(f"isc{q}"))
                hold(e, "vector", tr[2].sem, tr[2].at(f"isc{q}"))

        def dve_topk(e, tr, q, r):
            src = isc[q] if r == 0 else work[q]
            if r % 2 == 0:
                e.sem_inc(passed["vector"], 1)
            v_.max(top8, src).then_inc(tr[2].sem, tr[2].did(f"top{q}.{r}"))
            hold(e, "vector", tr[2].sem, tr[2].at(f"top{q}.{r}"))
            v_.match_replace(work[q], top8, src, TAKEN).then_inc(tr[2].sem, tr[2].did(f"take{q}.{r}"))
            hold(e, "vector", tr[2].sem, tr[2].at(f"take{q}.{r}"))
            if r == TOPK // 8 - 1:
                nk = P * (q + 1)
                step(e, tr, v_.tensor_tensor(ibias[q], work[q], isc[q], ALU.not_equal), f"kept{q}")
                step(e, tr, v_.tensor_scalar(ibias[q], ibias[q], 1.0, -NEG, ALU.subtract, ALU.mult), f"bias{q}")
                step(e, tr, v_.tensor_tensor(ibias[q], ibias[q], cmask[:, S - nk:S], ALU.add), f"ibias{q}")

        def dve_mix1(e, tr, so, lay):
            for i in range(N_PROJ + 3):
                if 1 <= i <= N_PROJ:
                    name = MIX1_TILES[i - 1][0]
                    if name in HEAD_AT and HEAD_AT[name][1] is not None:
                        c = chain.index(name)
                        n = S if name == "KA" else 512
                        e.wait_ge(tr[1].sem, tr[1].at(name + ".rstd"))
                        r = HEAD_AT[name][1]
                        v_.scalar_tensor_tensor(ybuf[:, c % 2, 0:n], bank((i - 1) % 4, 0, n), h1[:, r:r + 1],
                                                rstd[:, c % 2, 0:n], ALU.mult,
                                                ALU.mult).then_inc(tr[2].sem, tr[2].did("y." + name))
                if 2 <= i <= N_PROJ + 1:
                    name = MIX1_TILES[i - 2][0]
                    if name in HEAD_AT:
                        c = chain.index(name)
                        nb = 1 if name in ("KI", "KA") else 2
                        n = nb * S
                        shape = lambda ap: ap.rearrange("p (b s) -> p b s", b=nb)
                        e.wait_ge(tr[0].sem, tr[0].at("rot." + name))
                        v_.tensor_tensor(shape(tbuf[:, c % 2, 0:n]), shape(bank(5, 0, n)), bc(sinT[:], nb),
                                         ALU.mult).then_inc(tr[2].sem, tr[2].did("t." + name))
                        step(e, tr, v_.tensor_tensor(shape(ubuf[:, c % 2, 0:n]), shape(ybuf[:, c % 2, 0:n]), bc(cosT[:], nb),
                                                     ALU.mult), "u." + name)
                        at = HEAD_AT[name][0]
                        v_.tensor_tensor(heads[:, at:at + nb, :].rearrange("p b s -> p (b s)"), tbuf[:, c % 2, 0:n],
                                         ubuf[:, c % 2, 0:n], ALU.add).then_inc(tr[2].sem, tr[2].did("h." + name))
                if 6 <= i <= 11:
                    dve_index(e, tr, i - 6)
                if 8 <= i <= 11:
                    for r in (2 * (i - 8), 2 * (i - 8) + 1):
                        dve_topk(e, tr, 0, r)
            for j, (gr, q) in enumerate(UNITS):
                nk = P * (q + 1)
                e.wait_ge(so[0].sem, so[0].at(f"s{j}"))
                z = smb[:, j % 2, 0:4 * nk].rearrange("p (m n) -> p m n", m=4)
                mask = ibias[q] if gr == "A" else cmask[:, S - nk:S]
                for c in range(2):
                    src = bank(4 + c, 0, 2 * nk).rearrange("p (i n) -> p i n", i=2)
                    ins = v_.scalar_tensor_tensor(z[:, 2 * c:2 * c + 2, :], src, HD ** -0.5, bc(mask, 2), ALU.mult, ALU.add)
                    if c == 0:
                        ins.then_inc(so[2].sem, so[2].did(f"sm{j}.0"))
                step(e, so, ins, f"sm{j}")
                v_.tensor_reduce(nmax[:, j % 2, :], z, AX.X, ALU.max, negate=True).then_inc(so[2].sem, so[2].did(f"nm{j}"))
                e.wait_ge(so[1].sem, so[1].at(f"e{j}"))
                ri = rinv[:, j % 2, :]
                step(e, so, v_.reciprocal(ri, rsum[:, j % 2, :]), f"ri{j}")
                if gr[0] == "C":
                    second_maps = ri[:, 2:4]
                    step(e, so, v_.tensor_scalar(second_maps, second_maps, lam[:, bass.ds(lay, 1)], None, ALU.mult), f"rl{j}")
                    step(e, so, v_.tensor_tensor(z, z, bcl(ri, nk), ALU.mult), f"pp{j}")
                    ins = v_.tensor_tensor(z[:, 0:2, :], z[:, 0:2, :], z[:, 2:4, :], ALU.subtract)
                else:
                    ins = v_.tensor_tensor(z, z, bcl(ri, nk), ALU.mult)
                ins.then_inc(so[2].sem, so[2].did(f"p{j}"))
                if j < 4:
                    for r in (2 * j, 2 * j + 1):
                        dve_topk(e, tr, 1, r)
            dve_parts(e, so, ol, oT1, oh, "oh", "ol", (0, 1))
            e.wait_ge(so[1].sem, so[1].at("gate11"))
            for b in range(4):
                e.wait_ge(tr[0].sem, tr[0].at(f"ya.{b}"))
                v_.scalar_tensor_tensor(blk2(merged, b), hidb(2 * b, 2), 1.0, bank(b), ALU.add, ALU.mult).then_inc(
                    tr[2].sem, tr[2].did(f"ma{b}"))
            for i in range(2):
                e.wait_ge(so[1].sem, so[1].at(f"c{i}.rstd"))
                o = blk2(oT1, 2 + i)
                v_.scalar_tensor_tensor(o, o, h1[:, 6:7], rstd[:, i, :], ALU.mult, ALU.mult).then_inc(
                    so[2].sem, so[2].did(f"nc{i}"))
            dve_parts(e, so, ol, oT1, oh, "oh", "ol", (2, 3))
            for n, h0, b0 in (("b", 8, 4), ("c", 16, 0)):
                for b in range(4):
                    tmp = smb[:, b // 2, (b % 2) * 512:(b % 2 + 1) * 512]
                    e.wait_ge(tr[0].sem, tr[0].at(f"y{n}.{b}"))
                    step(e, tr, v_.scalar_tensor_tensor(tmp, hidb(h0 + 2 * b, 2), 1.0, bank(b0 + b), ALU.add, ALU.mult),
                         f"g{n}{b}")
                    v_.tensor_tensor(blk2(merged, b), blk2(merged, b), tmp, ALU.add).then_inc(
                        tr[2].sem, tr[2].did(f"m{n}{b}"))
            dve_parts(e, tr, xl, merged, xh, "mh", "ml")
            dve_residual(e, lambda b: e.wait_ge(tr[0].sem, tr[0].at(f"out.{b}")))

        def dve_setup(e):
            pr = (pro_pe, pro_act, pro_dve, pro_pool)
            e.sem_inc(hid_done, 4)
            e.sem_inc(lo_ready, SLOTS)
            step(e, pr, v_.memset(invrow[0:1, :], 0.0), "inv0")
            for i, f in enumerate(inv_freq):
                o = invrow[0:1, :].rearrange("p (h r j) -> p h r j", h=2, j=8)[:, :, 0:2, i]
                ins = v_.memset(o, f)
            ins.then_inc(pro_dve.sem, pro_dve.did("invrow"))
            v_.memset(consts[:, 0:1], EPS)
            v_.memset(consts[:, 1:2], LN_EPS).then_inc(pro_dve.sem, pro_dve.did("consts"))
            for b in range(4):
                e.wait_ge(pro_pe.sem, pro_pe.at(f"x{b}"))
                v_.tensor_copy(blk2(x, b), bank(b)).then_inc(x_upd, 1)
            e.wait_ge(params_in, N_PARAM)
            l4 = lamb.rearrange("p (l a b d) -> p l a b d", l=LAYERS, a=2, b=2)
            lp = lprod.rearrange("p (l a d) -> p l a d", l=LAYERS, a=2)
            step(e, pr, v_.tensor_tensor(lp, l4[:, :, :, 0, :], l4[:, :, :, 1, :], ALU.mult), "lprod")
            v_.tensor_reduce(lsum.rearrange("p (l a) -> p l a", l=LAYERS), lp, AX.X, ALU.add).then_inc(
                pro_dve.sem, pro_dve.did("lsum"))
            v_.tensor_copy(posf, pos_i).then_inc(pro_dve.sem, pro_dve.did("posf"))
            e.wait_ge(pro_pe.sem, pro_pe.at("small"))
            step(e, pr, v_.tensor_copy(invf, bank(7, 0, 1)), "invf")
            step(e, pr, v_.tensor_scalar(ang, posf, invf, None, ALU.mult), "ang")
            magic = 1.5 * 2.0 ** 23
            step(e, pr, v_.tensor_scalar(red, ang, 1.0 / TWO_PI, magic, ALU.mult, ALU.add), "turns0")
            step(e, pr, v_.tensor_scalar(red, red, magic, None, ALU.subtract), "turns")
            c1 = 6.28125
            c2 = float(np.float32(np.round((TWO_PI - c1) * 2 ** 21) / 2 ** 21))
            c3 = TWO_PI - c1 - c2
            for i, c in enumerate((c1, c2, c3)):
                step(e, pr, v_.scalar_tensor_tensor(ang, red, -c, ang, ALU.mult, ALU.add), f"red{i}")
            lim = 3.1415925
            step(e, pr, v_.tensor_scalar(red, ang, lim, -lim, ALU.min, ALU.max), "redsin")
            step(e, pr, v_.scalar_tensor_tensor(ang, red, -1.0, red, ALU.mult, ALU.max), "absang")
            step(e, pr, v_.tensor_scalar(red2, ang, -1.0, math.pi / 2, ALU.mult, ALU.add), "angles")
            e.wait_ge(pro_act.sem, pro_act.at("lexp"))
            l2 = lexp.rearrange("p (l a) -> p l a", l=LAYERS)
            for l in range(LAYERS):
                step(e, pr, v_.tensor_tensor(lam[:, l:l + 1], l2[:, l, 0:1], l2[:, l, 1:2], ALU.subtract), f"lam{l}")
                step(e, pr, v_.tensor_scalar(lam[:, l:l + 1], lam[:, l:l + 1], lam_init[l], None, ALU.add), f"lami{l}")
                e.wait_ge(pro_act.sem, pro_act.at("small"))
                c = small[:, 7 * l + 6:7 * l + 7]
                step(e, pr, v_.tensor_scalar(c, c, 1.0 - lam_init[l], None, ALU.mult), f"subln{l}")
            e.wait_ge(pro_act.sem, pro_act.at("decay"))
            step(e, pr, v_.tensor_scalar(gd[0:8, 0, 0:LAYERS], gd[0:8, 0, 4:4 + LAYERS], -1.0, None, ALU.mult), "ndecay")
            e.wait_ge(pro_act.sem, pro_act.at("cos"))
            e.wait_ge(pro_pool.sem, pro_pool.at("masks"))

        def dve_conv(e, n0, n1):
            for n in range(n0, min(n1, 2 * TAPS * 4)):
                hf, tap, b4 = n // (4 * TAPS), n // 4 % TAPS, n % 4
                b = 4 * hf + b4
                src = glu[:, b, tap:tap + S]
                w = g2[:, b, W_DW + tap:W_DW + tap + 1]
                if tap == 0:
                    e.wait_ge(m2[2].sem, m2[2].at(f"glu.{b // 2}.{b % 2}"))
                    ins = v_.tensor_scalar(conv[:, b, :], src, w, g2[:, b, W_B:W_B + 1], ALU.mult, ALU.add)
                else:
                    e.wait_ge(cv[2].sem, cv[2].at(f"cv.{hf}.{tap - 1}.{b4}"))
                    ins = v_.scalar_tensor_tensor(conv[:, b, :], src, w, conv[:, b, :], ALU.mult, ALU.add)
                ins.then_inc(cv[2].sem, cv[2].did(f"cv.{hf}.{tap}.{b4}"))

        def dve_mix2(e, lay):
            did = lambda ins, n: ins.then_inc(m2[2].sem, m2[2].did(n))
            did(v_.memset(glu[:, :, 0:TAPS - 1], 0.0), "pad0")
            did(v_.memset(qpad[:, :, :, 0:CTAPS - 1], 0.0), "pad1")
            e.wait_ge(m2[0].sem, m2[0].at("p.A0"))
            step(e, m2, v_.tensor_scalar(ab[0:8, 0, :], PS[0:8, 1, 0:S], gd[0:8, 1, bass.ds(lay, 1)], None, ALU.add), "cp.A0")
            did(v_.scalar_tensor_tensor(lg[0:8, 0, :], ab[0:8, 0, :], -1.0, ab[0:8, 0, :], ALU.mult, ALU.max), "absa")
            e.wait_ge(m2[1].sem, m2[1].at("cp.BETA0"))
            did(v_.tensor_scalar(ab[0:8, 1, :], ab[0:8, 1, :], 1.0, 0.5, ALU.add, ALU.mult), "beta")
            steps = 0
            for i, name in enumerate(mix2):
                num = int("".join(ch for ch in name if ch.isdigit()))
                if name.startswith("GLU_G"):
                    e.wait_ge(m2[1].sem, m2[1].at(f"gth.{num}.1"))
                    z = gth[:, num % 2, :]
                    step(e, m2, v_.tensor_scalar(z, z, 1.0, 0.5, ALU.add, ALU.mult), f"sg{num}")
                    for b in range(2):
                        did(v_.scalar_tensor_tensor(glu[:, 2 * num + b, TAPS - 1:], bank((i - 1) % 4, b * S, (b + 1) * S),
                                                    g2[:, 2 * num + b, B_A:B_A + 1], z[:, b * S:(b + 1) * S], ALU.add,
                                                    ALU.mult), f"glu.{num}.{b}")
                if name == "GLU_G0":
                    e.wait_ge(m2[1].sem, m2[1].at("sp.ln"))
                    step(e, m2, v_.scalar_tensor_tensor(lg[0:8, 2, :], ab[0:8, 0, :], 0.0, lg[0:8, 1, :], ALU.max, ALU.add), "softplus")
                    step(e, m2, v_.tensor_scalar(lg[0:8, 2, :], lg[0:8, 2, :], gd[0:8, 0, bass.ds(lay, 1)], None, ALU.mult), "decay")
                    for c in range(QT):
                        did(v_.tensor_tensor_scan(lg[0:8, 3, c * P:(c + 1) * P], ones[0:8, :], lg[0:8, 2, c * P:(c + 1) * P],
                                                  0.0, ALU.mult, ALU.add), f"gsum{c}")
                if name.startswith("QKV"):
                    e.wait_ge(m2[1].sem, m2[1].at("cp." + name))
                    for tap in range(CTAPS):
                        for b in range(2):
                            src = qpad[:, num % 2, b, tap:tap + S]
                            r = W_CV + 3 * tap + num // 4
                            w = g2[:, 2 * (num % 4) + b, r:r + 1]
                            o = heads[:, 2 * num + b, :]
                            if tap == 0:
                                ins = v_.tensor_scalar(o, src, w, None, ALU.mult)
                            else:
                                e.wait_ge(m2[2].sem, m2[2].at(f"q.{num}.{tap - 1}.{b}"))
                                ins = v_.scalar_tensor_tensor(o, src, w, o, ALU.mult, ALU.add)
                            did(ins, f"q.{num}.{tap}.{b}")
                if name == "Z0":
                    for j in range(8):
                        e.wait_ge(m2[1].sem, m2[1].at(f"l2.{j}.rstd"))
                        z = blk2(heads, j)
                        did(v_.scalar_tensor_tensor(z, z, P ** -0.5 if j < 4 else 1.0, rstd[:, j % 2, :], ALU.mult,
                                                    ALU.mult), f"l2n{j}")
                if i >= mix2.index("GLU_G1"):
                    more = 5 if name.startswith("QKV") else 4 if name == "Z0" else 9 if name.startswith("GATE") else 14
                    dve_conv(e, steps, steps + more)
                    steps += more
            assert steps >= 2 * TAPS * 4
            e.wait_ge(m2[1].sem, m2[1].at("btok"))
            step(e, m2, v_.tensor_tensor(bgtok, bgtok, btok, ALU.mult), "bgtok")
            dve_delta(e)
            for i in range(4):
                e.wait_ge(dl[1].sem, dl[1].at(f"o{i}.rstd"))
                z = blk2(oT2, i)
                step(e, dl, v_.scalar_tensor_tensor(z, z, h2[:, 0:1], rstd[:, i % 2, :], ALU.mult, ALU.mult), f"on{i}")
                v_.tensor_tensor(z, z, hidb(16 + 2 * i, 2), ALU.mult).then_inc(dl[2].sem, dl[2].did(f"oz{i}"))
            dve_parts(e, dl, ol, oT2, oh, "oh", "ol")
            dve_parts(e, cv, cl, conv, ch, "ch", "cl")
            for b in range(4):
                e.wait_ge(m2[0].sem, m2[0].at(f"ya.{b}"))
                did(v_.scalar_tensor_tensor(blk2(merged, b), hidb(2 * b, 2), 1.0, bank(b), ALU.add, ALU.mult), f"ma{b}")
            for b in range(4):
                e.wait_ge(m2[1].sem, m2[1].at(f"yo{2 * b + 1}"))
                step(e, m2, v_.scalar_tensor_tensor(sqp(b), hidb(8 + 2 * b, 2), 1.0, sqp(b), ALU.add, ALU.mult), f"gb{b}")
                did(v_.tensor_tensor(blk2(merged, b), blk2(merged, b), sqp(b), ALU.add), f"mb{b}")
            dve_parts(e, m2, xl, merged, xh, "mh", "ml")

        def dve_conv_norm(e, g, l):
            if g == 0 and l in (2, 3):
                e.wait_ge(cv[1].sem, cv[1].at("mean"))
                for k in (2 * (l - 2), 2 * (l - 2) + 1):
                    z = conv[:, 2 * k:2 * k + 2, :]
                    v_.tensor_tensor(z, z, bc(rstd[:, 1, 0:S], 2), ALU.subtract).then_inc(cv[2].sem, cv[2].did(f"cent{k}"))
            if g == 1 and l <= 4:
                e.wait_ge(cv[1].sem, cv[1].at("ln.rstd"))
                for k in (2 * (l - 1), 2 * (l - 1) + 1):
                    v_.scalar_tensor_tensor(conv[:, k, :], conv[:, k, :], g2[:, k, LN_G:LN_G + 1], rstd[:, 0, 0:S],
                                            ALU.mult, ALU.mult).then_inc(cv[2].sem, cv[2].did(f"lnx{k}"))

        def dve_delta(e):
            did = lambda ins, n: ins.then_inc(dl[2].sem, dl[2].did(n))
            wp = lambda n: e.wait_ge(dl[0].sem, dl[0].at(n))
            wa = lambda n: e.wait_ge(dl[1].sem, dl[1].at(n))
            four = lambda b: bank(b).rearrange("p (h n) -> p h n", h=4)
            tt = v_.tensor_tensor
            for g in range(2):
                hs = slice(4 * g, 4 * g + 4)
                for c in range(QT):
                    wp(f"{g}.gb.{c}")
                    did(tt(DU["gbm", c], four(4 * c), bc(tmask, 4), ALU.add), f"{g}.gbm.{c}")
                    if c == 0:
                        did(tt(cdec, four(0)[:, :, P - 1], gtok[:, 0, hs], ALU.subtract), f"{g}.cd0")
                for c in range(QT):
                    wa(f"{g}.dt.{c}")
                    wp(f"{g}.kk.{c}")
                    did(tt(DU["at", c], four(4 * c + 2), DU["gbm", c], ALU.mult), f"{g}.at0.{c}")
                    wp(f"{g}.qk.{c}")
                    did(tt(DU["qkt", c], four(4 * c + 3), DU["gbm", c], ALU.mult), f"{g}.qkt.{c}")
                    e.wait_ge(dl[2].sem, dl[2].at(f"{g}.at0.{c}"))
                    did(tt(DU["at", c], DU["at", c], four(4 * c + 1), ALU.mult), f"{g}.at.{c}")
                for c in range(QT):
                    e.wait_ge(dl[3].sem, dl[3].at(f"{g}.al0.{c}"))
                    did(tt(DU["U", c], bc(ident, 4), DU["al", c], ALU.subtract), f"{g}.U0.{c}")
                wa(f"{g}.cdec")
                for c in range(QT):
                    wp(f"{g}.vt.{c}")
                    did(tt(DU["vx", c], four(4 * c + 3), bcl(btok[:, c, hs], P), ALU.mult), f"{g}.vx.{c}")
                    col = cdec if c == 0 else bgtok[:, 1, hs]
                    did(tt(DU["kx", c], four(4 * c + 2), bcl(col, P), ALU.mult), f"{g}.kx.{c}")
                wa(f"{g}.eg")
                did(tt(qd, qd, heads[:, hs, P:S], ALU.mult), f"{g}.qd")
                for l in range(1, 7):
                    for c in range(QT):
                        U, T = DU["U", c], DU["T", c]
                        wp(f"{g}.pt{l}.{c}" if l < 6 else f"{g}.pu{l}.{c}")
                        did(tt(U, U, four(4 * c), ALU.subtract), f"{g}.U{l}.{c}")
                        if l < 6:
                            did(tt(T, T, four(4 * c + 1), ALU.subtract), f"{g}.T{l}.{c}")
                    dve_conv_norm(e, g, l)
                wp(f"{g}.ws")
                wa(f"{g}.uc.1")
                did(tt(DU["u", 1], DU["u", 1], four(4), ALU.subtract), f"{g}.vn")

        @block.vector
        def _(e):
            dve_setup(e)
            with e.Fori(0, LAYERS) as lay:
                env.lay = lay
                tr = first["norm"]
                v_.tensor_copy(g1[:], cols1[:, :, bass.ds(lay * 3, 3)])
                step(e, tr, v_.tensor_copy(h1[:, 0:7], small[:, bass.ds(lay * 7, 7)]), "gains")
                t = Tiles(lay * (T1 // SLOTS))
                for half in range(2):
                    if half == 1:
                        dve_scale(e, tr, "mix", lambda k: g1[:, k, 1:2])
                        dve_mix1(e, first["mix"], first["soft"], lay)
                        t.k = T1 - FFN_TILES
                    f = lay * 2 + half
                    dve_ffn(e, t, f, tr, f"f{half}", lambda k: g1[:, k, 2 * half:2 * half + 1])
                    dve_residual(e, lambda b: e.wait_ge(down_ready, f * 4 + (b + 1)))
            env.lay = 0
            if BLOCKS > 1:
                e.wait_ge(pro_act.sem, pro_act.at("small2"))
                with e.Fori(0, LAYERS) as lay:
                    env.lay = lay
                    tr = second["norm"]
                    v_.tensor_copy(g2[:], cols2[:, :, bass.ds(lay * R2, R2)])
                    step(e, tr, v_.tensor_copy(h2[:, 0:1], small2[:, bass.ds(lay, 1)]), "gains")
                    for r in (G_P1, G_PM, G_P2, B_G):
                        step(e, tr, v_.tensor_scalar(g2[:, :, r], g2[:, :, r], 0.5, None, ALU.mult), f"half{r}")
                    t = Tiles(lay * (T2 // SLOTS) + LAYERS * (T1 // SLOTS))
                    for half in range(2):
                        if half == 1:
                            t.k = T2 - FFN_TILES
                            dve_scale(e, tr, "mix", lambda k: g2[:, k, G_MX:G_MX + 1])
                            dve_mix2(e, lay)
                            dve_post(e, tr, "pmix", lambda k: g2[:, k, G_PM:G_PM + 1])
                        gp, gq = ((G_F1, G_P1), (G_F2, G_P2))[half]
                        dve_ffn(e, t, lay * 2 + (4 + half), tr, f"f{half}", lambda k: g2[:, k, gp:gp + 1])
                        dve_post(e, tr, f"pf{half}", lambda k: g2[:, k, gq:gq + 1])
            env.lay = 0

        def pool_mix2(e, t):
            low(e, t, 1, nc.gpsimd, True)
            low(e, t, 2 * len(mix2) + 2, nc.gpsimd)
            for g in range(2):
                for l in range(7):
                    for c in range(QT):
                        if l == 0:
                            e.wait_ge(dl[2].sem, dl[2].at(f"{g}.at.{c}"))
                        elif l == 1:
                            e.wait_ge(dl[2].sem, dl[2].at(f"{g}.U0.{c}"))
                        else:
                            e.wait_ge(dl[0].sem, dl[0].at(f"{g}.m{l - 1}.{c}"))
                        nc.gpsimd.tensor_tensor(DU["al", c], DU["at", c], bc(levels[:, l, :], 4), ALU.mult).then_inc(
                            dl[3].sem, dl[3].did(f"{g}.al{l}.{c}"))
            low(e, t, 3 * KB - AHEAD, nc.gpsimd)

        @block.gpsimd
        def _(e):
            p_ = nc.gpsimd
            T = pro_pool
            n = [0]

            def ok(ins, name=None):
                name = name or f"s{n[0]}"
                n[0] += 1
                ins.then_inc(T.sem, T.did(name))
                e.wait_ge(T.sem, T.at(name))

            def fill(buf, pattern, base, mult, op, value, name=None):
                ok(p_.affine_select(out=buf, in_=buf, compare_op=op, fill=value, base=base, pattern=pattern,
                                    channel_multiplier=mult), name)
            ok(p_.memset(ident[:], 0.0))
            fill(ident[:], [[-1, P]], 0, 1, ALU.not_equal, 1.0, "ident")
            ok(p_.memset(ones[:], 1.0), "ones")
            ok(p_.memset(ones64[:], 0.0))
            for h in range(2):
                c = ones64[:, h * HD:(h + 1) * HD]
                ok(p_.memset(c, 1.0))
                if h == 0:
                    fill(c, [[0, HD]], HD - 1, -1, ALU.is_ge, 0.0)
                else:
                    fill(c, [[0, HD]], -HD, 1, ALU.is_ge, 0.0)
            ok(p_.memset(rot[:], 0.0))
            for h in range(2):
                fill(rot[:, h * HD:h * HD + 8], [[-1, 8]], -(h * HD + 8), 1, ALU.not_equal, -1.0)
                fill(rot[:, h * HD + 8:h * HD + 16], [[-1, 8]], -(h * HD), 1, ALU.not_equal, 1.0)
            ok(p_.memset(cmask[:], 0.0))
            fill(cmask[:, P:S], [[-1, P]], 0, 1, ALU.is_ge, NEG)
            ok(p_.memset(tmask[:], 0.0))
            fill(tmask[:], [[1, P]], 0, -1, ALU.is_ge, NEG)
            ok(p_.memset(levels[:], 0.0))
            for l in range(7):
                w = 1 << l
                v = levels[:, l, :].rearrange("p (i y) -> p i y", y=2 * w)[:, :, w:2 * w]
                ok(p_.memset(v, 1.0))
                fill(v, [[-2 * w, P // (2 * w)], [0, w]], 0, 1, ALU.is_ge, 0.0)
                fill(v, [[2 * w, P // (2 * w)], [0, w]], w - 1, -1, ALU.is_ge, 0.0, "masks" if l == 6 else None)
            e.wait_ge(pro_act.sem, pro_act.at("cos"))
            with e.Fori(0, LAYERS) as lay:
                env.lay = lay
                tr = first["mix"]
                t = Tiles(lay * (T1 // SLOTS), FFN_TILES, KEY_TILES)
                low(e, t, 1, nc.gpsimd, True)
                low(e, t, T1 - FFN_TILES - t.k, nc.gpsimd)
            if BLOCKS > 1:
                env.lay = LAYERS - 1
                e.wait_ge(first["mix"][2].sem, first["mix"][2].at("mc3"))
                load_params2(e)
                with e.Fori(0, LAYERS) as lay:
                    env.lay = lay
                    pool_mix2(e, Tiles(lay * (T2 // SLOTS) + LAYERS * (T1 // SLOTS), FFN_TILES))
            env.lay = 0

    assert not (counted and env.missing), env.missing[0][1]
    return {n: t.names for n, t in tracks.items()}


BLOCKS = 2


def kernel(**inputs):
    import concourse.bacc as bacc
    from concourse.bass_utils import run_bass_kernel_spmd

    def build(plan):
        nc = bacc.Bacc("TRN2", target_bir_lowering=False, num_devices=1)
        args = {k: nc.dram_tensor(f"in_{k}_dram", v.shape, mybir.dt.from_np(v.dtype), kind="ExternalInput").ap()
                for k, v in arrays.items()}
        out = nc.dram_tensor("out_0_dram", (1, S, D), F32, kind="ExternalOutput").ap()
        return nc, program(nc, args, out, plan)

    arrays = {k: np.ascontiguousarray(v) for k, v in inputs.items()}
    _, plan = build({})
    nc, _ = build(plan)
    r = run_bass_kernel_spmd(nc, [{f"in_{k}_dram": v for k, v in arrays.items()}], core_ids=[0])
    return r.results[0]["out_0_dram"]
```
